# Optimizing a Trainium2 kernel written in Bass

```python
import jax
import jax.numpy as jnp
from jax import lax
import numpy as np

D_MODEL = 1024
BATCH = 1
SEQ = 256
DEPTH = 1
DEC_BATCH = 1
DEC_SEQ = 1024
PAST_LEN = 512

GRID_W = 64
HEAD_DIM = 64
ATTN_HEADS = 8
ATTN_KV_HEADS = 2
ATTN_GROUP = ATTN_HEADS // ATTN_KV_HEADS
ATTN_Q_W = ATTN_HEADS * HEAD_DIM
ATTN_KV_W = ATTN_KV_HEADS * HEAD_DIM
Q_BLOCK = 128
ROPE_THETA = 10000.0
DN_HEADS = 8
DN_DK = 64
DN_DV = 64
DN_K_W = DN_HEADS * DN_DK
DN_V_W = DN_HEADS * DN_DV
DN_DIRS = 2
CONV_W = 3
CONV_CH = 2 * DN_K_W + DN_V_W
CHUNK = 64
N_GROUPS = 4
EXPERTS_PER_GROUP = 4
N_EXPERTS = N_GROUPS * EXPERTS_PER_GROUP
TOP_K_IN_GROUP = 2
D_FF_EXPERT = 256
N_MOD = 6
EPS = 1e-6
IN_SPLITS = (ATTN_Q_W, ATTN_KV_W, ATTN_KV_W, DN_K_W, DN_K_W, DN_V_W,
             DN_DIRS * DN_HEADS, DN_DIRS * DN_HEADS, DN_V_W, D_MODEL, D_MODEL)
IN_W = ATTN_Q_W + 2 * ATTN_KV_W + 2 * DN_K_W + 2 * DN_V_W + 2 * DN_DIRS * DN_HEADS + 2 * D_MODEL

kernel_name = 'hybrid_flow_gqa_deltanet_hmoe_step'

def split_sizes(x, sizes):
    idx = np.cumsum(np.array(sizes))[:-1].tolist()
    return jnp.split(x, idx, axis=-1)

def rmsnorm(x, w):
    xf = x.astype(jnp.float32)
    y = xf * lax.rsqrt(jnp.mean(xf * xf, axis=-1, keepdims=True) + EPS)
    return (y * w.astype(jnp.float32)).astype(x.dtype)

def l2norm(x):
    return x * lax.rsqrt(jnp.sum(x * x, axis=-1, keepdims=True) + EPS)

def heads(x, n, d):
    b, l, _ = x.shape
    return x.reshape(b, l, n, d).transpose(0, 2, 1, 3)

def merge_heads(x):
    b, n, l, d = x.shape
    return x.transpose(0, 2, 1, 3).reshape(b, l, n * d)

def axial_rope(x):
    L = x.shape[2]
    rows = L // GRID_W
    row = jnp.repeat(jnp.arange(rows), GRID_W).astype(jnp.float32)
    col = jnp.tile(jnp.arange(GRID_W), rows).astype(jnp.float32)
    half = HEAD_DIM // 2
    inv = jnp.power(ROPE_THETA, -jnp.arange(0, half, 2, dtype=jnp.float32) / half)

    def rot(xa, pos):
        ang = pos[:, None] * inv[None, :]
        cos, sin = jnp.cos(ang), jnp.sin(ang)
        x1, x2 = xa[..., :half // 2], xa[..., half // 2:]
        return jnp.concatenate([x1 * cos - x2 * sin, x2 * cos + x1 * sin], axis=-1)

    xf = x.astype(jnp.float32)
    out = jnp.concatenate([rot(xf[..., :half], row), rot(xf[..., half:], col)], axis=-1)
    return out.astype(x.dtype)

def block_attention(q, k, v):
    B, H, Lq, Dh = q.shape
    nb = Lq // Q_BLOCK
    qb = jnp.moveaxis(q.reshape(B, ATTN_KV_HEADS, ATTN_GROUP, nb, Q_BLOCK, Dh), 3, 0)
    kf = k.astype(jnp.float32)
    vf = v.astype(jnp.float32)
    scale = Dh ** -0.5

    def one_block(qblk):
        s = jnp.einsum('bkgqd,bksd->bkgqs', qblk.astype(jnp.float32), kf) * scale
        p = jax.nn.softmax(s, axis=-1)
        return jnp.einsum('bkgqs,bksd->bkgqd', p, vf)

    o = lax.map(one_block, qb)
    o = jnp.moveaxis(o, 0, 3).reshape(B, H, Lq, Dh)
    return o.astype(q.dtype)

def centred_conv(x, w):
    L = x.shape[1]
    pad = CONV_W // 2
    xp = jnp.pad(x, ((0, 0), (pad, pad), (0, 0)))
    return sum(xp[:, i:i + L] * w[i] for i in range(CONV_W))

def gated_delta_chunked(q, k, v, beta, g, s0):
    B, H, L, DK = q.shape
    DV = v.shape[-1]
    n = L // CHUNK
    q = q.reshape(B, H, n, CHUNK, DK)
    k = k.reshape(B, H, n, CHUNK, DK)
    v = v.reshape(B, H, n, CHUNK, DV)
    beta = beta.reshape(B, H, n, CHUNK)
    g = jnp.cumsum(g.reshape(B, H, n, CHUNK), axis=-1)
    incl = jnp.tril(jnp.ones((CHUNK, CHUNK), dtype=bool))
    strict = jnp.tril(jnp.ones((CHUNK, CHUNK), dtype=bool), -1)
    diff = g[..., :, None] - g[..., None, :]
    decay = jnp.where(incl, jnp.exp(jnp.where(incl, diff, 0.0)), 0.0)
    k_beta = k * beta[..., None]
    v_beta = v * beta[..., None]
    lmat = jnp.where(strict, jnp.einsum('bhnik,bhnjk->bhnij', k_beta, k) * decay, 0.0)
    eye = jnp.eye(CHUNK, dtype=q.dtype)
    tmat = lax.linalg.triangular_solve(eye + lmat, jnp.broadcast_to(eye, lmat.shape),
                                       left_side=True, lower=True, unit_diagonal=True)
    u = jnp.einsum('bhnij,bhnjv->bhniv', tmat, v_beta)
    w = jnp.einsum('bhnij,bhnjk->bhnik', tmat, k_beta * jnp.exp(g)[..., None])
    intra = jnp.where(incl, jnp.einsum('bhnik,bhnjk->bhnij', q, k) * decay, 0.0)
    g_last = g[..., -1]
    q_dec = q * jnp.exp(g)[..., None]
    k_dec = k * jnp.exp(g_last[..., None] - g)[..., None]

    def step(S, xs):
        q_c, k_c, u_c, w_c, a_c, gl_c = xs
        v_new = u_c - jnp.einsum('bhck,bhkv->bhcv', w_c, S)
        o_c = jnp.einsum('bhck,bhkv->bhcv', q_c, S) + jnp.einsum('bhij,bhjv->bhiv', a_c, v_new)
        S = S * jnp.exp(gl_c)[..., None, None] + jnp.einsum('bhck,bhcv->bhkv', k_c, v_new)
        return S, o_c

    xs = tuple(jnp.moveaxis(t, 2, 0) for t in (q_dec, k_dec, u, w, intra, g_last))
    s_final, o = lax.scan(step, s0, xs)
    o = jnp.moveaxis(o, 0, 2).reshape(B, H, L, DV)
    return o, s_final

def delta_branch(dq, dk, dv, dbeta, dalpha, dgate, conv_w, a_log, dt_bias, dn_norm, s0):
    B, L, _ = dq.shape
    qkv = jax.nn.silu(centred_conv(jnp.concatenate([dq, dk, dv], axis=-1), conv_w))
    q, k, v = split_sizes(qkv, (DN_K_W, DN_K_W, DN_V_W))
    q = l2norm(heads(q, DN_HEADS, DN_DK).astype(jnp.float32)) * (DN_DK ** -0.5)
    k = l2norm(heads(k, DN_HEADS, DN_DK).astype(jnp.float32))
    v = heads(v, DN_HEADS, DN_DV).astype(jnp.float32)
    beta = jax.nn.sigmoid(dbeta.astype(jnp.float32)).reshape(B, L, DN_DIRS, DN_HEADS)
    g = -jnp.exp(a_log.astype(jnp.float32)) * jax.nn.softplus(
        dalpha.astype(jnp.float32).reshape(B, L, DN_DIRS, DN_HEADS) + dt_bias.astype(jnp.float32))
    beta = beta.transpose(2, 0, 3, 1)
    g = g.transpose(2, 0, 3, 1)
    o_f, s_f = gated_delta_chunked(q, k, v, beta[0], g[0], s0[:, 0])
    o_b, s_b = gated_delta_chunked(jnp.flip(q, 2), jnp.flip(k, 2), jnp.flip(v, 2),
                                   jnp.flip(beta[1], -1), jnp.flip(g[1], -1), s0[:, 1])
    o = rmsnorm(o_f + jnp.flip(o_b, 2), dn_norm)
    o = merge_heads(o).astype(dgate.dtype) * jax.nn.silu(dgate)
    return o, jnp.stack([s_f, s_b], axis=1)

def token_mixers(h, p, l, prefix_k, prefix_v, prefix_state):
    B, L, _ = h.shape
    proj = h @ p['w_in'][l]
    aq, ak, av, dq, dk, dv, dbeta, dalpha, dgate, g_attn, g_dn = split_sizes(proj, IN_SPLITS)
    aq = rmsnorm(heads(aq, ATTN_HEADS, HEAD_DIM), p['q_norm'][l])
    ak = rmsnorm(heads(ak, ATTN_KV_HEADS, HEAD_DIM), p['k_norm'][l])
    av = heads(av, ATTN_KV_HEADS, HEAD_DIM)
    if prefix_k is not None:
        keys = jnp.concatenate([prefix_k.astype(ak.dtype), axial_rope(ak)], axis=2)
        vals = jnp.concatenate([prefix_v.astype(av.dtype), av], axis=2)
        o_attn = block_attention(axial_rope(aq), keys, vals)
        s0 = prefix_state.astype(jnp.float32)
    else:
        o_attn = block_attention(aq, ak, av)
        s0 = jnp.zeros((B, DN_DIRS, DN_HEADS, DN_DK, DN_DV), jnp.float32)
    o_attn = merge_heads(o_attn)
    o_dn, s_final = delta_branch(dq, dk, dv, dbeta, dalpha, dgate, p['conv_w'][l], p['a_log'][l],
                                 p['dt_bias'][l], p['dn_norm'][l], s0)
    merged = (jax.nn.sigmoid(g_attn) * (o_attn @ p['w_attn_br'][l])
              + jax.nn.sigmoid(g_dn) * (o_dn @ p['w_dn_br'][l]))
    return merged @ p['w_out'][l], ak, av, s_final.astype(h.dtype)

def hier_moe(h, w_rg, b_rg, w_re, b_re, w_gate, w_up, w_down):
    B, L, D = h.shape
    t = h.reshape(B * L, D)
    T = t.shape[0]
    gp = jax.nn.softmax((t @ w_rg + b_rg).astype(jnp.float32), axis=-1)
    g_top, g_idx = lax.top_k(gp, 1)
    el = (t @ w_re + b_re).astype(jnp.float32).reshape(T, N_GROUPS, EXPERTS_PER_GROUP)
    el = jnp.take_along_axis(el, g_idx[:, :, None], axis=1)[:, 0]
    ep = jax.nn.softmax(el, axis=-1)
    e_top, e_idx = lax.top_k(ep, TOP_K_IN_GROUP)
    wts = e_top / jnp.sum(e_top, axis=-1, keepdims=True) * g_top
    expert = g_idx * EXPERTS_PER_GROUP + e_idx
    combine = jnp.sum(jax.nn.one_hot(expert, N_EXPERTS, dtype=jnp.float32) * wts[..., None], axis=1)
    hid = jax.nn.silu(jnp.einsum('td,edf->tef', t, w_gate)) * jnp.einsum('td,edf->tef', t, w_up)
    hid = hid * combine[..., None].astype(hid.dtype)
    y = jnp.einsum('tef,efd->td', hid, w_down)
    return y.reshape(B, L, D)

def adaln(cond, w_mod, b_mod):
    return (jax.nn.silu(cond) @ w_mod + b_mod)[:, None, :]

def trunk_layer(x, mod, p, l, prefix_k, prefix_v, prefix_state):
    shift1, scale1, gate1, shift2, scale2, gate2 = jnp.split(mod, N_MOD, axis=-1)
    h = rmsnorm(x, p['norm_mix'][l]) * (1.0 + scale1) + shift1
    m, ctx_k, ctx_v, ctx_state = token_mixers(h, p, l, prefix_k, prefix_v, prefix_state)
    x = x + gate1 * m
    h = rmsnorm(x, p['norm_ffn'][l]) * (1.0 + scale2) + shift2
    x = x + gate2 * hier_moe(h, p['w_rg'][l], p['b_rg'][l], p['w_re'][l], p['b_re'][l],
                             p['w_gate_e'][l], p['w_up_e'][l], p['w_down_e'][l])
    return x, ctx_k, ctx_v, ctx_state

def setup_inputs(seed: int = 0) -> dict:
    key = jax.random.key(seed)
    ks = jax.random.split(key, 32)
    f32 = jnp.float32
    D = D_MODEL

    def nrm(k, shape, scale):
        return jax.random.normal(k, shape, f32) * scale

    dt = jnp.exp(jax.random.uniform(ks[15], (DEPTH, DN_DIRS, DN_HEADS), f32, float(np.log(1e-3)), float(np.log(1e-1))))
    return {
        'x_prompt': nrm(ks[0], (BATCH, SEQ, D), 1.0),
        'x_sample': nrm(ks[1], (DEC_BATCH, DEC_SEQ, D), 1.0),
        'c': nrm(ks[2], (DEC_BATCH, D), 1.0),
        'cache_attn_k': nrm(ks[3], (DEC_BATCH, DEPTH, ATTN_KV_HEADS, PAST_LEN, HEAD_DIM), 1.0),
        'cache_attn_v': nrm(ks[4], (DEC_BATCH, DEPTH, ATTN_KV_HEADS, PAST_LEN, HEAD_DIM), 1.0),
        'state_delta': nrm(ks[5], (DEC_BATCH, DEPTH, DN_DIRS, DN_HEADS, DN_DK, DN_DV), 0.1),
        'c_ctx': nrm(ks[6], (D,), 1.0),
        'w_mod': nrm(ks[7], (DEPTH, D, N_MOD * D), D ** -0.5),
        'b_mod': nrm(ks[8], (DEPTH, N_MOD * D), 0.02),
        'norm_mix': 1.0 + nrm(ks[9], (DEPTH, D), 0.02),
        'norm_ffn': 1.0 + nrm(ks[10], (DEPTH, D), 0.02),
        'norm_final': 1.0 + nrm(ks[11], (D,), 0.02),
        'w_in': nrm(ks[12], (DEPTH, D, IN_W), D ** -0.5),
        'q_norm': 1.0 + nrm(ks[13], (DEPTH, HEAD_DIM), 0.02),
        'k_norm': 1.0 + nrm(ks[14], (DEPTH, HEAD_DIM), 0.02),
        'conv_w': nrm(ks[16], (DEPTH, CONV_W, CONV_CH), CONV_W ** -0.5),
        'a_log': jnp.log(jax.random.uniform(ks[17], (DEPTH, DN_DIRS, DN_HEADS), f32, 1.0, 16.0)),
        'dt_bias': jnp.log(jnp.expm1(dt)),
        'dn_norm': 1.0 + nrm(ks[18], (DEPTH, DN_DV), 0.02),
        'w_attn_br': nrm(ks[19], (DEPTH, ATTN_Q_W, D), ATTN_Q_W ** -0.5),
        'w_dn_br': nrm(ks[20], (DEPTH, DN_V_W, D), DN_V_W ** -0.5),
        'w_out': nrm(ks[21], (DEPTH, D, D), D ** -0.5),
        'w_rg': nrm(ks[22], (DEPTH, D, N_GROUPS), D ** -0.5),
        'b_rg': nrm(ks[23], (DEPTH, N_GROUPS), 0.01),
        'w_re': nrm(ks[24], (DEPTH, D, N_EXPERTS), D ** -0.5),
        'b_re': nrm(ks[25], (DEPTH, N_EXPERTS), 0.01),
        'w_gate_e': nrm(ks[26], (DEPTH, N_EXPERTS, D, D_FF_EXPERT), D ** -0.5),
        'w_up_e': nrm(ks[27], (DEPTH, N_EXPERTS, D, D_FF_EXPERT), D ** -0.5),
        'w_down_e': nrm(ks[28], (DEPTH, N_EXPERTS, D_FF_EXPERT, D), D_FF_EXPERT ** -0.5),
    }

def reference(x_prompt, x_sample, c, cache_attn_k, cache_attn_v, state_delta,
              c_ctx, w_mod, b_mod, norm_mix, norm_ffn, norm_final, w_in, q_norm, k_norm,
              conv_w, a_log, dt_bias, dn_norm, w_attn_br, w_dn_br, w_out,
              w_rg, b_rg, w_re, b_re, w_gate_e, w_up_e, w_down_e):
    p = dict(norm_mix=norm_mix, norm_ffn=norm_ffn, w_in=w_in, q_norm=q_norm, k_norm=k_norm,
             conv_w=conv_w, a_log=a_log, dt_bias=dt_bias, dn_norm=dn_norm,
             w_attn_br=w_attn_br, w_dn_br=w_dn_br, w_out=w_out,
             w_rg=w_rg, b_rg=b_rg, w_re=w_re, b_re=b_re,
             w_gate_e=w_gate_e, w_up_e=w_up_e, w_down_e=w_down_e)
    x_ctx = x_prompt
    x_lat = x_sample
    new_k, new_v, new_s = [], [], []
    for l in range(DEPTH):
        mod_ctx = adaln(c_ctx[None, :], w_mod[l], b_mod[l])
        x_ctx, ck, cv, cs = trunk_layer(x_ctx, mod_ctx, p, l, None, None, None)
        new_k.append(ck)
        new_v.append(cv)
        new_s.append(cs)
        mod_lat = adaln(c, w_mod[l], b_mod[l])
        x_lat, _, _, _ = trunk_layer(x_lat, mod_lat, p, l, cache_attn_k[:, l], cache_attn_v[:, l], state_delta[:, l])
    y_prompt = rmsnorm(x_ctx, norm_final)
    y_sample = rmsnorm(x_lat, norm_final)
    new_attn_k = jnp.stack(new_k, axis=1)
    new_attn_v = jnp.stack(new_v, axis=1)
    new_state_delta = jnp.stack(new_s, axis=1)
    return (y_prompt, y_sample, new_attn_k, new_attn_v, new_state_delta)


_drawn_inputs = setup_inputs


def setup_inputs(seed=0):
    import zlib

    import numpy as np

    out = dict(_drawn_inputs(seed))
    spreads = {}
    factors = {'state_delta': 2.944,
     'norm_final': 22.016,
     'q_norm': 8.0,
     'k_norm': 2.868,
     'dn_norm': 3.09,
     'b_rg': 12.294,
     'b_re': 24.968,
     'cache_attn_k': 8.0,
     'cache_attn_v': 8.0}
    for name, (base, spread) in spreads.items():
        noise = np.random.default_rng([zlib.crc32(name.encode()), seed]).standard_normal(out[name].shape)
        drawn = base * np.exp(spread * noise) if base else spread * noise
        out[name] = jnp.asarray(drawn.astype(out[name].dtype))
    for name, factor in factors.items():
        out[name] = (out[name] * factor).astype(out[name].dtype)
    return out
```

```python
from contextlib import ExitStack

import numpy as np

import concourse.bass as bass
from concourse import mybir

F32 = mybir.dt.float32
I32 = mybir.dt.int32
U32 = mybir.dt.uint32
ALU = mybir.AluOpType
ACT = mybir.ActivationFunctionType
AX = mybir.AxisListType

P = 128
D = 1024
KD = D // P
CTX, LAT, PAST = 256, 1024, 512
T = CTX + LAT
NT = T // P
GROUPS = [(0, 256), (256, 512), (768, 512)]
HD = 64
NH, NKV = 8, 2
C = 64
NCH = T // C
CTX_CH, LAT_CH = CTX // C, LAT // C
PAIRS = 8
EPS = 1e-6
NE, FF = 16, 256
MT = 2 * T // P + NE - 1
COL = dict(aq=0, ak=512, av=640, dq=768, dk=1280, dv=1792, ba=2304, dgate=2336, gattn=2848, gdn=3872)
NW = 6
LEVELS = 6


def shape_constants():
    part, free = np.arange(P), np.arange(P)
    half, t = part // C, part % C
    same = (half[:, None] == half[None, :]).astype(np.float32)
    j = np.arange(C)
    upto = [t[:, None] <= j[None, :], t[:, None] >= j[None, :]]
    upto_bd = [(t[:, None] <= t[None, :]) * same, (t[:, None] >= t[None, :]) * same]
    level = []
    for d in range(2):
        for l in range(LEVELS):
            b = 1 << l
            r, c = t[:, None] // b, j[None, :] // b
            lo, hi = (r, c) if d == 0 else (c, r)
            level.append((hi == lo + 1) & (lo % 2 == 0))
    rot = np.zeros((P, P), np.float32)
    for m in range(P):
        if m % 32 < 16:
            rot[m + 16, m] = -1.0
        else:
            rot[m - 16, m] = 1.0
    before = (part[:, None] < free[None, :]).astype(np.float32)
    parts = [np.eye(P), same, np.ones((P, P))] + upto + upto_bd + level + [t[:, None] == j[None, :], rot, before]
    return np.concatenate([np.asarray(a, np.float32) for a in parts], axis=1)


def small_constants():
    rows = [np.arange(T // P) * 128.0, np.arange(MT), (np.arange(NE)[None, :] < np.arange(NE)[:, None]).ravel()]
    row = np.concatenate([np.asarray(r, np.float32) for r in rows])
    return np.broadcast_to(row, (P, row.size)).copy()


def rotary_tables():
    half = HD // 2
    pos = np.arange(LAT)
    inv = np.power(np.float32(10000.0), -np.arange(0, half, 2, dtype=np.float32) / np.float32(half)).astype(np.float32)
    d = np.arange(P) % HD
    where = np.where((d < half)[:, None], (pos // 64)[None, :], (pos % 64)[None, :]).astype(np.float32)
    ang = (where * inv[d % 16][:, None]).astype(np.float32)
    return np.cos(ang).astype(np.float32), np.sin(ang).astype(np.float32)


def build(nc, a, outs):
    ctx = ExitStack()
    with ctx:
        def sb(name, shape, dt=F32):
            return ctx.enter_context(nc.sbuf_tensor(name, shape, dt))

        def sem(name):
            return ctx.enter_context(nc.semaphore(name))

        const_np, small_np = shape_constants(), small_constants()
        cos_np, sin_np = rotary_tables()
        const_d = nc.inline_tensor(const_np, name="shape_constants")
        small_d = nc.inline_tensor(small_np, name="small_constants")
        cos_d = nc.inline_tensor(cos_np, name="rotary_cos")
        sin_d = nc.inline_tensor(sin_np, name="rotary_sin")

        attn_d = nc.dram_tensor("attn_out_scratch", [P, 4, T], F32).ap()
        h2_d = nc.dram_tensor("h2_scratch", [T, D], F32).ap()
        slot_d = nc.dram_tensor("slot_token", [MT * P, 1], U32).ap()
        y_d = nc.dram_tensor("slot_output", [MT * P, D], F32).ap()

        cst = sb("cst", [P, const_np.shape[1]])
        at = [0]

        def take(n):
            at[0] += n
            return cst[:, at[0] - n:at[0]]

        ident, same_head, ones = take(P), take(P), take(P)
        upto = take(2 * C).rearrange("p (d c) -> p d c", d=2)
        upto_bd = take(2 * P).rearrange("p (d c) -> p d c", d=2)
        levels = take(2 * LEVELS * C).rearrange("p (d l c) -> p d l c", d=2, l=LEVELS)
        eye_st, rot, before = take(C), take(P), take(P)
        small = sb("small", [P, small_np.shape[1]])
        k128 = small[:, 0:10]
        tile_no = small[:, 10:10 + MT]
        precedes = small[:, 10 + MT:10 + MT + NE * NE].rearrange("p (e f) -> p e f", e=NE)

        cond = sb("cond", [P, KD, 2])
        cond_s = sb("cond_s", [P, KD, 2])
        b_mod = sb("b_mod", [P, 48])
        norm_mix = sb("norm_mix", [P, KD])
        norm_ffn = sb("norm_ffn", [P, KD])
        mod = sb("mod", [P, 48, 2])
        A1 = sb("A1", [P, KD, 2])
        A2 = sb("A2", [P, KD, 2])
        qk_w = sb("qk_w", [P, 2])
        conv_w = sb("conv_w", [P, 12, 3])
        dnn_w = sb("dnn_w", [P, 1])
        a_log = sb("a_log", [P, 16])
        dt_b = sb("dt_b", [P, 16])
        b_r = sb("b_r", [P, 20])
        stat = sb("stat", [P, 64])
        epsc = sb("epsc", [P, 5])
        ba = sb("ba", [P, NT, 32])
        bg = sb("bg", [P, 2, 2, NT, 8])
        bg_st = sb("bg_st", [P, 2, 2, NT, 8])
        S_ctx = sb("S_ctx", [P, PAIRS, C])
        S_lat = sb("S_lat", [P, PAIRS, C])

        R0 = sb("R0", [P, KD * T])
        R1 = sb("R1", [P, 8704])
        R3 = sb("R3", [P, 12 * T])
        R4 = sb("R4", [P, 12288])

        hT = R0[:, :].rearrange("p (k t) -> p k t", k=KD)
        x2 = R0[:, :].rearrange("p (n d) -> p n d", n=NT)
        qT = R1[:, 0:4 * T].rearrange("p (a t) -> p a t", a=4)
        kT = R1[:, 4 * T:4 * T + T + PAST]
        v_sb = R1[:, 6912:6912 + 14 * P].rearrange("p (n d) -> p n d", n=14)

        ps = ctx.enter_context(nc.psum_tensor("ps", [P, 8, 512], F32))

        block = ctx.enter_context(nc.Block())

        names = """params_in consts_in cond_sig cond_ready eps_ready onr_sum onr_root wmod_used ssx_ready rstdx_ready
          xn_ready xt_done xt_used w_used vw_in vba_mm vba_used past_in pastT pastT_used gemm gemm_used conv_ready
          sigm_ready z_ready sq_ready ssq root_ready rot_mm rot_used y_ready tile_done kout_mm kout_used kv_out
          dec_abs beta_ready dec_ln bg_ready bg_moved sc_ready mx_ready p_ready pt_mm pt_dve pt_act pv_done o_ready
          ot_mm ot_used attn_out bd_zeroed dn_pe dn_dve dn_act dn_stage dn_acc state_in state_out osq_ready
          on_ready odT_mm od_ready dgw_in gate_mm gsig_ready gate_used attn_back mw_used merge_mm msig_ready merged
          row_rhs row_mm row_used ow_in out_mm out_used rw_in ss2_ready h2_ready h2t_mm h2t_used rout_mm rout_used
          lg_shift lg_exp masks_ready rank_mm pos_ready slot_zero slot_scat idx_in ew_used hst_mm hst_used gu_mm
          gu_sig hid_ready hidt_mm hidt_used dn_mm ysb_ready x3_ready ss3_ready out_ready fin_out dve_chain
          act_chain pool_chain arrivals""".split()
        rings = dict(wmod_in=3, x_in=3, w_in=NW, mw_in=2, xr_in=2, ew_in=2, hs_in=2, y_in=2, h2_out=2, y_out=2)
        names += [f"{n}{i}" for n, k in rings.items() for i in range(k)]
        S = {n: sem(n) for n in names}

        counts = {n: 0 for n in names}

        def count(name):
            counts[name] += 1
            return counts[name]

        def landed(n, buffers, dmas=1):
            return 16 * dmas * (n // buffers + 1)

        ctx.enter_context(nc.allow_non_contiguous_dma("parameters, once, and strips of weights"))

        w_in_v = a["w_in"][0].rearrange("(k p) n -> p k n", p=P)
        w_mod_v = a["w_mod"][0].rearrange("(k p) n -> p k n", p=P)

        wmod_sb = [R4[:, i * 4096:(i + 1) * 4096].rearrange("p (k n) -> p k n", k=KD) for i in range(3)]
        w_sb = [R4[:, i * 1024:(i + 1) * 1024].rearrange("p (k n) -> p k n", k=KD) for i in range(NW)]
        vw = R4[:, 6144:6144 + 1280].rearrange("p (k n) -> p k n", k=KD)

        TILES = [("aq", i) for i in range(4)] + [("ak", 0)] + [(n, i) for n in ("dq", "dk", "dv") for i in range(4)]
        NA = 5

        x_v = [a["x_prompt"][0].rearrange("(n p) d -> n p d", p=P), a["x_sample"][0].rearrange("(n p) d -> n p d", p=P)]

        def x_tile(n):
            return x_v[0][n] if n < 2 else x_v[1][n - 2]

        xs = [R3[:, i * D:(i + 1) * D] for i in range(3)]
        xn = [R3[:, (3 + i) * D:(4 + i) * D] for i in range(2)]
        junk = R3[:, 5 * D:6 * D]

        TP = T + 4
        def scratch(n):
            base, r = (6144, R3) if n < NA else (0, R1)
            o = base
            raw = [r[:, o + i * TP:o + (i + 1) * TP] for i in range(2)]
            sq = [r[:, o + (2 + i) * TP:o + (2 + i) * TP + T] for i in range(2)]
            tmp = r[:, o + 4 * TP:o + 4 * TP + T]
            rstd = r[:, o + 5 * TP:o + 5 * TP + T]
            return raw[n % 2], sq[n % 2], tmp, rstd

        cos_t, sin_t = R3[:, 1536:2560], R3[:, 2560:3584]
        dT = R3[:, :].rearrange("p (a t) -> p a t", a=12)

        def out_of(n):
            kind, i = TILES[n]
            if kind == "aq":
                return qT[:, i, :]
            if kind == "ak":
                return kT[:, 0:T]
            return dT[:, {"dq": 0, "dk": 4, "dv": 8}[kind] + i, :]

        def stats(n):
            return TILES[n][0] != "dv"

        past = R3[:, 0:2 * 4 * P].rearrange("p (n c) -> p n c", c=P)
        ktok = R3[:, 1024:1024 + 2 * P].rearrange("p (n c) -> p n c", c=P)

        p_sb = [R3[:, i * 1536:(i + 1) * 1536] for i in range(2)]
        pT = [R3[:, 3072 + i * 1536:3072 + (i + 1) * 1536].rearrange("p (n c) -> p n c", c=P) for i in range(2)]
        o_tok = R3[:, 6144:6144 + 512]
        oT = R3[:, 6656:6656 + 4 * T].rearrange("p (a t) -> p a t", a=4)
        ast = R3[:, 12000:12000 + 64]
        ITEMS = [(qt, g, h4) for qt in range(NT) for h4 in range(4) for g in range(2)]

        def keys(qt):
            return (0, 2, 0) if qt < 2 else (CTX, 12, 2)

        oacc = R1[:, 0:NCH * 256].rearrange("p (c a d) -> p c a d", c=NCH, a=4)
        spot = {"R4": 0, "R1": NCH * 256}

        def scr(n, region="R4"):
            o = spot[region]
            spot[region] += n
            r = {"R4": R4, "R1": R1}[region][:, o:o + n]
            return r.rearrange("p (a c) -> p a c", a=PAIRS)

        k_bd, q_bd, v_bd, ktok_bd, L_bd, A_bd, X_bd, U_bd, T_bd = [scr(1024) for _ in range(9)]
        X_st, U_st, T_st, gM, Dm, E = [scr(512) for _ in range(6)]
        V_st, R_st, vn, vd, o1, oo = [scr(512, "R1") for _ in range(6)]
        gs = sb("gs", [P, 64])

        PE_STEPS = ["g", "kk", "kq", "kt0", "kt1", "v", "ks", "qs", "x0", "t0"]
        for l in range(1, LEVELS):
            PE_STEPS += [f"x{l}", f"u{l}"] + ([f"t{l}"] if l < LEVELS - 1 else [])
        PE_STEPS += ["vn", "av", "s"]
        DVE_STEPS = ["gm0", "gm1", "b0", "b1", "gc", "glg", "diff", "abs", "eb", "l0", "l1", "x0", "u0", "t0",
                     "ea", "a0", "a1", "r0", "r1", "r2"]
        for l in range(1, LEVELS):
            DVE_STEPS += [f"x{l}"] + ([f"u{l}", f"t{l}"] if l < LEVELS - 1 else ["ub0", "ub1"])
        DVE_STEPS += ["vd", "o0", "o1", "s0", "s1"]
        ACT_STEPS = ["eg", "e", "kt0", "kt1", "v"]
        for l in range(LEVELS - 1):
            ACT_STEPS += [f"xb{l}0", f"xb{l}1", f"tb{l}0", f"tb{l}1"]
        ACT_STEPS += ["vn"]
        STAGE_STEPS = [f"{x}{d}{h}" for x in "kqv" for d in "fb" for h in "01"]
        ORDER = {"dn_pe": PE_STEPS, "dn_dve": DVE_STEPS, "dn_act": ACT_STEPS, "dn_stage": STAGE_STEPS, "dn_acc": ["f", "b"]}
        CHUNKS = [(s, CTX_CH - 1 - s) for s in range(CTX_CH)] + \
                 [(CTX_CH + s, CTX_CH + LAT_CH - 1 - s) for s in range(LAT_CH)]

        def value(name, step, s):
            return s * len(ORDER[name]) + ORDER[name].index(step) + 1

        def flat(x):
            return x.rearrange("p a c -> p (a c)")

        def bank8(i):
            return ps[:, i, :].rearrange("p (a c) -> p a c", a=PAIRS)

        odT = R3[:, 0:4 * T].rearrange("p (a t) -> p a t", a=4)
        mT = R3[:, 4 * T:12 * T].rearrange("p (k t) -> p k t", k=KD)
        onsq = R4[:, 0:5120]
        onr = R4[:, 5120:5120 + 80]
        on_bd = [R4[:, 5248 + i * 512:5248 + (i + 1) * 512].rearrange("p (a c) -> p a c", a=4) for i in range(2)]
        dgw = R4[:, 6400:6400 + 4096].rearrange("p (k n) -> p k n", k=KD)
        sgd = R4[:, 10496:10496 + 512]
        tdg = R4[:, 11008:11008 + 512]
        onf = R1[:, 6400:6400 + 1024].rearrange("p (c a d) -> p c a d", c=4, a=4)
        odn_raw = R3[:, 8 * T:12 * T].rearrange("p (a t) -> p a t", a=4)

        MWB = 3072
        mw = [R4[:, i * MWB:(i + 1) * MWB] for i in range(2)]
        aoT = R1[:, 0:4 * T].rearrange("p (a t) -> p a t", a=4)
        sg = [R4[:, 6144 + i * 512:6656 + i * 512] for i in range(4)]
        m1 = [R4[:, 8192 + i * 512:8704 + i * 512] for i in range(4)]
        MU = [(c, g) for c in range(KD) for g in range(3)]

        ROWS = ["gate1", "A2", "B2", "gate2"]
        rows = R1[:, 0:8192].rearrange("p (r c d) -> p r c d", r=4, c=2)
        row_rhs = [R4[:, 10240 + i * 512:10752 + i * 512] for i in range(2)]
        ow = R4[:, 0:8192].rearrange("p (k n) -> p k n", k=KD)
        xr = [R4[:, 8192 + i * D:8192 + (i + 1) * D] for i in range(2)]

        CTX_ITEMS = 8 * CTX // P
        NSTAT = NA + 8
        bt = R3[:, 13900:14060].rearrange("p (n c) -> p n c", n=NT)
        gt = R3[:, 14060:14220].rearrange("p (n c) -> p n c", n=NT)
        zt = R3[:, 14220:14380].rearrange("p (n c) -> p n c", n=NT)
        one_c, eps_head, eps_unit = epsc[:, 0:1], epsc[:, 2:3], epsc[:, 3:4]

        h2 = [R3[:, i * D:(i + 1) * D] for i in range(2)]
        h2T = [R3[:, (2 + i) * D:(3 + i) * D].rearrange("p (k t) -> p k t", k=KD) for i in range(2)]
        rw = R3[:, 4096:4096 + 160].rearrange("p (k n) -> p k n", k=KD)
        lg = R3[:, 4352:4352 + 200].rearrange("p (n c) -> p n c", n=NT)
        rs = R3[:, 4608:4608 + 3000]
        EW = 6144
        ew = [R4[:, i * EW:(i + 1) * EW] for i in range(2)]
        hs = [R3[:, 8192 + i * D:8192 + (i + 1) * D] for i in range(2)]
        hsT = [h2T[i] for i in range(2)]
        hid = R3[:, 11264:11264 + 256]
        sgh = R3[:, 11520:11520 + 256]
        hidT = R3[:, 11776:11776 + 256].rearrange("p (k t) -> p k t", k=2)
        y_sb = [R3[:, 12032 + i * D:12032 + (i + 1) * D] for i in range(2)]
        rat = [4608]

        def rsc(*shape):
            n = int(np.prod(shape))
            rat[0] += n
            r = R3[:, rat[0] - n:rat[0]]
            if len(shape) == 2:
                r = r.rearrange("p (a b) -> p a b", a=shape[0])
            return r

        r_gm, r_m1, r_m2, r_seen, r_not = [rsc(NT, 1) for _ in range(5)]
        r_ohg, r_oh1, r_oh2, r_el, r_el2, r_sel = [rsc(NT, 4) for _ in range(6)]
        r_e5 = rsc(NT, 5)
        m_one, m_two, m_all, r_cnt = [rsc(NT, NE) for _ in range(4)]
        r_pre = rsc(NT + 1, NE)
        r_cmp = rsc(MT * NE)
        r_nt, r_base, r_tex = rsc(NE), rsc(NE), rsc(MT)
        r_pos = rsc(2, NT)
        assert rat[0] <= 8192
        slot_i = sb("slot_i", [P, MT], U32)
        pos_i = sb("pos_i", [P, 2, NT], U32)
        tok_i = sb("tok_i", [P, NT], I32)
        tex_i = sb("tex_i", [P, MT], I32)
        nf_row = R3[:, 14080:14080 + 1024]
        wts = sb("wts", [P, 2, NT])
        yg = [R3[:, i * D:(i + 1) * D] for i in range(4)]

        y_out_v = [outs[0][0].rearrange("(n p) d -> n p d", p=P), outs[1][0].rearrange("(n p) d -> n p d", p=P)]

        def moe_weights(t):
            return ew[t % 2]

        @block.sync
        def _(sp):
            for o, i in [(cst[:], const_d.ap()), (small[:], small_d.ap())]:
                sp.dma_start(o, i).then_inc(S["consts_in"], 16)
            small_loads = [
                (cond[:, :, 0], a["c_ctx"].rearrange("(k p) -> p k", p=P)),
                (cond[:, :, 1], a["c"][0].rearrange("(k p) -> p k", p=P)),
                (b_mod[:], a["b_mod"][0].rearrange("(k p) -> p k", p=P)),
                (norm_mix[:], a["norm_mix"][0].rearrange("(k p) -> p k", p=P)),
                (norm_ffn[:], a["norm_ffn"][0].rearrange("(k p) -> p k", p=P)),
                (a_log[:], a["a_log"].rearrange("x d h -> x (d h)").broadcast_to([P, 16])),
                (dt_b[:], a["dt_bias"].rearrange("x d h -> x (d h)").broadcast_to([P, 16])),
                (b_r[:, 0:4], a["b_rg"].broadcast_to([P, 4])),
                (b_r[:, 4:20], a["b_re"].broadcast_to([P, 16])),
            ]
            for h in range(2):
                small_loads += [(qk_w[h * HD:(h + 1) * HD, 0:1], a["q_norm"][0].unsqueeze(1)),
                                (qk_w[h * HD:(h + 1) * HD, 1:2], a["k_norm"][0].unsqueeze(1)),
                                (dnn_w[h * HD:(h + 1) * HD, 0:1], a["dn_norm"][0].unsqueeze(1))]
            for tap in range(3):
                small_loads.append((conv_w[:, :, tap], a["conv_w"][0, tap].rearrange("(k p) -> p k", p=P)))
            for o, i in small_loads:
                sp.dma_start(o, i).then_inc(S["params_in"], 16)
            for i in range(12):
                if i - 2 > 0:
                    sp.wait_ge(S["wmod_used"], i - 2)
                sp.dma_start(wmod_sb[i % 3], w_mod_v[:, :, i * 512:(i + 1) * 512]).then_inc(S[f"wmod_in{i % 3}"], 16)
                if i < 3:
                    sp.dma_start(xs[i], x_tile(i)).then_inc(S[f"x_in{i}"], 16)
            for n in range(3, NT):
                if n - 2 > 0:
                    sp.wait_ge(S["xn_ready"], n - 2)
                sp.dma_start(xs[n % 3], x_tile(n)).then_inc(S[f"x_in{n % 3}"], 16)
            sp.wait_ge(S["wmod_used"], 12)

            def strip(n):
                kind, i = TILES[n]
                if n - NW + 1 > 0:
                    sp.wait_ge(S["w_used"], n - NW + 1)
                if kind == "aq":
                    for g in range(2):
                        col = COL["aq"] + (i + 4 * g) * HD
                        sp.dma_start(w_sb[n % NW][:, :, g * HD:(g + 1) * HD], w_in_v[:, :, col:col + HD]).then_inc(S[f"w_in{n % NW}"], 16)
                else:
                    col = COL[kind] + i * P
                    sp.dma_start(w_sb[n % NW], w_in_v[:, :, col:col + P]).then_inc(S[f"w_in{n % NW}"], 16)

            for n in range(NA):
                strip(n)
            sp.dma_start(vw[:, :, 0:P], w_in_v[:, :, COL["av"]:COL["av"] + P]).then_inc(S["vw_in"], 16)
            sp.dma_start(vw[:, :, P:160], w_in_v[:, :, COL["ba"]:COL["ba"] + 32]).then_inc(S["vw_in"], 16)
            sp.wait_ge(S["xt_done"], 2 * NT)
            sp.dma_start(cos_t, cos_d.ap()).then_inc(S["past_in"], 16)
            sp.dma_start(sin_t, sin_d.ap()).then_inc(S["past_in"], 16)
            for g in range(2):
                sp.dma_start(past[:, 0:4, g * HD:(g + 1) * HD], a["cache_attn_k"][0, 0, g].rearrange("(n p) d -> p n d", p=P)).then_inc(S["past_in"], 16)
                sp.dma_start(v_sb[:, NT:14, g * HD:(g + 1) * HD], a["cache_attn_v"][0, 0, g].rearrange("(n p) d -> p n d", p=P)).then_inc(S["past_in"], 16)
            sp.wait_ge(S["vba_used"], NT)
            for g in range(2):
                sp.dma_start(outs[3][0, 0, g].rearrange("(n p) d -> p n d", p=P), v_sb[:, 0:2, g * HD:(g + 1) * HD]).then_inc(S["kv_out"], 16)
            sp.wait_ge(S["kout_used"], 1)
            for g in range(2):
                sp.dma_start(outs[2][0, 0, g].rearrange("(n p) d -> p n d", p=P), ktok[:, :, g * HD:(g + 1) * HD]).then_inc(S["kv_out"], 16)
            sp.wait_ge(S["kv_out"], 64)
            sp.wait_ge(S["bg_ready"], 1)
            for h in range(2):
                for cp in range(2):
                    for x in range(2):
                        sp.dma_start(bg_st[h * C:(h + 1) * C, x, cp], bg[cp * C:(cp + 1) * C, x, h]).then_inc(S["bg_moved"], 16)
            sp.wait_ge(S["bg_moved"], 128)
            sp.sem_inc(S["arrivals"], 1)
            sp.wait_ge(S["arrivals"], 5 * 1)
            for n in range(NA, NA + NW):
                strip(n)
            sp.wait_ge(S["ot_used"], NT)
            sp.dma_start(attn_d, oT).then_inc(S["attn_out"], 16)
            sp.wait_ge(S["attn_out"], 16)
            sp.sem_inc(S["arrivals"], 1)
            sp.wait_ge(S["arrivals"], 5 * 2)
            for n in range(NA + NW, len(TILES)):
                strip(n)
            for d in range(2):
                for h in range(2):
                    sp.dma_start(S_lat[h * HD:(h + 1) * HD, 4 * d:4 * d + 4, :], a["state_delta"][0, 0, d].rearrange("(a h) k v -> h k a v", h=2)[h]).then_inc(S["state_in"], 16)
            sp.sem_inc(S["arrivals"], 1)
            sp.wait_ge(S["arrivals"], 5 * 3)
            if value("dn_dve", "s1", CTX_CH - 1) > 0:
                sp.wait_ge(S["dn_dve"], value("dn_dve", "s1", CTX_CH - 1))
            for d in range(2):
                for h in range(2):
                    sp.dma_start(outs[4][0, 0, d].rearrange("(a h) k v -> h k a v", h=2)[h], S_ctx[h * HD:(h + 1) * HD, 4 * d:4 * d + 4, :]).then_inc(S["state_out"], 16)
            sp.wait_ge(S["state_out"], 64)
            sp.sem_inc(S["arrivals"], 1)
            sp.wait_ge(S["arrivals"], 5 * 4)
            sp.dma_start(dgw, w_in_v[:, :, COL["dgate"]:COL["dgate"] + 512]).then_inc(S["dgw_in"], 16)
            sp.sem_inc(S["arrivals"], 1)
            sp.wait_ge(S["arrivals"], 5 * 5)
            sp.dma_start(aoT, attn_d).then_inc(S["attn_back"], 16)
            wa = a["w_attn_br"][0].rearrange("(k p) n -> p k n", p=P)
            wd = a["w_dn_br"][0].rearrange("(k p) n -> p k n", p=P)
            for c in range(KD):
                if c - 1 > 0:
                    sp.wait_ge(S["mw_used"], c - 1)
                b = mw[c % 2]
                cs = slice(c * P, (c + 1) * P)
                sp.dma_start(b[:, 0:1024].rearrange("p (k n) -> p k n", k=KD), w_in_v[:, :, COL["gattn"] + c * P:COL["gattn"] + (c + 1) * P]).then_inc(S[f"mw_in{c % 2}"], 16)
                sp.dma_start(b[:, 1024:2048].rearrange("p (k n) -> p k n", k=KD), w_in_v[:, :, COL["gdn"] + c * P:COL["gdn"] + (c + 1) * P]).then_inc(S[f"mw_in{c % 2}"], 16)
                sp.dma_start(b[:, 2048:2560].rearrange("p (k n) -> p k n", k=4), wa[:, :, cs]).then_inc(S[f"mw_in{c % 2}"], 16)
                sp.dma_start(b[:, 2560:3072].rearrange("p (k n) -> p k n", k=4), wd[:, :, cs]).then_inc(S[f"mw_in{c % 2}"], 16)
            sp.sem_inc(S["arrivals"], 1)
            sp.wait_ge(S["arrivals"], 5 * 6)
            sp.dma_start(ow, a["w_out"][0].rearrange("(k p) n -> p k n", p=P)).then_inc(S["ow_in"], 16)
            for n in range(NT):
                if n - 1 > 0:
                    sp.wait_ge(S["out_used"], n - 1)
                sp.dma_start(xr[n % 2], x_tile(n)).then_inc(S[f"xr_in{n % 2}"], 16)
            sp.sem_inc(S["arrivals"], 1)
            sp.wait_ge(S["arrivals"], 5 * 7)
            sp.dma_start(rw[:, :, 0:4], a["w_rg"][0].rearrange("(k p) n -> p k n", p=P)).then_inc(S["rw_in"], 16)
            sp.dma_start(rw[:, :, 4:20], a["w_re"][0].rearrange("(k p) n -> p k n", p=P)).then_inc(S["rw_in"], 16)
            sp.dma_start(nf_row, a["norm_final"].unsqueeze(0).broadcast_to([P, D])).then_inc(S["rw_in"], 16)
            for n in range(NT):
                sp.wait_ge(S["h2_ready"], n + 1)
                sp.dma_start(h2_d[n * P:(n + 1) * P, :], h2[n % 2]).then_inc(S[f"h2_out{n % 2}"], 16)
            sp.wait_ge(S["pos_ready"], 1)
            for t in range(MT):
                e = sp.value_load(tex_i[0:1, t:t + 1], min_val=0, max_val=NE - 1)
                if t - 1 > 0:
                    sp.wait_ge(S["ew_used"], t - 1)
                b = ew[t % 2]
                for half, name in enumerate(("w_gate_e", "w_up_e")):
                    src = a[name][0][bass.ds(e, 1)].rearrange("e (k p) f -> p (e k) f", p=P)
                    sp.dma_start(b[:, 0:4096].rearrange("p (k n) -> p k n", k=KD)[:, :, half * FF:(half + 1) * FF], src).then_inc(S[f"ew_in{t % 2}"], 16)
                src = a["w_down_e"][0][bass.ds(e, 1)].rearrange("e (k p) n -> p (e k) n", p=P)
                sp.dma_start(b[:, 4096:6144].rearrange("p (k n) -> p k n", k=2), src).then_inc(S[f"ew_in{t % 2}"], 16)
            sp.sem_inc(S["arrivals"], 1)
            sp.wait_ge(S["arrivals"], 5 * 8)
            for n in range(NT):
                sp.wait_ge(S["out_ready"], n + 1)
                sp.dma_start(y_out_v[0][n] if n < 2 else y_out_v[1][n - 2], x2[:, n, :]).then_inc(S["fin_out"], 16)
            sp.wait_ge(S["fin_out"], 16 * NT)

        @block.tensor
        def _(pe):
            mm = nc.tensor.matmul
            turn128 = nc.tensor.transpose


            pe.wait_ge(S["consts_in"], 32)
            pe.wait_ge(S["cond_ready"], 1)
            for i in range(12):
                pe.wait_ge(S[f"wmod_in{i % 3}"], landed(i, 3))
                for f in range(4):
                    o = 2 * (4 * i + f)
                    for k in range(KD):
                        last = mm(ps[:, 0, o:o + 2], wmod_sb[i % 3][:, k, f * P:(f + 1) * P], cond_s[:, k, :],
                                  start=(k == 0), stop=(k == KD - 1))
                last.then_inc(S["wmod_used"], 1)
            for n in range(NT):
                pe.wait_ge(S["xn_ready"], n + 1)
                for h in range(2):
                    u = 2 * n + h
                    if u - 3 > 0:
                        pe.wait_ge(S["xt_used"], u - 3)
                    for k in range(4):
                        last = turn128(ps[:, 1 + u % 4, k * P:(k + 1) * P], xn[n % 2][:, (4 * h + k) * P:(4 * h + k + 1) * P], ident)
                    last.then_inc(S["xt_done"], 1)
            pe.wait_ge(S["xt_used"], 2 * NT)

            def gemm(n):
                pe.wait_ge(S[f"w_in{n % NW}"], 16 * (n // NW + 1 + (n % NW < 4)))
                for g, (c0, w) in enumerate(GROUPS):
                    u = 3 * n + g
                    if u - 3 > 0:
                        pe.wait_ge(S["gemm_used"], u - 3)
                    for k in range(KD):
                        last = mm(ps[:, u % 4, 0:w], w_sb[n % NW][:, k, :], hT[:, k, c0:c0 + w],
                                  start=(k == 0), stop=(k == KD - 1))
                    last.then_inc(S["gemm"], 1)
                pe.wait_ge(S["gemm"], 3 * n + 3)
                pe.sem_inc(S["w_used"], 1)

            def ssq(n):
                if not stats(n):
                    return
                pe.wait_ge(S["sq_ready"], n + 1)
                if 3 * n > 0:
                    pe.wait_ge(S["root_ready"], 3 * n)
                if 2 * min(n, NA) > 0:
                    pe.wait_ge(S["rot_used"], 2 * min(n, NA))
                for g, (c0, w) in enumerate(GROUPS):
                    mm(ps[:, 4 + g, 0:w], same_head, scratch(n)[1][:, c0:c0 + w], start=True, stop=True).then_inc(S["ssq"], 1)

            def rotate(n):
                pe.wait_ge(S["y_ready"], n + 1)
                for g in (1, 2):
                    c0, w = GROUPS[g]
                    mm(ps[:, 4 + g, 0:w], rot, out_of(n)[:, c0:c0 + w], start=True, stop=True).then_inc(S["rot_mm"], 1)

            def tiles(first, end):
                for n in range(first, end + 2):
                    if n < end:
                        gemm(n)
                    if first <= n - 2 < NA:
                        rotate(n - 2)
                    if first <= n - 1 < end:
                        ssq(n - 1)

            pe.wait_ge(S["past_in"], 96)
            tiles(0, NA)
            pe.wait_ge(S["vw_in"], 32)
            pe.wait_ge(S["gemm_used"], 3 * NA)
            for n in range(NT):
                if n - 1 > 0:
                    pe.wait_ge(S["vba_used"], n - 1)
                for k in range(KD):
                    last = mm(ps[:, n % 2, 0:160], hT[:, k, n * P:(n + 1) * P], vw[:, k, :], start=(k == 0), stop=(k == KD - 1))
                last.then_inc(S["vba_mm"], 1)
            for n in range(4):
                last = turn128(ps[:, 2, n * P:(n + 1) * P], past[:, n, :], ident)
            last.then_inc(S["pastT"], 1)
            pe.wait_ge(S["tile_done"], NA)
            for n in range(2):
                last = turn128(ps[:, 3, n * P:(n + 1) * P], kT[:, n * P:(n + 1) * P], ident)
            last.then_inc(S["kout_mm"], 1)
            pe.wait_ge(S["kout_mm"], 1)
            pe.sem_inc(S["arrivals"], 1)
            pe.wait_ge(S["arrivals"], 5 * 1)

            def scores(i):
                qt, g, h4 = ITEMS[i]
                c0, nk, _ = keys(qt)
                if i - 1 > 0:
                    pe.wait_ge(S["pt_dve"], i - 1)
                if i - 1 - CTX_ITEMS > 0:
                    pe.wait_ge(S["pt_act"], i - 1 - CTX_ITEMS)
                lo = slice(g * HD, (g + 1) * HD)
                for j in range((nk + 3) // 4):
                    w = min(512, nk * P - j * 512)
                    last = mm(ps[:, 3 * (i % 2) + j, 0:w], qT[lo, h4, qt * P:(qt + 1) * P], kT[lo, c0 + j * 512:c0 + j * 512 + w],
                              start=True, stop=True)
                last.then_inc(S["sc_ready"], 1)

            def turn(i):
                nk = keys(ITEMS[i][0])[1]
                pe.wait_ge(S["p_ready"], i + 1)
                for j in range(nk):
                    last = turn128(ps[:, 3 * (i % 2) + j // 4, (j % 4) * P:(j % 4 + 1) * P], p_sb[i % 2][:, j * P:(j + 1) * P], ident)
                last.then_inc(S["pt_mm"], 1)

            def values(i):
                qt, g, h4 = ITEMS[i]
                _, nk, v0 = keys(qt)
                pe.wait_ge(S["pt_dve"], i + 1)
                if i + 1 - CTX_ITEMS > 0:
                    pe.wait_ge(S["pt_act"], i + 1 - CTX_ITEMS)
                if i % 8 == 0:
                    if qt - 1 > 0:
                        pe.wait_ge(S["ot_used"], qt - 1)
                h = h4 + 4 * g
                for j in range(nk):
                    last = mm(ps[:, 6 + qt % 2, h * HD:(h + 1) * HD], pT[i % 2][:, j, :], v_sb[:, v0 + j, g * HD:(g + 1) * HD],
                              start=(j == 0), stop=(j == nk - 1))
                last.then_inc(S["pv_done"], 1)

            def turn_out(qt):
                pe.wait_ge(S["o_ready"], qt + 1)
                for k in range(4):
                    last = turn128(ps[:, 6 + qt % 2, k * P:(k + 1) * P], o_tok[:, k * P:(k + 1) * P], ident)
                last.then_inc(S["ot_mm"], 1)

            NI = len(ITEMS)
            for i in range(NI + 2):
                if i < NI:
                    scores(i)
                if 1 <= i <= NI:
                    turn(i - 1)
                if i >= 2:
                    values(i - 2)
                    if (i - 2) % 8 == 2 and i > 8:
                        turn_out((i - 2) // 8 - 1)
            turn_out(NT - 1)
            pe.wait_ge(S["ot_used"], NT)
            pe.sem_inc(S["arrivals"], 1)
            pe.wait_ge(S["arrivals"], 5 * 2)
            tiles(NA, len(TILES))
            pe.wait_ge(S["tile_done"], len(TILES))
            pe.sem_inc(S["arrivals"], 1)
            pe.wait_ge(S["arrivals"], 5 * 3)

            pe.wait_ge(S["bd_zeroed"], 1)
            for s, (cf, cb) in enumerate(CHUNKS):
                S_st = S_ctx if s < CTX_CH else S_lat

                def cols(p):
                    ch = cf if p < 4 else cb
                    return slice(ch * C, (ch + 1) * C)

                def product(step, bank, lhs, rhs):
                    for p in range(PAIRS):
                        last = mm(bank8(bank)[:, p, :], lhs(p), rhs(p), start=True, stop=True)
                    last.then_inc(S["dn_pe"], 1)

                pe.wait_ge(S["dn_dve"], value("dn_dve", "gm1", s))
                mm(ps[:, 5, :], same_head, flat(gM), start=True, stop=True)
                for d, ch in ((0, cf), (1, cb)):
                    g = bg_st[:, 1, ch % 2, ch // 2, 4 * d:4 * d + 4]
                    mm(ps[:, 6, 4 * d:4 * d + 4], upto_bd[:, d, :], g, start=True, stop=True)
                    last = mm(ps[:, 6, 8 + 4 * d:12 + 4 * d], same_head, g, start=True, stop=True)
                last.then_inc(S["dn_pe"], 1)
                if s == CTX_CH:
                    pe.wait_ge(S["state_in"], 64)
                pe.wait_ge(S["dn_stage"], value("dn_stage", "vb1", s))
                if s - 1 >= 0:
                    pe.wait_ge(S["dn_dve"], value("dn_dve", "s1", s - 1))
                product("kk", 0, lambda p: k_bd[:, p, :], lambda p: dT[:, 4 + p % 4, cols(p)])
                product("kq", 1, lambda p: k_bd[:, p, :], lambda p: dT[:, p % 4, cols(p)])
                for b in range(2):
                    for p in range(4):
                        last = turn128(ps[:, 2 + b, p * P:(p + 1) * P], k_bd[:, 4 * b + p, :], ident)
                    last.then_inc(S["dn_pe"], 1)
                product("v", 4, lambda p: v_bd[:, p, :], lambda p: eye_st)
                pe.wait_ge(S["dn_act"], value("dn_act", "kt1", s))
                product("ks", 7, lambda p: k_bd[:, p, :], lambda p: S_st[:, p, :])
                product("qs", 2, lambda p: q_bd[:, p, :], lambda p: S_st[:, p, :])
                pe.wait_ge(S["dn_dve"], value("dn_dve", "l1", s))
                product("x0", 0, lambda p: L_bd[:, p, :], lambda p: eye_st)
                pe.wait_ge(S["dn_act"], value("dn_act", "xb01", s))
                product("t0", 4, lambda p: X_bd[:, p, :], lambda p: eye_st)
                for l in range(1, LEVELS):
                    pe.wait_ge(S["dn_dve"], value("dn_dve", f"u{l - 1}", s))
                    product(f"x{l}", 0, lambda p: L_bd[:, p, :], lambda p: U_st[:, p, :])
                    pe.wait_ge(S["dn_dve"], value("dn_dve", f"x{l}", s))
                    pe.wait_ge(S["dn_act"], value("dn_act", f"tb{l - 1}1", s))
                    product(f"u{l}", 3, lambda p: T_bd[:, p, :], lambda p: X_st[:, p, :])
                    if l < LEVELS - 1:
                        pe.wait_ge(S["dn_act"], value("dn_act", f"xb{l}1", s))
                        product(f"t{l}", 4, lambda p: X_bd[:, p, :], lambda p: T_st[:, p, :])
                pe.wait_ge(S["dn_dve"], value("dn_dve", "ub1", s))
                product("vn", 7, lambda p: U_bd[:, p, :], lambda p: R_st[:, p, :])
                pe.wait_ge(S["dn_act"], value("dn_act", "vn", s))
                product("av", 1, lambda p: A_bd[:, p, :], lambda p: vn[:, p, :])
                pe.wait_ge(S["dn_dve"], value("dn_dve", "vd", s))
                product("s", 0, lambda p: ktok_bd[:, p, :], lambda p: vd[:, p, :])
            pe.wait_ge(S["dn_pe"], len(CHUNKS) * len(PE_STEPS))
            pe.sem_inc(S["arrivals"], 1)
            pe.wait_ge(S["arrivals"], 5 * 4)

            for u in range(NCH // 2):
                if u - 1 > 0:
                    pe.wait_ge(S["od_ready"], u - 1)
                for cc in range(2):
                    pe.wait_ge(S["on_ready"], 2 * u + cc + 1)
                    for p in range(4):
                        last = mm(ps[:, u % 2, p * P + cc * C:p * P + (cc + 1) * C], on_bd[cc][:, p, :], eye_st, start=True, stop=True)
                last.then_inc(S["odT_mm"], 1)
            pe.wait_ge(S["dgw_in"], 16)
            for n in range(4):
                for g, (c0, w) in enumerate(GROUPS):
                    u = 3 * n + g
                    if u - 1 > 0:
                        pe.wait_ge(S["gate_used"], u - 1)
                    for k in range(KD):
                        last = mm(ps[:, 2 + u % 2, 0:w], dgw[:, k, n * P:(n + 1) * P], hT[:, k, c0:c0 + w], start=(k == 0), stop=(k == KD - 1))
                    last.then_inc(S["gate_mm"], 1)
            pe.wait_ge(S["gate_used"], 12)
            pe.sem_inc(S["arrivals"], 1)
            pe.wait_ge(S["arrivals"], 5 * 5)

            pe.wait_ge(S["attn_back"], 16)
            for u, (c, g) in enumerate(MU):
                c0, w = GROUPS[g]
                pe.wait_ge(S[f"mw_in{c % 2}"], landed(c, 2, 4))
                if u - 1 > 0:
                    pe.wait_ge(S["merged"], u - 1)
                b = mw[c % 2]
                o = 4 * (u % 2)
                wk = b[:, 0:2048].rearrange("p (x k n) -> p x k n", x=2, k=KD)
                wb = b[:, 2048:3072].rearrange("p (x k n) -> p x k n", x=2, k=4)
                for x in range(2):
                    for k in range(KD):
                        mm(ps[:, o + x, 0:w], wk[:, x, k, :], hT[:, k, c0:c0 + w], start=(k == 0), stop=(k == KD - 1))
                    for k in range(4):
                        last = mm(ps[:, o + 2 + x, 0:w], wb[:, x, k, :], (aoT, odT)[x][:, k, c0:c0 + w], start=(k == 0), stop=(k == 3))
                last.then_inc(S["merge_mm"], 1)
                if g == 2:
                    pe.wait_ge(S["merge_mm"], u + 1)
                    pe.sem_inc(S["mw_used"], 1)
            pe.wait_ge(S["merged"], len(MU))
            pe.sem_inc(S["arrivals"], 1)
            pe.wait_ge(S["arrivals"], 5 * 6)

            for u in range(16):
                pe.wait_ge(S["row_rhs"], u + 1)
                if u - 1 > 0:
                    pe.wait_ge(S["row_used"], u - 1)
                mm(ps[:, u % 2, :], ones, row_rhs[u % 2], start=True, stop=True).then_inc(S["row_mm"], 1)
            pe.wait_ge(S["ow_in"], 16)
            pe.wait_ge(S["row_used"], 16)
            for n in range(NT):
                if n - 1 > 0:
                    pe.wait_ge(S["out_used"], n - 1)
                for h in range(2):
                    for k in range(KD):
                        last = mm(ps[:, 2 * (n % 2) + h, :], mT[:, k, n * P:(n + 1) * P], ow[:, k, h * 512:(h + 1) * 512],
                                  start=(k == 0), stop=(k == KD - 1))
                last.then_inc(S["out_mm"], 1)
            pe.wait_ge(S["out_used"], NT)
            pe.sem_inc(S["arrivals"], 1)
            pe.wait_ge(S["arrivals"], 5 * 7)

            pe.wait_ge(S["rw_in"], 48)
            for n in range(NT):
                pe.wait_ge(S["h2_ready"], n + 1)
                for h in range(2):
                    u = 2 * n + h
                    if u - 1 > 0:
                        pe.wait_ge(S["h2t_used"], u - 1)
                    for k in range(4):
                        last = turn128(ps[:, u % 2, k * P:(k + 1) * P], h2[n % 2][:, (4 * h + k) * P:(4 * h + k + 1) * P], ident)
                    last.then_inc(S["h2t_mm"], 1)
                pe.wait_ge(S["h2t_used"], 2 * n + 2)
                if n - 1 > 0:
                    pe.wait_ge(S["rout_used"], n - 1)
                for k in range(KD):
                    last = mm(ps[:, 2 + n % 2, 0:20], h2T[n % 2][:, k, :], rw[:, k, :], start=(k == 0), stop=(k == KD - 1))
                last.then_inc(S["rout_mm"], 1)
            pe.wait_ge(S["masks_ready"], 1)
            mm(ps[:, 4, 0:NT * NE], before, flat(m_all), start=True, stop=True)
            mm(ps[:, 5, 0:NT * NE], ones, flat(m_all), start=True, stop=True).then_inc(S["rank_mm"], 1)
            pe.wait_ge(S["pos_ready"], 1)
            def turn_slots(t):
                pe.wait_ge(S[f"hs_in{t % 2}"], landed(t, 2))
                for h in range(2):
                    if 2 * t - 1 + h > 0:
                        pe.wait_ge(S["hst_used"], 2 * t - 1 + h)
                    for k in range(4):
                        last = turn128(ps[:, h, k * P:(k + 1) * P], hs[t % 2][:, (4 * h + k) * P:(4 * h + k + 1) * P], ident)
                    last.then_inc(S["hst_mm"], 1)

            turn_slots(0)
            for t in range(MT):
                b = ew[t % 2]
                pe.wait_ge(S["hst_used"], 2 * t + 2)
                pe.wait_ge(S[f"ew_in{t % 2}"], landed(t, 2, 3))
                if t > 0:
                    pe.wait_ge(S["hid_ready"], t)
                for k in range(KD):
                    last = mm(ps[:, 2, :], hsT[t % 2][:, k, :], b[:, k * 512:(k + 1) * 512], start=(k == 0), stop=(k == KD - 1))
                last.then_inc(S["gu_mm"], 1)
                if t + 1 < MT:
                    turn_slots(t + 1)
                pe.wait_ge(S["hid_ready"], t + 1)
                for k in range(2):
                    last = turn128(ps[:, 3, k * P:(k + 1) * P], hid[:, k * P:(k + 1) * P], ident)
                last.then_inc(S["hidt_mm"], 1)
                pe.wait_ge(S["hidt_used"], t + 1)
                if t - 1 > 0:
                    pe.wait_ge(S["ysb_ready"], t - 1)
                o = 4 + 2 * (t % 2)
                for h in range(2):
                    for k in range(2):
                        last = mm(ps[:, o + h, :], hidT[:, k, :], b[:, 4096 + k * D + h * 512:4096 + k * D + (h + 1) * 512],
                                  start=(k == 0), stop=(k == 1))
                last.then_inc(S["dn_mm"], 1)
                pe.wait_ge(S["dn_mm"], t + 1)
                pe.sem_inc(S["ew_used"], 1)
            pe.sem_inc(S["arrivals"], 1)
            pe.wait_ge(S["arrivals"], 5 * 8)

        @block.scalar
        def _(act):
            f = nc.scalar.activation
            act.wait_ge(S["params_in"], 16 * 18)
            f(cond_s[:], cond[:], ACT.Sigmoid).then_inc(S["cond_sig"], 1)
            act.wait_ge(S["cond_sig"], count("cond_sig"))
            act.wait_ge(S["eps_ready"], 1)
            for n in range(NT):
                act.wait_ge(S[f"x_in{n % 3}"], landed(n, 3))
                f(junk, xs[n % 3], ACT.Square, accum_out=stat[:, n:n + 1]).then_inc(S["act_chain"], 1)
                act.wait_ge(S["act_chain"], count("act_chain"))
                f(stat[:, 16 + n:17 + n], stat[:, n:n + 1], ACT.Sqrt, bias=eps_unit, scale=1.0 / D).then_inc(S["ssx_ready"], 1)
                act.wait_ge(S["ssx_ready"], count("ssx_ready"))
                act.wait_ge(S["rstdx_ready"], n + 1)
                if 2 * (n - 1) > 0:
                    act.wait_ge(S["xt_done"], 2 * (n - 1))
                f(xn[n % 2], xs[n % 3], ACT.Copy, scale=stat[:, 16 + n:17 + n]).then_inc(S["xn_ready"], 1)
                act.wait_ge(S["xn_ready"], count("xn_ready"))

            def roots(n):
                if stats(n):
                    if n > 0:
                        act.wait_ge(S["tile_done"], n)
                    for g, (c0, w) in enumerate(GROUPS):
                        act.wait_ge(S["ssq"], 3 * n + g + 1)
                        f(scratch(n)[3][:, c0:c0 + w], ps[:, 4 + g, 0:w], ACT.Sqrt, bias=eps_head if n < NA else eps_unit).then_inc(S["root_ready"], 1)
                        act.wait_ge(S["root_ready"], count("root_ready"))

            def tile(n, first):
                raw, sq, tmp, _ = scratch(n)
                if n - 1 > 0:
                    act.wait_ge(S["tile_done"], n - 1)
                for g, (c0, w) in enumerate(GROUPS):
                    u = 3 * n + g
                    act.wait_ge(S["gemm"], u + 1)
                    o = c0 + 1 if g == 0 else c0 + 3
                    f(raw[:, o:o + w], ps[:, u % 4, 0:w], ACT.Copy).then_inc(S["gemm_used"], 1)
                    act.wait_ge(S["gemm_used"], count("gemm_used"))
                if n > first:
                    roots(n - 1)
                if n < NA:
                    for g, (c0, w) in enumerate(GROUPS):
                        o = c0 + 1 if g == 0 else c0 + 3
                        signal = "sq_ready" if g == 2 else "act_chain"
                        f(sq[:, c0:c0 + w], raw[:, o:o + w], ACT.Square).then_inc(S[signal], 1)
                        act.wait_ge(S[signal], count(signal))
                else:
                    if n - NA + 1 > 0:
                        act.wait_ge(S["conv_ready"], n - NA + 1)
                    f(sq, tmp, ACT.Sigmoid).then_inc(S["sigm_ready"], 1)
                    act.wait_ge(S["sigm_ready"], count("sigm_ready"))
                    if n - NA + 1 > 0:
                        act.wait_ge(S["z_ready"], n - NA + 1)
                    if stats(n):
                        f(sq, out_of(n), ACT.Square).then_inc(S["sq_ready"], 1)
                        act.wait_ge(S["sq_ready"], count("sq_ready"))

            for n in range(NA):
                tile(n, 0)
            roots(NA - 1)
            act.wait_ge(S["dec_abs"], 1)
            f(bt, ba[:, :, 0:16], ACT.Sigmoid).then_inc(S["beta_ready"], 1)
            act.wait_ge(S["beta_ready"], count("beta_ready"))
            f(gt, gt, ACT.Exp, scale=-1.0).then_inc(S["act_chain"], 1)
            act.wait_ge(S["act_chain"], count("act_chain"))
            f(gt, gt, ACT.Ln, bias=one_c).then_inc(S["act_chain"], 1)
            act.wait_ge(S["act_chain"], count("act_chain"))
            f(a_log[:], a_log[:], ACT.Exp).then_inc(S["dec_ln"], 1)
            act.wait_ge(S["dec_ln"], count("dec_ln"))
            act.sem_inc(S["arrivals"], 1)
            act.wait_ge(S["arrivals"], 5 * 1)

            NI = len(ITEMS)

            def probs(i):
                nk = keys(ITEMS[i][0])[1]
                act.wait_ge(S["mx_ready"], i + 1)
                if i - 1 > 0:
                    act.wait_ge(S["pt_mm"], i - 1)
                w = nk * P
                src = ps[:, 3 * (i % 2):3 * (i % 2) + 3, :].rearrange("p b c -> p (b c)")[:, 0:w]
                col = 8 * ((i // 8) % 2) + ITEMS[i][2] + 4 * ITEMS[i][1]
                f(p_sb[i % 2][:, 0:w], src, ACT.Exp, bias=ast[:, 32 + i % 2:33 + i % 2], scale=HD ** -0.5,
                  accum_out=ast[:, col:col + 1]).then_inc(S["p_ready"], 1)
                act.wait_ge(S["p_ready"], count("p_ready"))

            def probs_turned(i):
                if i < CTX_ITEMS:
                    return
                act.wait_ge(S["pt_mm"], i + 1)
                if i - 1 > 0:
                    act.wait_ge(S["pv_done"], i - 1)
                b = 3 * (i % 2)
                f(flat(pT[i % 2])[:, 512:1536], ps[:, b + 1:b + 3, :].rearrange("p b c -> p (b c)"), ACT.Copy).then_inc(S["pt_act"], 1)
                act.wait_ge(S["pt_act"], count("pt_act"))

            def out_turned(qt):
                act.wait_ge(S["ot_mm"], qt + 1)
                f(oT[:, :, qt * P:(qt + 1) * P], ps[:, 6 + qt % 2, :].rearrange("p (a c) -> p a c", a=4), ACT.Copy).then_inc(S["ot_used"], 1)
                act.wait_ge(S["ot_used"], count("ot_used"))

            for i in range(NI + 2):
                if i < NI:
                    probs(i)
                if 1 <= i <= NI:
                    probs_turned(i - 1)
                if i >= 2 and (i - 2) % 8 == 3 and i > 8:
                    out_turned((i - 2) // 8 - 1)
            out_turned(NT - 1)
            act.sem_inc(S["arrivals"], 1)
            act.wait_ge(S["arrivals"], 5 * 2)
            act.wait_ge(S["bd_zeroed"], 1)
            for n in range(NA, len(TILES)):
                tile(n, NA)
            act.sem_inc(S["arrivals"], 1)
            act.wait_ge(S["arrivals"], 5 * 3)

            act.wait_ge(S["bd_zeroed"], 2)
            for s in range(len(CHUNKS)):

                act.wait_ge(S["dn_dve"], value("dn_dve", "glg", s))
                f(gs[:, 24:48], gs[:, 0:24], ACT.Exp).then_inc(S["dn_act"], 1)
                act.wait_ge(S["dn_act"], count("dn_act"))
                act.wait_ge(S["dn_dve"], value("dn_dve", "abs", s))
                f(flat(E), flat(Dm), ACT.Exp, scale=-1.0).then_inc(S["dn_act"], 1)
                act.wait_ge(S["dn_act"], count("dn_act"))
                for b in range(2):
                    act.wait_ge(S["dn_pe"], value("dn_pe", f"kt{b}", s))
                    f(flat(ktok_bd)[:, b * 512:(b + 1) * 512], ps[:, 2 + b, :], ACT.Copy).then_inc(S["dn_act"], 1)
                    act.wait_ge(S["dn_act"], count("dn_act"))
                act.wait_ge(S["dn_pe"], value("dn_pe", "v", s))
                f(flat(V_st), ps[:, 4, :], ACT.Copy).then_inc(S["dn_act"], 1)
                act.wait_ge(S["dn_act"], count("dn_act"))
                for l in range(LEVELS - 1):
                    for nm, st, bd in (("x", X_st, X_bd), ("t", T_st, T_bd)):
                        act.wait_ge(S["dn_dve"], value("dn_dve", f"{nm}{l}", s))
                        for h in range(2):
                            lo = slice(h * C, (h + 1) * C)
                            f(bd[lo, :, lo], st[lo, :, :], ACT.Copy).then_inc(S["dn_act"], 1)
                            act.wait_ge(S["dn_act"], count("dn_act"))
                act.wait_ge(S["dn_pe"], value("dn_pe", "vn", s))
                f(flat(vn), ps[:, 7, :], ACT.Copy).then_inc(S["dn_act"], 1)
                act.wait_ge(S["dn_act"], count("dn_act"))
            act.sem_inc(S["arrivals"], 1)
            act.wait_ge(S["arrivals"], 5 * 4)
            f(onsq, R1[:, 0:5120], ACT.Square).then_inc(S["osq_ready"], 1)
            act.wait_ge(S["osq_ready"], count("osq_ready"))
            act.wait_ge(S["onr_sum"], 1)
            f(onr, onr, ACT.Sqrt, bias=eps_head).then_inc(S["onr_root"], 1)
            act.wait_ge(S["onr_root"], count("onr_root"))
            for n in range(4):
                for g, (c0, w) in enumerate(GROUPS):
                    u = 3 * n + g
                    act.wait_ge(S["gate_mm"], u + 1)
                    if u > 0:
                        act.wait_ge(S["gate_used"], u)
                    f(sgd[:, 0:w], ps[:, 2 + u % 2, 0:w], ACT.Sigmoid).then_inc(S["gsig_ready"], 1)
                    act.wait_ge(S["gsig_ready"], count("gsig_ready"))
            act.sem_inc(S["arrivals"], 1)
            act.wait_ge(S["arrivals"], 5 * 5)
            for u, (c, g) in enumerate(MU):
                w = GROUPS[g][1]
                act.wait_ge(S["merge_mm"], u + 1)
                if u - 1 > 0:
                    act.wait_ge(S["merged"], u - 1)
                for x in range(2):
                    f(sg[2 * (u % 2) + x][:, 0:w], ps[:, 4 * (u % 2) + x, 0:w], ACT.Sigmoid).then_inc(S["msig_ready"], 1)
                    act.wait_ge(S["msig_ready"], count("msig_ready"))
            act.sem_inc(S["arrivals"], 1)
            act.wait_ge(S["arrivals"], 5 * 6)
            for u in range(16):
                act.wait_ge(S["row_mm"], u + 1)
                r, c, h = u // 4, (u // 2) % 2, u % 2
                f(rows[:, r, c, h * 512:(h + 1) * 512], ps[:, u % 2, :], ACT.Copy).then_inc(S["row_used"], 1)
                act.wait_ge(S["row_used"], count("row_used"))
            act.sem_inc(S["arrivals"], 1)
            act.wait_ge(S["arrivals"], 5 * 7)
            for n in range(NT):
                f(y_sb[0], x2[:, n, :], ACT.Square, accum_out=stat[:, 32 + n:33 + n]).then_inc(S["act_chain"], 1)
                act.wait_ge(S["act_chain"], count("act_chain"))
            f(stat[:, 32:42], stat[:, 32:42], ACT.Sqrt, bias=eps_unit, scale=1.0 / D).then_inc(S["ss2_ready"], 1)
            act.wait_ge(S["ss2_ready"], count("ss2_ready"))
            for n in range(NT):
                for h in range(2):
                    u = 2 * n + h
                    act.wait_ge(S["h2t_mm"], u + 1)
                    if n - 1 > 0:
                        act.wait_ge(S["rout_mm"], n - 1)
                    f(h2T[n % 2][:, 4 * h:4 * h + 4, :], ps[:, u % 2, :].rearrange("p (k t) -> p k t", k=4), ACT.Copy).then_inc(S["h2t_used"], 1)
                    act.wait_ge(S["h2t_used"], count("h2t_used"))
            act.wait_ge(S["lg_shift"], 1)
            f(flat(r_e5), flat(r_e5), ACT.Exp).then_inc(S["lg_exp"], 1)
            act.wait_ge(S["lg_exp"], count("lg_exp"))
            def slots_turned(t):
                for h in range(2):
                    act.wait_ge(S["hst_mm"], 2 * t + h + 1)
                    if t - 1 > 0:
                        act.wait_ge(S["gu_mm"], t - 1)
                    f(hsT[t % 2][:, 4 * h:4 * h + 4, :], ps[:, h, :].rearrange("p (k t) -> p k t", k=4), ACT.Copy).then_inc(S["hst_used"], 1)
                    act.wait_ge(S["hst_used"], count("hst_used"))

            slots_turned(0)
            for t in range(MT):
                act.wait_ge(S["gu_mm"], t + 1)
                f(sgh, ps[:, 2, 0:FF], ACT.Sigmoid).then_inc(S["gu_sig"], 1)
                act.wait_ge(S["gu_sig"], count("gu_sig"))
                if t + 1 < MT:
                    slots_turned(t + 1)
                act.wait_ge(S["dn_mm"], t + 1)
                if t - 2 >= 0:
                    act.wait_ge(S[f"y_out{(t - 2) % 2}"], landed(t - 2, 2))
                o = 4 + 2 * (t % 2)
                f(y_sb[t % 2], ps[:, o:o + 2, :].rearrange("p b c -> p (b c)"), ACT.Copy).then_inc(S["ysb_ready"], 1)
                act.wait_ge(S["ysb_ready"], count("ysb_ready"))
                act.dma_start(y_d[t * P:(t + 1) * P, :], y_sb[t % 2]).then_inc(S[f"y_out{t % 2}"], 16)
            for t in (MT - 2, MT - 1):
                act.wait_ge(S[f"y_out{t % 2}"], landed(t, 2))
            act.sem_inc(S["arrivals"], 1)
            act.wait_ge(S["arrivals"], 5 * 8)
            for n in range(NT):
                act.wait_ge(S["x3_ready"], n + 1)
                f(y_sb[0], x2[:, n, :], ACT.Square, accum_out=stat[:, 48 + n:49 + n]).then_inc(S["act_chain"], 1)
                act.wait_ge(S["act_chain"], count("act_chain"))
                f(stat[:, 48 + n:49 + n], stat[:, 48 + n:49 + n], ACT.Sqrt, bias=eps_unit, scale=1.0 / D).then_inc(S["ss3_ready"], 1)
                act.wait_ge(S["ss3_ready"], count("ss3_ready"))

        @block.vector
        def _(dve):
            v = nc.vector

            def bc(x, shape):
                return x.to_broadcast([P] + shape)

            for col, x in ((0, 1.0), (2, HD * EPS), (3, EPS)):
                signal = "eps_ready" if col == 3 else "dve_chain"
                v.memset(epsc[:, col:col + 1], x).then_inc(S[signal], 1)
                dve.wait_ge(S[signal], count(signal))
            dve.wait_ge(S["params_in"], 16 * 18)
            dve.wait_ge(S["cond_sig"], 1)
            v.tensor_tensor(cond_s[:], cond_s[:], cond[:], ALU.mult).then_inc(S["cond_ready"], 1)
            dve.wait_ge(S["cond_ready"], count("cond_ready"))
            for n in range(NT):
                dve.wait_ge(S["ssx_ready"], n + 1)
                v.reciprocal(stat[:, 16 + n:17 + n], stat[:, 16 + n:17 + n]).then_inc(S["rstdx_ready"], 1)
                dve.wait_ge(S["rstdx_ready"], count("rstdx_ready"))
                if n == 1:
                    dve.wait_ge(S["wmod_used"], 12)
                    v.tensor_tensor(mod[:], ps[:, 0, 0:96].rearrange("p (f c) -> p f c", c=2), bc(b_mod[:].unsqueeze(2), [48, 2]), ALU.add).then_inc(S["dve_chain"], 1)
                    dve.wait_ge(S["dve_chain"], count("dve_chain"))
                    for A_, f0, nw in ((A1, 8, norm_mix), (A2, 32, norm_ffn)):
                        v.scalar_tensor_tensor(A_[:], mod[:, f0:f0 + KD, :], 1.0, bc(nw[:].unsqueeze(2), [KD, 2]), ALU.add, ALU.mult).then_inc(S["dve_chain"], 1)
                        dve.wait_ge(S["dve_chain"], count("dve_chain"))
                if n >= 1:
                    for m in ([n - 1] if n < NT - 1 else [n - 1, n]):
                        ci = 0 if m < 2 else 1
                        for h in range(2):
                            u = 2 * m + h
                            dve.wait_ge(S["xt_done"], u + 1)
                            for k in range(4):
                                kk = 4 * h + k
                                signal = "xt_used" if k == 3 else "dve_chain"
                                v.tensor_scalar(hT[:, kk, m * P:(m + 1) * P], ps[:, 1 + u % 4, k * P:(k + 1) * P],
                                                A1[:, kk, ci:ci + 1], mod[:, kk, ci:ci + 1], ALU.mult, ALU.add).then_inc(S[signal], 1)
                                dve.wait_ge(S[signal], count(signal))
            v.tensor_scalar(qk_w[:], qk_w[:], 8.0, None, ALU.mult).then_inc(S["dve_chain"], 1)
            dve.wait_ge(S["dve_chain"], count("dve_chain"))
            v.tensor_scalar(dnn_w[:], dnn_w[:], 8.0, None, ALU.mult).then_inc(S["dve_chain"], 1)
            dve.wait_ge(S["dve_chain"], count("dve_chain"))

            SEG = [(0, 256, 1), (256, 1024, 259)]

            def norm_tile(n):
                raw, _, tmp, rstd = scratch(n)
                y = out_of(n)
                dve.wait_ge(S["root_ready"], 3 * n + 3)
                v.reciprocal(rstd, rstd).then_inc(S["dve_chain"], 1)
                dve.wait_ge(S["dve_chain"], count("dve_chain"))
                wcol = qk_w[:, 0:1] if TILES[n][0] == "aq" else qk_w[:, 1:2]
                for x, (c0, w, o) in enumerate(SEG):
                    signal = "y_ready" if x else "dve_chain"
                    v.scalar_tensor_tensor(y[:, c0:c0 + w], raw[:, o:o + w], wcol, rstd[:, c0:c0 + w], ALU.mult, ALU.mult).then_inc(S[signal], 1)
                    dve.wait_ge(S[signal], count(signal))
                dve.wait_ge(S["past_in"], 96)
                for g in (1, 2):
                    dve.wait_ge(S["rot_mm"], 2 * n + g)
                    c0, w = GROUPS[g]
                    v.tensor_tensor(tmp[:, c0:c0 + w], ps[:, 4 + g, 0:w], sin_t[:, c0 - CTX:c0 - CTX + w], ALU.mult).then_inc(S["rot_used"], 1)
                    dve.wait_ge(S["rot_used"], count("rot_used"))
                v.tensor_tensor(y[:, CTX:T], y[:, CTX:T], cos_t, ALU.mult).then_inc(S["dve_chain"], 1)
                dve.wait_ge(S["dve_chain"], count("dve_chain"))
                v.tensor_tensor(y[:, CTX:T], y[:, CTX:T], tmp[:, CTX:T], ALU.add).then_inc(S["tile_done"], 1)
                dve.wait_ge(S["tile_done"], count("tile_done"))

            for n in range(NA):
                norm_tile(n)
            for n in range(NT):
                dve.wait_ge(S["vba_mm"], n + 1)
                v.tensor_copy(v_sb[:, n, :], ps[:, n % 2, 0:P]).then_inc(S["dve_chain"], 1)
                dve.wait_ge(S["dve_chain"], count("dve_chain"))
                v.tensor_copy(ba[:, n, :], ps[:, n % 2, P:160]).then_inc(S["vba_used"], 1)
                dve.wait_ge(S["vba_used"], count("vba_used"))
            dve.wait_ge(S["pastT"], 1)
            v.tensor_copy(kT[:, T:T + PAST], ps[:, 2, :]).then_inc(S["pastT_used"], 1)
            dve.wait_ge(S["pastT_used"], count("pastT_used"))
            dve.wait_ge(S["kout_mm"], 1)
            v.tensor_copy(flat(ktok), ps[:, 3, 0:2 * P]).then_inc(S["kout_used"], 1)
            dve.wait_ge(S["kout_used"], count("kout_used"))
            v.tensor_tensor(zt, ba[:, :, 16:32], bc(dt_b[:].unsqueeze(1), [NT, 16]), ALU.add).then_inc(S["dve_chain"], 1)
            dve.wait_ge(S["dve_chain"], count("dve_chain"))
            v.scalar_tensor_tensor(gt, zt, -1.0, zt, ALU.mult, ALU.max).then_inc(S["dec_abs"], 1)
            dve.wait_ge(S["dec_abs"], count("dec_abs"))
            v.tensor_scalar(zt, zt, 0.0, None, ALU.max).then_inc(S["dve_chain"], 1)
            dve.wait_ge(S["dve_chain"], count("dve_chain"))
            dve.wait_ge(S["beta_ready"], 1)
            dve.wait_ge(S["dec_ln"], 1)
            v.tensor_tensor(gt, gt, zt, ALU.add).then_inc(S["dve_chain"], 1)
            dve.wait_ge(S["dve_chain"], count("dve_chain"))
            v.scalar_tensor_tensor(gt, gt, -1.0, bc(a_log[:].unsqueeze(1), [NT, 16]), ALU.mult, ALU.mult).then_inc(S["dve_chain"], 1)
            dve.wait_ge(S["dve_chain"], count("dve_chain"))
            for h in range(2):
                v.tensor_copy(bg[:, 0, h], bt.rearrange("p n (e h) -> p h n e", h=2)[:, h]).then_inc(S["dve_chain"], 1)
                dve.wait_ge(S["dve_chain"], count("dve_chain"))
                signal = "bg_ready" if h else "dve_chain"
                v.tensor_copy(bg[:, 1, h], gt.rearrange("p n (e h) -> p h n e", h=2)[:, h]).then_inc(S[signal], 1)
                dve.wait_ge(S[signal], count(signal))
            dve.sem_inc(S["arrivals"], 1)
            dve.wait_ge(S["arrivals"], 5 * 1)

            NI = len(ITEMS)

            def largest(i):
                w = keys(ITEMS[i][0])[1] * P
                dve.wait_ge(S["sc_ready"], i + 1)
                if i - 1 > 0:
                    dve.wait_ge(S["p_ready"], i - 1)
                src = ps[:, 3 * (i % 2):3 * (i % 2) + 3, :].rearrange("p b c -> p (b c)")[:, 0:w]
                v.tensor_reduce(ast[:, 34:35], src, AX.X, ALU.max).then_inc(S["dve_chain"], 1)
                dve.wait_ge(S["dve_chain"], count("dve_chain"))
                v.tensor_scalar(ast[:, 32 + i % 2:33 + i % 2], ast[:, 34:35], -HD ** -0.5, None, ALU.mult).then_inc(S["mx_ready"], 1)
                dve.wait_ge(S["mx_ready"], count("mx_ready"))

            def probs_turned(i):
                dve.wait_ge(S["pt_mm"], i + 1)
                if i - 1 > 0:
                    dve.wait_ge(S["pv_done"], i - 1)
                w = 256 if i < CTX_ITEMS else 512
                v.tensor_copy(flat(pT[i % 2])[:, 0:w], ps[:, 3 * (i % 2), 0:w]).then_inc(S["pt_dve"], 1)
                dve.wait_ge(S["pt_dve"], count("pt_dve"))

            def heads_out(qt):
                dve.wait_ge(S["pv_done"], 8 * (qt + 1))
                if qt > 0:
                    dve.wait_ge(S["ot_mm"], qt)
                v.reciprocal(ast[:, 16:24], ast[:, 8 * (qt % 2):8 * (qt % 2) + 8]).then_inc(S["dve_chain"], 1)
                dve.wait_ge(S["dve_chain"], count("dve_chain"))
                v.tensor_tensor(o_tok.rearrange("p (h d) -> p h d", h=NH), bank8(6 + qt % 2), bc(ast[:, 16:24].unsqueeze(2), [NH, HD]), ALU.mult).then_inc(S["o_ready"], 1)
                dve.wait_ge(S["o_ready"], count("o_ready"))

            for i in range(NI + 2):
                if i < NI:
                    largest(i)
                if 1 <= i <= NI:
                    probs_turned(i - 1)
                if i >= 2 and (i - 2) % 8 == 7:
                    heads_out((i - 2) // 8)
            dve.sem_inc(S["arrivals"], 1)
            dve.wait_ge(S["arrivals"], 5 * 2)

            dve.wait_ge(S["bd_zeroed"], 1)

            def convolve(n):
                raw, _, tmp, _ = scratch(n)
                ct = TILES.index(("dq", 0))
                dve.wait_ge(S["gemm_used"], 3 * n + 3)
                for tap in (1, 0, 2):
                    wc = conv_w[:, n - ct, tap:tap + 1]
                    for x, (c0, w, o) in enumerate(SEG):
                        src = raw[:, o - 1 + tap:o - 1 + tap + w]
                        if tap == 1:
                            v.tensor_scalar(tmp[:, c0:c0 + w], src, wc, None, ALU.mult).then_inc(S["dve_chain"], 1)
                            dve.wait_ge(S["dve_chain"], count("dve_chain"))
                        else:
                            signal = "conv_ready" if tap == 2 and x else "dve_chain"
                            v.scalar_tensor_tensor(tmp[:, c0:c0 + w], src, wc, tmp[:, c0:c0 + w], ALU.mult, ALU.add).then_inc(S[signal], 1)
                            dve.wait_ge(S[signal], count(signal))

            def silu(n):
                _, sq, tmp, _ = scratch(n)
                if n - NA + 1 > 0:
                    dve.wait_ge(S["sigm_ready"], n - NA + 1)
                v.tensor_tensor(out_of(n), tmp, sq, ALU.mult).then_inc(S["z_ready"], 1)
                dve.wait_ge(S["z_ready"], count("z_ready"))
                if not stats(n):
                    v.tensor_scalar(epsc[:, 1:2], epsc[:, 0:1], 1.0, None, ALU.mult).then_inc(S["tile_done"], 1)
                    dve.wait_ge(S["tile_done"], count("tile_done"))

            def unit(n):
                rstd = scratch(n)[3]
                dve.wait_ge(S["root_ready"], 3 * n + 3)
                v.reciprocal(rstd, rstd).then_inc(S["dve_chain"], 1)
                dve.wait_ge(S["dve_chain"], count("dve_chain"))
                sc = HD ** -0.5 if TILES[n][0] == "dq" else 1.0
                v.scalar_tensor_tensor(out_of(n), out_of(n), sc, rstd, ALU.mult, ALU.mult).then_inc(S["tile_done"], 1)
                dve.wait_ge(S["tile_done"], count("tile_done"))

            for n in range(NA, len(TILES) + 1):
                if n < len(TILES):
                    convolve(n)
                if n - 1 >= NA and stats(n - 1):
                    unit(n - 1)
                if n < len(TILES):
                    silu(n)
            dve.sem_inc(S["arrivals"], 1)
            dve.wait_ge(S["arrivals"], 5 * 3)

            dve.wait_ge(S["bd_zeroed"], 2)
            dve.wait_ge(S["state_in"], 64)
            for s, (cf, cb) in enumerate(CHUNKS):
                S_st = S_ctx if s < CTX_CH else S_lat


                def row(c0):
                    return bc(gs[:, c0:c0 + PAIRS].unsqueeze(2), [PAIRS, C])

                def dirs(x):
                    return x.rearrange("p (d a) c -> p d a c", d=2)

                both = [(0, cf), (1, cb)]
                for d, ch in both:
                    g = bg_st[:, 1, ch % 2, ch // 2, 4 * d:4 * d + 4]
                    v.tensor_tensor(gM[:, 4 * d:4 * d + 4, :], bc(upto[:, d, :].unsqueeze(1), [4, C]), bc(g.unsqueeze(2), [4, C]), ALU.mult).then_inc(S["dn_dve"], 1)
                    dve.wait_ge(S["dn_dve"], count("dn_dve"))
                for d, ch in both:
                    v.tensor_copy(gs[:, 48 + 4 * d:52 + 4 * d], bg_st[:, 0, ch % 2, ch // 2, 4 * d:4 * d + 4]).then_inc(S["dn_dve"], 1)
                    dve.wait_ge(S["dn_dve"], count("dn_dve"))
                dve.wait_ge(S["dn_pe"], value("dn_pe", "g", s))
                v.tensor_copy(gs[:, 0:16], ps[:, 6, 0:16]).then_inc(S["dn_dve"], 1)
                dve.wait_ge(S["dn_dve"], count("dn_dve"))
                v.tensor_tensor(gs[:, 16:24], gs[:, 8:16], gs[:, 0:8], ALU.subtract).then_inc(S["dn_dve"], 1)
                dve.wait_ge(S["dn_dve"], count("dn_dve"))
                v.tensor_tensor(Dm, row(0), bank8(5), ALU.subtract).then_inc(S["dn_dve"], 1)
                dve.wait_ge(S["dn_dve"], count("dn_dve"))
                v.scalar_tensor_tensor(flat(Dm), flat(Dm), -1.0, flat(Dm), ALU.mult, ALU.max).then_inc(S["dn_dve"], 1)
                dve.wait_ge(S["dn_dve"], count("dn_dve"))
                dve.wait_ge(S["dn_act"], value("dn_act", "e", s))
                v.tensor_tensor(Dm, E, row(48), ALU.mult).then_inc(S["dn_dve"], 1)
                dve.wait_ge(S["dn_dve"], count("dn_dve"))
                dve.wait_ge(S["dn_pe"], value("dn_pe", "kk", s))
                for h in range(2):
                    lo = slice(h * C, (h + 1) * C)
                    v.tensor_tensor(L_bd[lo, :, lo], bank8(0)[lo], Dm[lo], ALU.mult).then_inc(S["dn_dve"], 1)
                    dve.wait_ge(S["dn_dve"], count("dn_dve"))

                def x_level(l):
                    dve.wait_ge(S["dn_pe"], value("dn_pe", f"x{l}", s))
                    m = levels[:, :, l, :].unsqueeze(2).to_broadcast([P, 2, 4, C])
                    v.tensor_tensor(dirs(X_st), dirs(bank8(0)), m, ALU.mult).then_inc(S["dn_dve"], 1)
                    dve.wait_ge(S["dn_dve"], count("dn_dve"))

                eye8 = bc(eye_st.unsqueeze(1), [PAIRS, C])
                x_level(0)
                v.tensor_tensor(U_st, eye8, X_st, ALU.subtract).then_inc(S["dn_dve"], 1)
                dve.wait_ge(S["dn_dve"], count("dn_dve"))
                dve.wait_ge(S["dn_pe"], value("dn_pe", "t0", s))
                v.tensor_tensor(T_st, eye8, bank8(4), ALU.subtract).then_inc(S["dn_dve"], 1)
                dve.wait_ge(S["dn_dve"], count("dn_dve"))
                v.tensor_tensor(dirs(E), dirs(E), upto.unsqueeze(2).to_broadcast([P, 2, 4, C]), ALU.mult).then_inc(S["dn_dve"], 1)
                dve.wait_ge(S["dn_dve"], count("dn_dve"))
                dve.wait_ge(S["dn_pe"], value("dn_pe", "kq", s))
                for h in range(2):
                    lo = slice(h * C, (h + 1) * C)
                    v.tensor_tensor(A_bd[lo, :, lo], bank8(1)[lo], E[lo], ALU.mult).then_inc(S["dn_dve"], 1)
                    dve.wait_ge(S["dn_dve"], count("dn_dve"))
                dve.wait_ge(S["dn_act"], value("dn_act", "v", s))
                dve.wait_ge(S["dn_pe"], value("dn_pe", "ks", s))
                v.tensor_tensor(R_st, bank8(7), row(24), ALU.mult).then_inc(S["dn_dve"], 1)
                dve.wait_ge(S["dn_dve"], count("dn_dve"))
                v.tensor_tensor(R_st, V_st, R_st, ALU.subtract).then_inc(S["dn_dve"], 1)
                dve.wait_ge(S["dn_dve"], count("dn_dve"))
                v.tensor_tensor(R_st, R_st, row(48), ALU.mult).then_inc(S["dn_dve"], 1)
                dve.wait_ge(S["dn_dve"], count("dn_dve"))
                for l in range(1, LEVELS):
                    x_level(l)
                    dve.wait_ge(S["dn_pe"], value("dn_pe", f"u{l}", s))
                    if l < LEVELS - 1:
                        v.tensor_tensor(U_st, U_st, bank8(3), ALU.subtract).then_inc(S["dn_dve"], 1)
                        dve.wait_ge(S["dn_dve"], count("dn_dve"))
                        dve.wait_ge(S["dn_pe"], value("dn_pe", f"t{l}", s))
                        v.tensor_tensor(T_st, T_st, bank8(4), ALU.subtract).then_inc(S["dn_dve"], 1)
                        dve.wait_ge(S["dn_dve"], count("dn_dve"))
                    else:
                        for h in range(2):
                            lo = slice(h * C, (h + 1) * C)
                            v.tensor_tensor(U_bd[lo, :, lo], U_st[lo], bank8(3)[lo], ALU.subtract).then_inc(S["dn_dve"], 1)
                            dve.wait_ge(S["dn_dve"], count("dn_dve"))
                dve.wait_ge(S["dn_act"], value("dn_act", "vn", s))
                v.tensor_tensor(vd, vn, row(40), ALU.mult).then_inc(S["dn_dve"], 1)
                dve.wait_ge(S["dn_dve"], count("dn_dve"))
                v.tensor_tensor(o1, bank8(2), row(24), ALU.mult).then_inc(S["dn_dve"], 1)
                dve.wait_ge(S["dn_dve"], count("dn_dve"))
                dve.wait_ge(S["dn_pe"], value("dn_pe", "av", s))
                if s - 1 >= 0:
                    dve.wait_ge(S["dn_acc"], value("dn_acc", "b", s - 1))
                v.tensor_tensor(oo, o1, bank8(1), ALU.add).then_inc(S["dn_dve"], 1)
                dve.wait_ge(S["dn_dve"], count("dn_dve"))
                v.tensor_tensor(S_st[:], S_st[:], row(32), ALU.mult).then_inc(S["dn_dve"], 1)
                dve.wait_ge(S["dn_dve"], count("dn_dve"))
                dve.wait_ge(S["dn_pe"], value("dn_pe", "s", s))
                v.tensor_tensor(S_st[:], S_st[:], bank8(0), ALU.add).then_inc(S["dn_dve"], 1)
                dve.wait_ge(S["dn_dve"], count("dn_dve"))
            dve.sem_inc(S["arrivals"], 1)
            dve.wait_ge(S["arrivals"], 5 * 4)

            for cc in range(2):
                v.memset(flat(on_bd[cc]), 0.0).then_inc(S["dve_chain"], 1)
                dve.wait_ge(S["dve_chain"], count("dve_chain"))
            dve.wait_ge(S["osq_ready"], 1)
            v.tensor_reduce(onr, onsq.rearrange("p (n d) -> p n d", d=C), AX.X, ALU.add).then_inc(S["onr_sum"], 1)
            dve.wait_ge(S["onr_sum"], count("onr_sum"))
            dve.wait_ge(S["onr_root"], 1)
            v.reciprocal(onr, onr).then_inc(S["dve_chain"], 1)
            dve.wait_ge(S["dve_chain"], count("dve_chain"))
            for u in range(NCH // 2):
                for cc in range(2):
                    ch = 2 * u + cc
                    if u > 0:
                        dve.wait_ge(S["odT_mm"], u)
                    for h in range(2):
                        lo = slice(h * C, (h + 1) * C)
                        r = onr[lo, 4 * ch:4 * ch + 4].unsqueeze(2).to_broadcast([C, 4, C])
                        signal = "on_ready" if h else "dve_chain"
                        v.tensor_tensor(on_bd[cc][lo, :, lo], oacc[lo, ch], r, ALU.mult).then_inc(S[signal], 1)
                        dve.wait_ge(S[signal], count(signal))
                dve.wait_ge(S["odT_mm"], u + 1)
                v.tensor_scalar(odT[:, :, u * P:(u + 1) * P], ps[:, u % 2, :].rearrange("p (a c) -> p a c", a=4), dnn_w[:, 0:1], None, ALU.mult).then_inc(S["od_ready"], 1)
                dve.wait_ge(S["od_ready"], count("od_ready"))
            for n in range(4):
                for g, (c0, w) in enumerate(GROUPS):
                    u = 3 * n + g
                    dve.wait_ge(S["gsig_ready"], u + 1)
                    v.tensor_tensor(tdg[:, 0:w], ps[:, 2 + u % 2, 0:w], sgd[:, 0:w], ALU.mult).then_inc(S["gate_used"], 1)
                    dve.wait_ge(S["gate_used"], count("gate_used"))
                    v.tensor_tensor(odT[:, n, c0:c0 + w], odT[:, n, c0:c0 + w], tdg[:, 0:w], ALU.mult).then_inc(S["dve_chain"], 1)
                    dve.wait_ge(S["dve_chain"], count("dve_chain"))
            dve.sem_inc(S["arrivals"], 1)
            dve.wait_ge(S["arrivals"], 5 * 5)
            for u, (c, g) in enumerate(MU):
                c0, w = GROUPS[g]
                dve.wait_ge(S["msig_ready"], 2 * u + 2)
                for x in range(2):
                    v.tensor_tensor(m1[x][:, 0:w], ps[:, 4 * (u % 2) + 2 + x, 0:w], sg[2 * (u % 2) + x][:, 0:w], ALU.mult).then_inc(S["dve_chain"], 1)
                    dve.wait_ge(S["dve_chain"], count("dve_chain"))
                v.tensor_tensor(mT[:, c, c0:c0 + w], m1[0][:, 0:w], m1[1][:, 0:w], ALU.add).then_inc(S["merged"], 1)
                dve.wait_ge(S["merged"], count("merged"))
            dve.sem_inc(S["arrivals"], 1)
            dve.wait_ge(S["arrivals"], 5 * 6)
            sources = [mod[:, 16:24, :], A2[:], mod[:, 24:32, :], mod[:, 40:48, :]]
            for u in range(16):
                r, c, h = u // 4, (u // 2) % 2, u % 2
                if u - 1 > 0:
                    dve.wait_ge(S["row_mm"], u - 1)
                col = sources[r][:, 4 * h:4 * h + 4, c:c + 1]
                v.tensor_tensor(row_rhs[u % 2].rearrange("p (k n) -> p k n", k=4), bc(ident.unsqueeze(1), [4, P]), bc(col, [4, P]), ALU.mult).then_inc(S["row_rhs"], 1)
                dve.wait_ge(S["row_rhs"], count("row_rhs"))
            dve.wait_ge(S["row_used"], 16)
            for n in range(NT):
                ci = 0 if n < 2 else 1
                dve.wait_ge(S["out_mm"], n + 1)
                dve.wait_ge(S[f"xr_in{n % 2}"], landed(n, 2))
                b = 2 * (n % 2)
                v.tensor_tensor(x2[:, n, :], ps[:, b:b + 2, :].rearrange("p b c -> p (b c)"), rows[:, 0, ci, :], ALU.mult).then_inc(S["dve_chain"], 1)
                dve.wait_ge(S["dve_chain"], count("dve_chain"))
                v.tensor_tensor(x2[:, n, :], x2[:, n, :], xr[n % 2], ALU.add).then_inc(S["out_used"], 1)
                dve.wait_ge(S["out_used"], count("out_used"))
            dve.sem_inc(S["arrivals"], 1)
            dve.wait_ge(S["arrivals"], 5 * 7)
            dve.wait_ge(S["ss2_ready"], 1)
            v.reciprocal(stat[:, 32:42], stat[:, 32:42]).then_inc(S["dve_chain"], 1)
            dve.wait_ge(S["dve_chain"], count("dve_chain"))
            for n in range(NT + 1):
                if n < NT:
                    ci = 0 if n < 2 else 1
                    if 2 * (n - 1) > 0:
                        dve.wait_ge(S["h2t_mm"], 2 * (n - 1))
                    if n - 2 >= 0:
                        dve.wait_ge(S[f"h2_out{(n - 2) % 2}"], landed(n - 2, 2))
                    v.scalar_tensor_tensor(h2[n % 2], x2[:, n, :], stat[:, 32 + n:33 + n], rows[:, 1, ci, :], ALU.mult, ALU.mult).then_inc(S["dve_chain"], 1)
                    dve.wait_ge(S["dve_chain"], count("dve_chain"))
                    v.tensor_tensor(h2[n % 2], h2[n % 2], rows[:, 2, ci, :], ALU.add).then_inc(S["h2_ready"], 1)
                    dve.wait_ge(S["h2_ready"], count("h2_ready"))
                if n:
                    if n > 0:
                        dve.wait_ge(S["rout_mm"], n)
                    v.tensor_tensor(lg[:, n - 1, :], ps[:, 2 + (n - 1) % 2, 0:20], b_r[:], ALU.add).then_inc(S["rout_used"], 1)
                    dve.wait_ge(S["rout_used"], count("rout_used"))

            def first_only(oh):
                v.tensor_copy(r_seen, oh[:, :, 0:1]).then_inc(S["dve_chain"], 1)
                dve.wait_ge(S["dve_chain"], count("dve_chain"))
                for k in range(1, 4):
                    v.tensor_scalar(r_not, r_seen, -1.0, 1.0, ALU.mult, ALU.add).then_inc(S["dve_chain"], 1)
                    dve.wait_ge(S["dve_chain"], count("dve_chain"))
                    v.tensor_tensor(oh[:, :, k:k + 1], oh[:, :, k:k + 1], r_not, ALU.mult).then_inc(S["dve_chain"], 1)
                    dve.wait_ge(S["dve_chain"], count("dve_chain"))
                    v.tensor_tensor(r_seen, r_seen, oh[:, :, k:k + 1], ALU.add).then_inc(S["dve_chain"], 1)
                    dve.wait_ge(S["dve_chain"], count("dve_chain"))

            def top(x, mx, oh):
                v.tensor_reduce(mx, x, AX.X, ALU.max).then_inc(S["dve_chain"], 1)
                dve.wait_ge(S["dve_chain"], count("dve_chain"))
                v.tensor_tensor(oh, x, bc(mx, [NT, 4]), ALU.is_equal).then_inc(S["dve_chain"], 1)
                dve.wait_ge(S["dve_chain"], count("dve_chain"))
                first_only(oh)

            lgG = lg[:, :, 0:4]
            top(lgG, r_gm, r_ohg)
            v.tensor_tensor(r_e5[:, :, 0:4], lgG, bc(r_gm, [NT, 4]), ALU.subtract).then_inc(S["dve_chain"], 1)
            dve.wait_ge(S["dve_chain"], count("dve_chain"))
            for e in range(4):
                v.tensor_tensor(r_sel, lg[:, :, 4 + e:20:4], r_ohg, ALU.mult).then_inc(S["dve_chain"], 1)
                dve.wait_ge(S["dve_chain"], count("dve_chain"))
                v.tensor_reduce(r_el[:, :, e:e + 1], r_sel, AX.X, ALU.add).then_inc(S["dve_chain"], 1)
                dve.wait_ge(S["dve_chain"], count("dve_chain"))
            top(r_el, r_m1, r_oh1)
            v.scalar_tensor_tensor(r_el2, r_oh1, -3e38, r_el, ALU.mult, ALU.add).then_inc(S["dve_chain"], 1)
            dve.wait_ge(S["dve_chain"], count("dve_chain"))
            top(r_el2, r_m2, r_oh2)
            v.tensor_tensor(r_e5[:, :, 4:5], r_m2, r_m1, ALU.subtract).then_inc(S["lg_shift"], 1)
            dve.wait_ge(S["lg_shift"], count("lg_shift"))
            for oh, dst in ((r_oh1, m_one), (r_oh2, m_two)):
                for g in range(4):
                    v.tensor_tensor(dst[:, :, 4 * g:4 * g + 4], oh, bc(r_ohg[:, :, g:g + 1], [NT, 4]), ALU.mult).then_inc(S["dve_chain"], 1)
                    dve.wait_ge(S["dve_chain"], count("dve_chain"))
            v.tensor_tensor(m_all, m_one, m_two, ALU.add).then_inc(S["masks_ready"], 1)
            dve.wait_ge(S["masks_ready"], count("masks_ready"))
            dve.wait_ge(S["lg_exp"], 1)
            v.tensor_reduce(r_gm, r_e5[:, :, 0:4], AX.X, ALU.add).then_inc(S["dve_chain"], 1)
            dve.wait_ge(S["dve_chain"], count("dve_chain"))
            v.tensor_scalar(r_m1, r_e5[:, :, 4:5], 1.0, None, ALU.add).then_inc(S["dve_chain"], 1)
            dve.wait_ge(S["dve_chain"], count("dve_chain"))
            v.tensor_tensor(r_gm, r_gm, r_m1, ALU.mult).then_inc(S["dve_chain"], 1)
            dve.wait_ge(S["dve_chain"], count("dve_chain"))
            v.reciprocal(wts[:, 0].unsqueeze(2), r_gm).then_inc(S["dve_chain"], 1)
            dve.wait_ge(S["dve_chain"], count("dve_chain"))
            v.tensor_tensor(wts[:, 1].unsqueeze(2), wts[:, 0].unsqueeze(2), r_e5[:, :, 4:5], ALU.mult).then_inc(S["dve_chain"], 1)
            dve.wait_ge(S["dve_chain"], count("dve_chain"))
            dve.wait_ge(S["rank_mm"], 1)
            v.tensor_copy(flat(r_cnt), ps[:, 5, 0:NT * NE]).then_inc(S["dve_chain"], 1)
            dve.wait_ge(S["dve_chain"], count("dve_chain"))
            v.memset(r_pre[:, 0, :], 0.0).then_inc(S["dve_chain"], 1)
            dve.wait_ge(S["dve_chain"], count("dve_chain"))
            for n in range(NT):
                v.tensor_tensor(r_pre[:, n + 1, :], r_pre[:, n, :], r_cnt[:, n, :], ALU.add).then_inc(S["dve_chain"], 1)
                dve.wait_ge(S["dve_chain"], count("dve_chain"))
            total = r_pre[:, NT, :]
            v.tensor_tensor(r_cmp[:, 0:NE * NT].rearrange("p (e k) -> p e k", e=NE), bc(total.unsqueeze(2), [NE, NT]), bc(k128.unsqueeze(1), [NE, NT]), ALU.is_gt).then_inc(S["dve_chain"], 1)
            dve.wait_ge(S["dve_chain"], count("dve_chain"))
            v.tensor_reduce(r_nt, r_cmp[:, 0:NE * NT].rearrange("p (e k) -> p e k", e=NE), AX.X, ALU.add).then_inc(S["dve_chain"], 1)
            dve.wait_ge(S["dve_chain"], count("dve_chain"))
            v.tensor_tensor(r_cmp[:, 0:NE * NE].rearrange("p (e k) -> p e k", e=NE), precedes, bc(r_nt.unsqueeze(1), [NE, NE]), ALU.mult).then_inc(S["dve_chain"], 1)
            dve.wait_ge(S["dve_chain"], count("dve_chain"))
            v.tensor_reduce(r_base, r_cmp[:, 0:NE * NE].rearrange("p (e k) -> p e k", e=NE), AX.X, ALU.add).then_inc(S["dve_chain"], 1)
            dve.wait_ge(S["dve_chain"], count("dve_chain"))
            v.tensor_tensor(r_nt, r_nt, r_base, ALU.add).then_inc(S["dve_chain"], 1)
            dve.wait_ge(S["dve_chain"], count("dve_chain"))
            v.tensor_scalar(r_base, r_base, float(P), None, ALU.mult).then_inc(S["dve_chain"], 1)
            dve.wait_ge(S["dve_chain"], count("dve_chain"))
            v.tensor_tensor(r_cnt, r_pre[:, 0:NT, :], bc(r_base.unsqueeze(1), [NT, NE]), ALU.add).then_inc(S["dve_chain"], 1)
            dve.wait_ge(S["dve_chain"], count("dve_chain"))
            v.tensor_tensor(r_cnt, r_cnt, ps[:, 4, 0:NT * NE].rearrange("p (n e) -> p n e", n=NT), ALU.add).then_inc(S["dve_chain"], 1)
            dve.wait_ge(S["dve_chain"], count("dve_chain"))
            for k, m in enumerate((m_one, m_two)):
                v.tensor_tensor(m, m, r_cnt, ALU.mult).then_inc(S["dve_chain"], 1)
                dve.wait_ge(S["dve_chain"], count("dve_chain"))
                v.tensor_reduce(r_pos[:, k, :], m, AX.X, ALU.add).then_inc(S["dve_chain"], 1)
                dve.wait_ge(S["dve_chain"], count("dve_chain"))
            v.tensor_copy(pos_i[:], r_pos).then_inc(S["dve_chain"], 1)
            dve.wait_ge(S["dve_chain"], count("dve_chain"))
            ends = r_cmp[:, 0:MT * NE].rearrange("p (t e) -> p t e", t=MT)
            v.tensor_tensor(ends, bc(tile_no.unsqueeze(2), [MT, NE]), bc(r_nt.unsqueeze(1), [MT, NE]), ALU.is_ge).then_inc(S["dve_chain"], 1)
            dve.wait_ge(S["dve_chain"], count("dve_chain"))
            v.tensor_reduce(r_tex, ends, AX.X, ALU.add).then_inc(S["dve_chain"], 1)
            dve.wait_ge(S["dve_chain"], count("dve_chain"))
            v.tensor_scalar(r_tex, r_tex, float(NE - 1), None, ALU.min).then_inc(S["dve_chain"], 1)
            dve.wait_ge(S["dve_chain"], count("dve_chain"))
            v.tensor_copy(tex_i[:], r_tex).then_inc(S["pos_ready"], 1)
            dve.wait_ge(S["pos_ready"], count("pos_ready"))
            for t in range(MT):
                dve.wait_ge(S["gu_sig"], t + 1)
                v.tensor_tensor(hid, ps[:, 2, 0:FF], sgh, ALU.mult).then_inc(S["dve_chain"], 1)
                dve.wait_ge(S["dve_chain"], count("dve_chain"))
                v.tensor_tensor(hid, hid, ps[:, 2, FF:2 * FF], ALU.mult).then_inc(S["hid_ready"], 1)
                dve.wait_ge(S["hid_ready"], count("hid_ready"))
                dve.wait_ge(S["hidt_mm"], t + 1)
                v.tensor_copy(flat(hidT), ps[:, 3, 0:FF]).then_inc(S["hidt_used"], 1)
                dve.wait_ge(S["hidt_used"], count("hidt_used"))
            dve.sem_inc(S["arrivals"], 1)
            dve.wait_ge(S["arrivals"], 5 * 8)
            for n in range(NT):
                ci = 0 if n < 2 else 1
                y0, y1 = yg[2 * (n % 2)], yg[2 * (n % 2) + 1]
                dve.wait_ge(S[f"y_in{n % 2}"], landed(n, 2, 2))
                v.tensor_scalar(y0, y0, wts[:, 0, n:n + 1], None, ALU.mult).then_inc(S["dve_chain"], 1)
                dve.wait_ge(S["dve_chain"], count("dve_chain"))
                v.scalar_tensor_tensor(y0, y1, wts[:, 1, n:n + 1], y0, ALU.mult, ALU.add).then_inc(S["dve_chain"], 1)
                dve.wait_ge(S["dve_chain"], count("dve_chain"))
                v.tensor_tensor(y0, y0, rows[:, 3, ci, :], ALU.mult).then_inc(S["dve_chain"], 1)
                dve.wait_ge(S["dve_chain"], count("dve_chain"))
                v.tensor_tensor(x2[:, n, :], x2[:, n, :], y0, ALU.add).then_inc(S["x3_ready"], 1)
                dve.wait_ge(S["x3_ready"], count("x3_ready"))
                dve.wait_ge(S["ss3_ready"], n + 1)
                st = stat[:, 48 + n:49 + n]
                v.reciprocal(st, st).then_inc(S["dve_chain"], 1)
                dve.wait_ge(S["dve_chain"], count("dve_chain"))
                v.scalar_tensor_tensor(x2[:, n, :], x2[:, n, :], st, nf_row, ALU.mult, ALU.mult).then_inc(S["out_ready"], 1)
                dve.wait_ge(S["out_ready"], count("out_ready"))

        @block.gpsimd
        def _(pool):
            g = nc.gpsimd
            g.iota(tok_i[:], pattern=[[P, NT]], base=0, channel_multiplier=1).then_inc(S["pool_chain"], 1)
            pool.wait_ge(S["pool_chain"], count("pool_chain"))
            g.memset(slot_i[:], 0).then_inc(S["pool_chain"], 1)
            pool.wait_ge(S["pool_chain"], count("pool_chain"))
            pool.dma_start(slot_d.rearrange("(t p) x -> p (t x)", p=P), slot_i[:]).then_inc(S["slot_zero"], 16)
            pool.wait_ge(S["slot_zero"], 16)
            pool.sem_inc(S["arrivals"], 1)
            pool.wait_ge(S["arrivals"], 5 * 1)
            pool.sem_inc(S["arrivals"], 1)
            pool.wait_ge(S["arrivals"], 5 * 2)
            for n in range(NA, NA + 2):
                raw = scratch(n)[0]
                for c0, w in ((0, 1), (257, 2), (1283, 1)):
                    signal = "bd_zeroed" if (n, c0) == (NA + 1, 1283) else "pool_chain"
                    g.memset(raw[:, c0:c0 + w], 0.0).then_inc(S[signal], 1)
                    pool.wait_ge(S[signal], count(signal))
            pool.sem_inc(S["arrivals"], 1)
            pool.wait_ge(S["arrivals"], 5 * 3)
            for b in (k_bd, q_bd, v_bd, L_bd, A_bd, X_bd, U_bd, T_bd):
                g.memset(flat(b), 0.0).then_inc(S["pool_chain"], 1)
                pool.wait_ge(S["pool_chain"], count("pool_chain"))
            g.memset(S_ctx[:], 0.0).then_inc(S["pool_chain"], 1)
            pool.wait_ge(S["pool_chain"], count("pool_chain"))
            g.memset(R1[:, 0:5120], 0.0).then_inc(S["bd_zeroed"], 1)
            pool.wait_ge(S["bd_zeroed"], count("bd_zeroed"))

            def stage(s):
                if s >= 1:
                    if value("dn_pe", "qs", s - 1) > 0:
                        pool.wait_ge(S["dn_pe"], value("dn_pe", "qs", s - 1))
                for bd, a0 in ((k_bd, 4), (q_bd, 0), (v_bd, 8)):
                    for d, ch in enumerate(CHUNKS[s]):
                        for h in range(2):
                            lo = slice(h * C, (h + 1) * C)
                            g.tensor_copy(bd[lo, 4 * d:4 * d + 4, lo], dT[lo, a0:a0 + 4, ch * C:(ch + 1) * C]).then_inc(S["dn_stage"], 1)
                            pool.wait_ge(S["dn_stage"], count("dn_stage"))

            stage(0)
            for s, pair in enumerate(CHUNKS):
                if s + 1 < len(CHUNKS):
                    stage(s + 1)
                if value("dn_dve", "o1", s) > 0:
                    pool.wait_ge(S["dn_dve"], value("dn_dve", "o1", s))
                for d, ch in enumerate(pair):
                    g.tensor_tensor(oacc[:, ch], oacc[:, ch], oo[:, 4 * d:4 * d + 4, :], ALU.add).then_inc(S["dn_acc"], 1)
                    pool.wait_ge(S["dn_acc"], count("dn_acc"))
            pool.sem_inc(S["arrivals"], 1)
            pool.wait_ge(S["arrivals"], 5 * 4)
            pool.sem_inc(S["arrivals"], 1)
            pool.wait_ge(S["arrivals"], 5 * 5)
            pool.sem_inc(S["arrivals"], 1)
            pool.wait_ge(S["arrivals"], 5 * 6)
            pool.sem_inc(S["arrivals"], 1)
            pool.wait_ge(S["arrivals"], 5 * 7)
            pool.wait_ge(S["pos_ready"], 1)
            for n in range(NT):
                for k in range(2):
                    pool.indirect_dma_start(slot_d, bass.IndirectOffsetOnAxis(ap=pos_i[:, k, n:n + 1], axis=0),
                                            tok_i[:, n:n + 1].bitcast(U32), None).then_inc(S["slot_scat"], 16)
            pool.wait_ge(S["slot_scat"], 32 * NT * 8 // 8)
            pool.dma_start(slot_i[:], slot_d.rearrange("(t p) x -> p (t x)", p=P)).then_inc(S["idx_in"], 16)
            pool.wait_ge(S["idx_in"], 16)
            for n in (NT - 2, NT - 1):
                pool.wait_ge(S[f"h2_out{n % 2}"], landed(n, 2))
            for t in range(MT):
                if 2 * (t - 1) > 0:
                    pool.wait_ge(S["hst_mm"], 2 * (t - 1))
                pool.indirect_dma_start(hs[t % 2], None, h2_d, bass.IndirectOffsetOnAxis(ap=slot_i[:, t:t + 1], axis=0)
                                        ).then_inc(S[f"hs_in{t % 2}"], 16)
            pool.sem_inc(S["arrivals"], 1)
            pool.wait_ge(S["arrivals"], 5 * 8)
            for n in range(NT):
                if n - 1 > 0:
                    pool.wait_ge(S["x3_ready"], n - 1)
                for k in range(2):
                    pool.indirect_dma_start(yg[2 * (n % 2) + k], None, y_d, bass.IndirectOffsetOnAxis(ap=pos_i[:, k, n:n + 1], axis=0)
                                            ).then_inc(S[f"y_in{n % 2}"], 16)


_INS = ["x_prompt", "x_sample", "c", "cache_attn_k", "cache_attn_v", "state_delta", "c_ctx", "w_mod", "b_mod", "norm_mix",
        "norm_ffn", "norm_final", "w_in", "q_norm", "k_norm", "conv_w", "a_log", "dt_bias", "dn_norm", "w_attn_br", "w_dn_br",
        "w_out", "w_rg", "b_rg", "w_re", "b_re", "w_gate_e", "w_up_e", "w_down_e"]
_OUTS = [(1, CTX, D), (1, LAT, D), (1, 1, NKV, CTX, HD), (1, 1, NKV, CTX, HD), (1, 1, 2, 8, HD, HD)]


def kernel(**inputs):
    import concourse.bacc as _bacc
    from concourse.bass_utils import run_bass_kernel_spmd as _run

    nc = _bacc.Bacc("TRN2", target_bir_lowering=False, num_devices=1)
    arrays, aps = {}, {}
    for name in _INS:
        x = np.ascontiguousarray(inputs[name])
        arrays[f"in_{name}_dram"] = x
        aps[name] = nc.dram_tensor(f"in_{name}_dram", x.shape, mybir.dt.from_np(x.dtype), kind="ExternalInput").ap()
    outs = [nc.dram_tensor(f"out_{i}_dram", s, F32, kind="ExternalOutput").ap() for i, s in enumerate(_OUTS)]
    build(nc, aps, outs)
    r = _run(nc, [arrays], core_ids=[0])
    return tuple(r.results[0][f"out_{i}_dram"] for i in range(len(_OUTS)))
```

```python
from contextlib import ExitStack

import numpy as np

import concourse.bass as bass
from concourse import mybir

F32 = mybir.dt.float32
I32 = mybir.dt.int32
U32 = mybir.dt.uint32
ALU = mybir.AluOpType
ACT = mybir.ActivationFunctionType
AX = mybir.AxisListType

P = 128
D = 1024
KD = D // P
CTX, LAT, PAST = 256, 1024, 512
T = CTX + LAT
NT = T // P
GROUPS = [(0, 256), (256, 512), (768, 512)]
HD = 64
NH, NKV = 8, 2
C = 64
NCH = T // C
CTX_CH, LAT_CH = CTX // C, LAT // C
PAIRS = 8
EPS = 1e-6
NE, FF = 16, 256
MT = 2 * T // P + NE - 1
COL = dict(aq=0, ak=512, av=640, dq=768, dk=1280, dv=1792, ba=2304, dgate=2336, gattn=2848, gdn=3872)
NW = 6
LEVELS = 6


def shape_constants():
    part, free = np.arange(P), np.arange(P)
    half, t = part // C, part % C
    same = (half[:, None] == half[None, :]).astype(np.float32)
    j = np.arange(C)
    upto = [t[:, None] <= j[None, :], t[:, None] >= j[None, :]]
    upto_bd = [(t[:, None] <= t[None, :]) * same, (t[:, None] >= t[None, :]) * same]
    level = []
    for d in range(2):
        for l in range(LEVELS):
            b = 1 << l
            r, c = t[:, None] // b, j[None, :] // b
            lo, hi = (r, c) if d == 0 else (c, r)
            level.append((hi == lo + 1) & (lo % 2 == 0))
    rot = np.zeros((P, P), np.float32)
    for m in range(P):
        if m % 32 < 16:
            rot[m + 16, m] = -1.0
        else:
            rot[m - 16, m] = 1.0
    before = (part[:, None] < free[None, :]).astype(np.float32)
    parts = [np.eye(P), same, np.ones((P, P))] + upto + upto_bd + level + [t[:, None] == j[None, :], rot, before]
    return np.concatenate([np.asarray(a, np.float32) for a in parts], axis=1)


def small_constants():
    rows = [np.arange(T // P) * 128.0, np.arange(MT), (np.arange(NE)[None, :] < np.arange(NE)[:, None]).ravel()]
    row = np.concatenate([np.asarray(r, np.float32) for r in rows])
    return np.broadcast_to(row, (P, row.size)).copy()


def rotary_tables():
    half = HD // 2
    pos = np.arange(LAT)
    inv = np.power(np.float32(10000.0), -np.arange(0, half, 2, dtype=np.float32) / np.float32(half)).astype(np.float32)
    d = np.arange(P) % HD
    where = np.where((d < half)[:, None], (pos // 64)[None, :], (pos % 64)[None, :]).astype(np.float32)
    ang = (where * inv[d % 16][:, None]).astype(np.float32)
    return np.cos(ang).astype(np.float32), np.sin(ang).astype(np.float32)


def build(nc, a, outs):
    ctx = ExitStack()
    with ctx:
        def sb(name, shape, dt=F32):
            return ctx.enter_context(nc.sbuf_tensor(name, shape, dt))

        def sem(name):
            return ctx.enter_context(nc.semaphore(name))

        const_np, small_np = shape_constants(), small_constants()
        cos_np, sin_np = rotary_tables()
        const_d = nc.inline_tensor(const_np, name="shape_constants")
        small_d = nc.inline_tensor(small_np, name="small_constants")
        cos_d = nc.inline_tensor(cos_np, name="rotary_cos")
        sin_d = nc.inline_tensor(sin_np, name="rotary_sin")

        attn_d = nc.dram_tensor("attn_out_scratch", [P, 4, T], F32).ap()
        h2_d = nc.dram_tensor("h2_scratch", [T, D], F32).ap()
        slot_d = nc.dram_tensor("slot_token", [MT * P, 1], U32).ap()
        y_d = nc.dram_tensor("slot_output", [MT * P, D], F32).ap()

        cst = sb("cst", [P, const_np.shape[1]])
        at = [0]

        def take(n):
            at[0] += n
            return cst[:, at[0] - n:at[0]]

        ident, same_head, ones = take(P), take(P), take(P)
        upto = take(2 * C).rearrange("p (d c) -> p d c", d=2)
        upto_bd = take(2 * P).rearrange("p (d c) -> p d c", d=2)
        levels = take(2 * LEVELS * C).rearrange("p (d l c) -> p d l c", d=2, l=LEVELS)
        eye_st, rot, before = take(C), take(P), take(P)
        small = sb("small", [P, small_np.shape[1]])
        k128 = small[:, 0:10]
        tile_no = small[:, 10:10 + MT]
        precedes = small[:, 10 + MT:10 + MT + NE * NE].rearrange("p (e f) -> p e f", e=NE)

        cond = sb("cond", [P, KD, 2])
        cond_s = sb("cond_s", [P, KD, 2])
        mod_row_sb = sb("mod_row_sb", [2, 1024])
        mod_rows = [mod_row_sb[:, i * 512:(i + 1) * 512] for i in range(2)]
        b_mod = sb("b_mod", [P, 48])
        norm_mix = sb("norm_mix", [P, KD])
        norm_ffn = sb("norm_ffn", [P, KD])
        mod = sb("mod", [P, 48, 2])
        A1 = sb("A1", [P, KD, 2])
        A2 = sb("A2", [P, KD, 2])
        qk_w = sb("qk_w", [P, 2])
        conv_w = sb("conv_w", [P, 12, 3])
        dnn_w = sb("dnn_w", [P, 1])
        a_log = sb("a_log", [P, 16])
        dt_b = sb("dt_b", [P, 16])
        b_r = sb("b_r", [P, 20])
        stat = sb("stat", [P, 64])
        epsc = sb("epsc", [P, 5])
        ba = sb("ba", [P, NT, 32])
        bg = sb("bg", [P, 2, 2, NT, 8])
        bg_st = sb("bg_st", [P, 2, 2, NT, 8])
        S_ctx = sb("S_ctx", [P, PAIRS, C])
        S_lat = sb("S_lat", [P, PAIRS, C])

        R0 = sb("R0", [P, KD * T])
        R1 = sb("R1", [P, 8704])
        R3 = sb("R3", [P, 12 * T])
        R4 = sb("R4", [P, 12288])

        hT = R0[:, :].rearrange("p (k t) -> p k t", k=KD)
        x2 = R0[:, :].rearrange("p (n d) -> p n d", n=NT)
        qT = R1[:, 0:4 * T].rearrange("p (a t) -> p a t", a=4)
        kT = R1[:, 4 * T:4 * T + T + PAST]
        v_sb = R1[:, 6912:6912 + 14 * P].rearrange("p (n d) -> p n d", n=14)

        ps = ctx.enter_context(nc.psum_tensor("ps", [P, 8, 512], F32))

        block = ctx.enter_context(nc.Block())

        names = """params_in consts_in cond_sig cond_ready eps_ready onr_sum onr_root wmod_used mod_row mod_turned ssx_ready rstdx_ready
          xn_ready xt_done xt_used w_used vw_in vba_mm vba_used past_in pastT pastT_used gemm gemm_used conv_ready
          sigm_ready z_ready sq_ready ssq root_ready rot_mm rot_used y_ready tile_done kout_mm kout_used kv_out
          dec_abs beta_ready dec_ln bg_ready bg_moved sc_ready mx_ready p_ready pt_mm pt_dve pt_act pv_done o_ready
          ot_mm ot_used attn_out bd_zeroed dn_pe0 dn_pe1 dn_dve0 dn_dve1 dn_act0 dn_act1 dn_stage0 dn_stage1 dn_acc0 dn_acc1 state_in state_out osq_ready
          on_ready odT_mm od_ready dgw_in gate_mm gsig_ready gate_used attn_back mw_used merge_mm msig_ready merged
          row_rhs row_mm row_used ow_in out_mm out_used rw_in ss2_ready h2_ready h2t_mm h2t_used rout_mm rout_used
          lg_shift lg_exp masks_ready rank_mm pos_ready slot_zero slot_scat idx_in ew_used hst_mm hst_used gu_mm
          gu_sig hid_ready hidt_mm hidt_used dn_mm ysb_ready x3_ready ss3_ready out_ready fin_out dve_chain
          act_chain pool_chain arrivals""".split()
        rings = dict(wmod_in=3, x_in=3, w_in=NW, mw_in=2, xr_in=2, ew_in=2, hs_in=2, y_in=2, h2_out=2, y_out=2)
        names += [f"{n}{i}" for n, k in rings.items() for i in range(k)]
        S = {n: sem(n) for n in names}

        counts = {n: 0 for n in names}

        def count(name):
            counts[name] += 1
            return counts[name]

        def landed(n, buffers, dmas=1):
            return 16 * dmas * (n // buffers + 1)

        ctx.enter_context(nc.allow_non_contiguous_dma("parameters, once, and strips of weights"))

        w_in_v = a["w_in"][0].rearrange("(k p) n -> p k n", p=P)
        w_mod_v = a["w_mod"][0].rearrange("(k p) n -> p k n", p=P)

        wmod_sb = [R4[:, i * 4096:(i + 1) * 4096].rearrange("p (k n) -> p k n", k=KD) for i in range(3)]
        w_sb = [R4[:, i * 1024:(i + 1) * 1024].rearrange("p (k n) -> p k n", k=KD) for i in range(NW)]
        vw = R4[:, 6144:6144 + 1280].rearrange("p (k n) -> p k n", k=KD)

        TILES = [("aq", i) for i in range(4)] + [("ak", 0)] + [(n, i) for n in ("dq", "dk", "dv") for i in range(4)]
        NA = 5

        x_v = [a["x_prompt"][0].rearrange("(n p) d -> n p d", p=P), a["x_sample"][0].rearrange("(n p) d -> n p d", p=P)]

        def x_tile(n):
            return x_v[0][n] if n < 2 else x_v[1][n - 2]

        xs = [R3[:, i * D:(i + 1) * D] for i in range(3)]
        xn = [R3[:, (3 + i) * D:(4 + i) * D] for i in range(2)]
        junk = R3[:, 5 * D:6 * D]

        TP = T + 4
        def scratch(n):
            base, r = (6144, R3) if n < NA else (0, R1)
            o = base
            raw = [r[:, o + i * TP:o + (i + 1) * TP] for i in range(2)]
            sq = [r[:, o + (2 + i) * TP:o + (2 + i) * TP + T] for i in range(2)]
            tmp = r[:, o + 4 * TP:o + 4 * TP + T]
            rstd = r[:, o + 5 * TP:o + 5 * TP + T]
            return raw[n % 2], sq[n % 2], tmp, rstd

        cos_t, sin_t = R3[:, 1536:2560], R3[:, 2560:3584]
        dT = R3[:, :].rearrange("p (a t) -> p a t", a=12)

        def out_of(n):
            kind, i = TILES[n]
            if kind == "aq":
                return qT[:, i, :]
            if kind == "ak":
                return kT[:, 0:T]
            return dT[:, {"dq": 0, "dk": 4, "dv": 8}[kind] + i, :]

        def stats(n):
            return TILES[n][0] != "dv"

        past = R3[:, 0:2 * 4 * P].rearrange("p (n c) -> p n c", c=P)
        ktok = R3[:, 1024:1024 + 2 * P].rearrange("p (n c) -> p n c", c=P)

        p_sb = [R3[:, i * 1536:(i + 1) * 1536] for i in range(2)]
        pT = [R3[:, 3072 + i * 1536:3072 + (i + 1) * 1536].rearrange("p (n c) -> p n c", c=P) for i in range(2)]
        o_tok = R3[:, 6144:6144 + 512]
        oT = R3[:, 6656:6656 + 4 * T].rearrange("p (a t) -> p a t", a=4)
        ast = R3[:, 12000:12000 + 64]
        ITEMS = [(qt, g, h4) for qt in range(NT) for h4 in range(4) for g in range(2)]

        def keys(qt):
            return (0, 2, 0) if qt < 2 else (CTX, 12, 2)

        oacc = R1[:, 0:NCH * 256].rearrange("p (c a d) -> p c a d", c=NCH, a=4)
        spot = {"R4": 0, "R1": NCH * 256}

        def scr(n, region="R4"):
            o = spot[region]
            spot[region] += n
            r = {"R4": R4, "R1": R1}[region][:, o:o + n]
            return r.rearrange("p (a c) -> p a c", a=PAIRS)

        k_bd, q_bd, v_bd, ktok_bd, L_bd, A_bd, X_bd, U_bd, T_bd = [scr(1024) for _ in range(9)]
        X_st, U_st, T_st, gM, Dm, E = [scr(512) for _ in range(6)]
        V_st, R_st, vn, vd, o1, oo = [scr(512, "R1") for _ in range(6)]
        gs = sb("gs", [P, 2, 28])

        X_SLOTS = [x for l in range(1, LEVELS) for x in (f"x{l}", f"u{l}")]
        SLOTS = ["decay", "keys", "state", "t0"] + X_SLOTS + ["new", "out"]
        ORDER = {
            "pe": ["g", "kkq", "kt", "v", "ks", "qs", "x0", "t0"]
                  + [x for l in range(1, LEVELS) for x in ((f"x{l}", f"u{l}", f"t{l}") if l < LEVELS - 1 else (f"x{l}", f"u{l}"))]
                  + ["vn", "av", "s"],
            "dve": ["gm", "b", "gc", "glg", "diff", "abs", "eb", "l0", "l1", "x0", "u0", "r0", "o0", "t0", "ea", "a0", "a1", "r1", "r2"]
                   + [x for l in range(1, LEVELS) for x in ((f"x{l}", f"u{l}", f"t{l}") if l < LEVELS - 1 else (f"x{l}", "ub0", "ub1"))]
                   + ["vd", "o1", "s0", "s1"],
            "act": ["eg", "e", "kt", "v"] + [f"{x}b{l}{h}" for l in range(LEVELS - 1) for x in "xt" for h in range(2)] + ["vn"],
            "stage": [f"{x}{h}" for x in "kqv" for h in range(2)],
            "acc": ["o"],
        }
        CHUNKS = [(s, CTX_CH - 1 - s) for s in range(CTX_CH)] + \
                 [(CTX_CH + s, CTX_CH + LAT_CH - 1 - s) for s in range(LAT_CH)]
        NCK, HALF = len(CHUNKS), len(SLOTS) // 2

        def value(engine, step, s):
            return s * len(ORDER[engine]) + ORDER[engine].index(step) + 1

        SCHEDULE = []
        for j in range(NCK * len(SLOTS) + HALF):
            for d, at_ in ((0, j), (1, j - HALF)):
                if 0 <= at_ < NCK * len(SLOTS):
                    SCHEDULE.append((d, at_ // len(SLOTS), SLOTS[at_ % len(SLOTS)]))

        def part(x, d):
            return x[:, 4 * d:4 * d + 4, :]

        def half(d, i, h):
            return ps[:, 4 * d + i, 256 * h:256 * h + 256].rearrange("p (a c) -> p a c", a=4)

        def flat(x):
            return x.rearrange("p a c -> p (a c)")

        def bank8(i):
            return ps[:, i, :].rearrange("p (a c) -> p a c", a=PAIRS)

        odT = R3[:, 0:4 * T].rearrange("p (a t) -> p a t", a=4)
        mT = R3[:, 4 * T:12 * T].rearrange("p (k t) -> p k t", k=KD)
        onsq = R4[:, 0:5120]
        onr = R4[:, 5120:5120 + 80]
        on_bd = [R4[:, 5248 + i * 512:5248 + (i + 1) * 512].rearrange("p (a c) -> p a c", a=4) for i in range(2)]
        dgw = R4[:, 6400:6400 + 4096].rearrange("p (k n) -> p k n", k=KD)
        sgd = R4[:, 10496:10496 + 512]
        tdg = R4[:, 11008:11008 + 512]

        MWB = 3072
        mw = [R4[:, i * MWB:(i + 1) * MWB] for i in range(2)]
        aoT = R1[:, 0:4 * T].rearrange("p (a t) -> p a t", a=4)
        sg = [R4[:, 6144 + i * 512:6656 + i * 512] for i in range(4)]
        m1 = [R4[:, 8192 + i * 512:8704 + i * 512] for i in range(4)]
        MU = [(c, g) for c in range(KD) for g in range(3)]

        rows = R1[:, 0:8192].rearrange("p (r c d) -> p r c d", r=4, c=2)
        row_rhs = [R4[:, 10240 + i * 512:10752 + i * 512] for i in range(2)]
        ow = R4[:, 0:8192].rearrange("p (k n) -> p k n", k=KD)
        xr = [R4[:, 8192 + i * D:8192 + (i + 1) * D] for i in range(2)]

        CTX_ITEMS = 8 * CTX // P
        bt = R3[:, 13900:14060].rearrange("p (n c) -> p n c", n=NT)
        gt = R3[:, 14060:14220].rearrange("p (n c) -> p n c", n=NT)
        zt = R3[:, 14220:14380].rearrange("p (n c) -> p n c", n=NT)
        one_c, eps_head, eps_unit = epsc[:, 0:1], epsc[:, 2:3], epsc[:, 3:4]

        h2 = [R3[:, i * D:(i + 1) * D] for i in range(2)]
        h2T = [R3[:, (2 + i) * D:(3 + i) * D].rearrange("p (k t) -> p k t", k=KD) for i in range(2)]
        rw = R3[:, 4096:4096 + 160].rearrange("p (k n) -> p k n", k=KD)
        lg = R3[:, 4352:4352 + 200].rearrange("p (n c) -> p n c", n=NT)
        rs = R3[:, 4608:4608 + 3000]
        EW = 6144
        ew = [R4[:, i * EW:(i + 1) * EW] for i in range(2)]
        hs = [R3[:, 8192 + i * D:8192 + (i + 1) * D] for i in range(2)]
        hsT = [h2T[i] for i in range(2)]
        hid = R3[:, 11264:11264 + 256]
        sgh = R3[:, 11520:11520 + 256]
        hidT = R3[:, 11776:11776 + 256].rearrange("p (k t) -> p k t", k=2)
        y_sb = [R3[:, 12032 + i * D:12032 + (i + 1) * D] for i in range(2)]
        rat = [4608]

        def rsc(*shape):
            n = int(np.prod(shape))
            rat[0] += n
            r = R3[:, rat[0] - n:rat[0]]
            if len(shape) == 2:
                r = r.rearrange("p (a b) -> p a b", a=shape[0])
            return r

        r_gm, r_m1, r_m2, r_seen, r_not = [rsc(NT, 1) for _ in range(5)]
        r_ohg, r_oh1, r_oh2, r_el, r_el2, r_sel = [rsc(NT, 4) for _ in range(6)]
        r_e5 = rsc(NT, 5)
        m_one, m_two, m_all, r_cnt = [rsc(NT, NE) for _ in range(4)]
        r_pre = rsc(NT + 1, NE)
        r_cmp = rsc(MT * NE)
        r_nt, r_base, r_tex = rsc(NE), rsc(NE), rsc(MT)
        r_pos = rsc(2, NT)
        assert rat[0] <= 8192
        slot_i = sb("slot_i", [P, MT], U32)
        pos_i = sb("pos_i", [P, 2, NT], U32)
        tok_i = sb("tok_i", [P, NT], I32)
        tex_i = sb("tex_i", [P, MT], I32)
        nf_row = R3[:, 14080:14080 + 1024]
        wts = sb("wts", [P, 2, NT])
        yg = [R3[:, i * D:(i + 1) * D] for i in range(4)]

        y_out_v = [outs[0][0].rearrange("(n p) d -> n p d", p=P), outs[1][0].rearrange("(n p) d -> n p d", p=P)]

        @block.sync
        def _(sp):
            for o, i in [(cst[:], const_d.ap()), (small[:], small_d.ap())]:
                sp.dma_start(o, i).then_inc(S["consts_in"], 16)
            small_loads = [
                (cond[:, :, 0], a["c_ctx"].rearrange("(k p) -> p k", p=P)),
                (cond[:, :, 1], a["c"][0].rearrange("(k p) -> p k", p=P)),
                (b_mod[:], a["b_mod"][0].rearrange("(k p) -> p k", p=P)),
                (norm_mix[:], a["norm_mix"][0].rearrange("(k p) -> p k", p=P)),
                (norm_ffn[:], a["norm_ffn"][0].rearrange("(k p) -> p k", p=P)),
                (a_log[:], a["a_log"].rearrange("x d h -> x (d h)").broadcast_to([P, 16])),
                (dt_b[:], a["dt_bias"].rearrange("x d h -> x (d h)").broadcast_to([P, 16])),
                (b_r[:, 0:4], a["b_rg"].broadcast_to([P, 4])),
                (b_r[:, 4:20], a["b_re"].broadcast_to([P, 16])),
            ]
            for h in range(2):
                small_loads += [(qk_w[h * HD:(h + 1) * HD, 0:1], a["q_norm"][0].unsqueeze(1)),
                                (qk_w[h * HD:(h + 1) * HD, 1:2], a["k_norm"][0].unsqueeze(1)),
                                (dnn_w[h * HD:(h + 1) * HD, 0:1], a["dn_norm"][0].unsqueeze(1))]
            for tap in range(3):
                small_loads.append((conv_w[:, :, tap], a["conv_w"][0, tap].rearrange("(k p) -> p k", p=P)))
            for o, i in small_loads:
                sp.dma_start(o, i).then_inc(S["params_in"], 16)
            for i in range(12):
                if i - 2 > 0:
                    sp.wait_ge(S["wmod_used"], i - 2)
                sp.dma_start(wmod_sb[i % 3], w_mod_v[:, :, i * 512:(i + 1) * 512]).then_inc(S[f"wmod_in{i % 3}"], 16)
                if i < 3:
                    sp.dma_start(xs[i], x_tile(i)).then_inc(S[f"x_in{i}"], 16)
            for n in range(3, NT):
                if n - 2 > 0:
                    sp.wait_ge(S["xn_ready"], n - 2)
                sp.dma_start(xs[n % 3], x_tile(n)).then_inc(S[f"x_in{n % 3}"], 16)
            sp.wait_ge(S["wmod_used"], 12)

            def strip(n):
                kind, i = TILES[n]
                if n - NW + 1 > 0:
                    sp.wait_ge(S["w_used"], n - NW + 1)
                if kind == "aq":
                    for g in range(2):
                        col = COL["aq"] + (i + 4 * g) * HD
                        sp.dma_start(w_sb[n % NW][:, :, g * HD:(g + 1) * HD], w_in_v[:, :, col:col + HD]).then_inc(S[f"w_in{n % NW}"], 16)
                else:
                    col = COL[kind] + i * P
                    sp.dma_start(w_sb[n % NW], w_in_v[:, :, col:col + P]).then_inc(S[f"w_in{n % NW}"], 16)

            for n in range(NA):
                strip(n)
            sp.dma_start(vw[:, :, 0:P], w_in_v[:, :, COL["av"]:COL["av"] + P]).then_inc(S["vw_in"], 16)
            sp.dma_start(vw[:, :, P:160], w_in_v[:, :, COL["ba"]:COL["ba"] + 32]).then_inc(S["vw_in"], 16)
            sp.wait_ge(S["xt_done"], 2 * NT)
            sp.dma_start(cos_t, cos_d.ap()).then_inc(S["past_in"], 16)
            sp.dma_start(sin_t, sin_d.ap()).then_inc(S["past_in"], 16)
            for g in range(2):
                sp.dma_start(past[:, 0:4, g * HD:(g + 1) * HD], a["cache_attn_k"][0, 0, g].rearrange("(n p) d -> p n d", p=P)).then_inc(S["past_in"], 16)
                sp.dma_start(v_sb[:, NT:14, g * HD:(g + 1) * HD], a["cache_attn_v"][0, 0, g].rearrange("(n p) d -> p n d", p=P)).then_inc(S["past_in"], 16)
            sp.wait_ge(S["vba_used"], NT)
            for g in range(2):
                sp.dma_start(outs[3][0, 0, g].rearrange("(n p) d -> p n d", p=P), v_sb[:, 0:2, g * HD:(g + 1) * HD]).then_inc(S["kv_out"], 16)
            sp.wait_ge(S["kout_used"], 1)
            for g in range(2):
                sp.dma_start(outs[2][0, 0, g].rearrange("(n p) d -> p n d", p=P), ktok[:, :, g * HD:(g + 1) * HD]).then_inc(S["kv_out"], 16)
            sp.wait_ge(S["kv_out"], 64)
            sp.wait_ge(S["bg_ready"], 1)
            for h in range(2):
                for cp in range(2):
                    for x in range(2):
                        sp.dma_start(bg_st[h * C:(h + 1) * C, x, cp], bg[cp * C:(cp + 1) * C, x, h]).then_inc(S["bg_moved"], 16)
            sp.wait_ge(S["bg_moved"], 128)
            sp.sem_inc(S["arrivals"], 1)
            sp.wait_ge(S["arrivals"], 5 * 1)
            for n in range(NA, NA + NW):
                strip(n)
            sp.wait_ge(S["ot_used"], NT)
            sp.dma_start(attn_d, oT).then_inc(S["attn_out"], 16)
            sp.wait_ge(S["attn_out"], 16)
            sp.sem_inc(S["arrivals"], 1)
            sp.wait_ge(S["arrivals"], 5 * 2)
            for n in range(NA + NW, len(TILES)):
                strip(n)
            for d in range(2):
                for h in range(2):
                    sp.dma_start(S_lat[h * HD:(h + 1) * HD, 4 * d:4 * d + 4, :], a["state_delta"][0, 0, d].rearrange("(a h) k v -> h k a v", h=2)[h]).then_inc(S["state_in"], 16)
            sp.sem_inc(S["arrivals"], 1)
            sp.wait_ge(S["arrivals"], 5 * 3)
            for d in range(2):
                if value("dve", "s1", CTX_CH - 1) > 0:
                    sp.wait_ge(S[f"dn_dve{d}"], value("dve", "s1", CTX_CH - 1))
                for h in range(2):
                    sp.dma_start(outs[4][0, 0, d].rearrange("(a h) k v -> h k a v", h=2)[h], S_ctx[h * HD:(h + 1) * HD, 4 * d:4 * d + 4, :]).then_inc(S["state_out"], 16)
            sp.wait_ge(S["state_out"], 64)
            sp.sem_inc(S["arrivals"], 1)
            sp.wait_ge(S["arrivals"], 5 * 4)
            sp.dma_start(dgw, w_in_v[:, :, COL["dgate"]:COL["dgate"] + 512]).then_inc(S["dgw_in"], 16)
            sp.sem_inc(S["arrivals"], 1)
            sp.wait_ge(S["arrivals"], 5 * 5)
            sp.dma_start(aoT, attn_d).then_inc(S["attn_back"], 16)
            wa = a["w_attn_br"][0].rearrange("(k p) n -> p k n", p=P)
            wd = a["w_dn_br"][0].rearrange("(k p) n -> p k n", p=P)
            for c in range(KD):
                if c - 1 > 0:
                    sp.wait_ge(S["mw_used"], c - 1)
                b = mw[c % 2]
                cs = slice(c * P, (c + 1) * P)
                sp.dma_start(b[:, 0:1024].rearrange("p (k n) -> p k n", k=KD), w_in_v[:, :, COL["gattn"] + c * P:COL["gattn"] + (c + 1) * P]).then_inc(S[f"mw_in{c % 2}"], 16)
                sp.dma_start(b[:, 1024:2048].rearrange("p (k n) -> p k n", k=KD), w_in_v[:, :, COL["gdn"] + c * P:COL["gdn"] + (c + 1) * P]).then_inc(S[f"mw_in{c % 2}"], 16)
                sp.dma_start(b[:, 2048:2560].rearrange("p (k n) -> p k n", k=4), wa[:, :, cs]).then_inc(S[f"mw_in{c % 2}"], 16)
                sp.dma_start(b[:, 2560:3072].rearrange("p (k n) -> p k n", k=4), wd[:, :, cs]).then_inc(S[f"mw_in{c % 2}"], 16)
            sp.sem_inc(S["arrivals"], 1)
            sp.wait_ge(S["arrivals"], 5 * 6)
            sp.dma_start(ow, a["w_out"][0].rearrange("(k p) n -> p k n", p=P)).then_inc(S["ow_in"], 16)
            for n in range(NT):
                if n - 1 > 0:
                    sp.wait_ge(S["out_used"], n - 1)
                sp.dma_start(xr[n % 2], x_tile(n)).then_inc(S[f"xr_in{n % 2}"], 16)
            sp.sem_inc(S["arrivals"], 1)
            sp.wait_ge(S["arrivals"], 5 * 7)
            sp.dma_start(rw[:, :, 0:4], a["w_rg"][0].rearrange("(k p) n -> p k n", p=P)).then_inc(S["rw_in"], 16)
            sp.dma_start(rw[:, :, 4:20], a["w_re"][0].rearrange("(k p) n -> p k n", p=P)).then_inc(S["rw_in"], 16)
            sp.dma_start(nf_row, a["norm_final"].unsqueeze(0).broadcast_to([P, D])).then_inc(S["rw_in"], 16)
            for n in range(NT):
                sp.wait_ge(S["h2_ready"], n + 1)
                sp.dma_start(h2_d[n * P:(n + 1) * P, :], h2[n % 2]).then_inc(S[f"h2_out{n % 2}"], 16)
            sp.wait_ge(S["pos_ready"], 1)
            for t in range(MT):
                e = sp.value_load(tex_i[0:1, t:t + 1], min_val=0, max_val=NE - 1)
                if t - 1 > 0:
                    sp.wait_ge(S["ew_used"], t - 1)
                b = ew[t % 2]
                for half, name in enumerate(("w_gate_e", "w_up_e")):
                    src = a[name][0][bass.ds(e, 1)].rearrange("e (k p) f -> p (e k) f", p=P)
                    sp.dma_start(b[:, 0:4096].rearrange("p (k n) -> p k n", k=KD)[:, :, half * FF:(half + 1) * FF], src).then_inc(S[f"ew_in{t % 2}"], 16)
                src = a["w_down_e"][0][bass.ds(e, 1)].rearrange("e (k p) n -> p (e k) n", p=P)
                sp.dma_start(b[:, 4096:6144].rearrange("p (k n) -> p k n", k=2), src).then_inc(S[f"ew_in{t % 2}"], 16)
            sp.sem_inc(S["arrivals"], 1)
            sp.wait_ge(S["arrivals"], 5 * 8)
            for n in range(NT):
                sp.wait_ge(S["out_ready"], n + 1)
                sp.dma_start(y_out_v[0][n] if n < 2 else y_out_v[1][n - 2], x2[:, n, :]).then_inc(S["fin_out"], 16)
            sp.wait_ge(S["fin_out"], 16 * NT)

        @block.tensor
        def _(pe):
            mm = nc.tensor.matmul
            turn128 = nc.tensor.transpose


            pe.wait_ge(S["consts_in"], 32)
            pe.wait_ge(S["cond_ready"], 1)
            for i in range(13):
                if i < 12:
                    pe.wait_ge(S[f"wmod_in{i % 3}"], landed(i, 3))
                    if i > 1:
                        pe.wait_ge(S["mod_row"], i - 1)
                    for k in range(KD):
                        last = mm(ps[0:2, 5 + i % 2, :], cond_s[:, k, :], wmod_sb[i % 3][:, k, :],
                                  start=(k == 0), stop=(k == KD - 1))
                    last.then_inc(S["wmod_used"], 1)
                if i > 0:
                    pe.wait_ge(S["mod_row"], i)
                    for f in range(4):
                        o = 2 * (4 * (i - 1) + f)
                        last = mm(ps[:, 0, o:o + 2], mod_rows[(i - 1) % 2][:, f * P:(f + 1) * P], ident[0:2, 0:2],
                                  start=True, stop=True)
                    last.then_inc(S["mod_turned"], 1)
            for n in range(NT):
                pe.wait_ge(S["xn_ready"], n + 1)
                for h in range(2):
                    u = 2 * n + h
                    if u - 3 > 0:
                        pe.wait_ge(S["xt_used"], u - 3)
                    for k in range(4):
                        last = turn128(ps[:, 1 + u % 4, k * P:(k + 1) * P], xn[n % 2][:, (4 * h + k) * P:(4 * h + k + 1) * P], ident)
                    last.then_inc(S["xt_done"], 1)
            pe.wait_ge(S["xt_used"], 2 * NT)

            def gemm(n):
                pe.wait_ge(S[f"w_in{n % NW}"], 16 * (n // NW + 1 + (n % NW < 4)))
                for g, (c0, w) in enumerate(GROUPS):
                    u = 3 * n + g
                    if u - 3 > 0:
                        pe.wait_ge(S["gemm_used"], u - 3)
                    for k in range(KD):
                        last = mm(ps[:, u % 4, 0:w], w_sb[n % NW][:, k, :], hT[:, k, c0:c0 + w],
                                  start=(k == 0), stop=(k == KD - 1))
                    last.then_inc(S["gemm"], 1)
                pe.wait_ge(S["gemm"], 3 * n + 3)
                pe.sem_inc(S["w_used"], 1)

            def ssq(n):
                if not stats(n):
                    return
                pe.wait_ge(S["sq_ready"], n + 1)
                if 3 * n > 0:
                    pe.wait_ge(S["root_ready"], 3 * n)
                if 2 * min(n, NA) > 0:
                    pe.wait_ge(S["rot_used"], 2 * min(n, NA))
                for g, (c0, w) in enumerate(GROUPS):
                    mm(ps[:, 4 + g, 0:w], same_head, scratch(n)[1][:, c0:c0 + w], start=True, stop=True).then_inc(S["ssq"], 1)

            def rotate(n):
                pe.wait_ge(S["y_ready"], n + 1)
                for g in (1, 2):
                    c0, w = GROUPS[g]
                    mm(ps[:, 4 + g, 0:w], rot, out_of(n)[:, c0:c0 + w], start=True, stop=True).then_inc(S["rot_mm"], 1)

            def tiles(first, end):
                for n in range(first, end + 2):
                    if n < end:
                        gemm(n)
                    if first <= n - 2 < NA:
                        rotate(n - 2)
                    if first <= n - 1 < end:
                        ssq(n - 1)

            pe.wait_ge(S["past_in"], 96)
            tiles(0, NA)
            pe.wait_ge(S["vw_in"], 32)
            pe.wait_ge(S["gemm_used"], 3 * NA)
            for n in range(NT):
                if n - 1 > 0:
                    pe.wait_ge(S["vba_used"], n - 1)
                for k in range(KD):
                    last = mm(ps[:, n % 2, 0:160], hT[:, k, n * P:(n + 1) * P], vw[:, k, :], start=(k == 0), stop=(k == KD - 1))
                last.then_inc(S["vba_mm"], 1)
            for n in range(4):
                last = turn128(ps[:, 2, n * P:(n + 1) * P], past[:, n, :], ident)
            last.then_inc(S["pastT"], 1)
            pe.wait_ge(S["tile_done"], NA)
            for n in range(2):
                last = turn128(ps[:, 3, n * P:(n + 1) * P], kT[:, n * P:(n + 1) * P], ident)
            last.then_inc(S["kout_mm"], 1)
            pe.wait_ge(S["kout_mm"], 1)
            pe.sem_inc(S["arrivals"], 1)
            pe.wait_ge(S["arrivals"], 5 * 1)

            def scores(i):
                qt, g, h4 = ITEMS[i]
                c0, nk, _ = keys(qt)
                if i - 1 > 0:
                    pe.wait_ge(S["pt_dve"], i - 1)
                if i - 1 - CTX_ITEMS > 0:
                    pe.wait_ge(S["pt_act"], i - 1 - CTX_ITEMS)
                lo = slice(g * HD, (g + 1) * HD)
                for j in range((nk + 3) // 4):
                    w = min(512, nk * P - j * 512)
                    last = mm(ps[:, 3 * (i % 2) + j, 0:w], qT[lo, h4, qt * P:(qt + 1) * P], kT[lo, c0 + j * 512:c0 + j * 512 + w],
                              start=True, stop=True)
                last.then_inc(S["sc_ready"], 1)

            def turn(i):
                nk = keys(ITEMS[i][0])[1]
                pe.wait_ge(S["p_ready"], i + 1)
                for j in range(nk):
                    last = turn128(ps[:, 3 * (i % 2) + j // 4, (j % 4) * P:(j % 4 + 1) * P], p_sb[i % 2][:, j * P:(j + 1) * P], ident)
                last.then_inc(S["pt_mm"], 1)

            def values(i):
                qt, g, h4 = ITEMS[i]
                _, nk, v0 = keys(qt)
                pe.wait_ge(S["pt_dve"], i + 1)
                if i + 1 - CTX_ITEMS > 0:
                    pe.wait_ge(S["pt_act"], i + 1 - CTX_ITEMS)
                if i % 8 == 0:
                    if qt - 1 > 0:
                        pe.wait_ge(S["ot_used"], qt - 1)
                h = h4 + 4 * g
                for j in range(nk):
                    last = mm(ps[:, 6 + qt % 2, h * HD:(h + 1) * HD], pT[i % 2][:, j, :], v_sb[:, v0 + j, g * HD:(g + 1) * HD],
                              start=(j == 0), stop=(j == nk - 1))
                last.then_inc(S["pv_done"], 1)

            def turn_out(qt):
                pe.wait_ge(S["o_ready"], qt + 1)
                for k in range(4):
                    last = turn128(ps[:, 6 + qt % 2, k * P:(k + 1) * P], o_tok[:, k * P:(k + 1) * P], ident)
                last.then_inc(S["ot_mm"], 1)

            NI = len(ITEMS)
            for i in range(NI + 2):
                if i < NI:
                    scores(i)
                if 1 <= i <= NI:
                    turn(i - 1)
                if i >= 2:
                    values(i - 2)
                    if (i - 2) % 8 == 2 and i > 8:
                        turn_out((i - 2) // 8 - 1)
            turn_out(NT - 1)
            pe.wait_ge(S["ot_used"], NT)
            pe.sem_inc(S["arrivals"], 1)
            pe.wait_ge(S["arrivals"], 5 * 2)
            tiles(NA, len(TILES))
            pe.wait_ge(S["tile_done"], len(TILES))
            pe.sem_inc(S["arrivals"], 1)
            pe.wait_ge(S["arrivals"], 5 * 3)

            pe.wait_ge(S["bd_zeroed"], 1)
            pe.wait_ge(S["state_in"], 64)

            def product(d, bank, lhs, rhs):
                for p in range(4):
                    last = mm(bank[:, p, :], lhs[:, 4 * d + p, :], rhs(p), start=True, stop=True)
                last.then_inc(S[f"dn_pe{d}"], 1)

            for d, s, slot in SCHEDULE:
                st = S_ctx if s < CTX_CH else S_lat
                ch = CHUNKS[s][d]
                cols = slice(ch * C, (ch + 1) * C)
                level = int(slot[1:]) if slot[0] in "xu" else 0
                if slot == "decay":
                    pe.wait_ge(S[f"dn_dve{d}"], value("dve", "gm", s))
                    if s - 1 >= 0:
                        pe.wait_ge(S[f"dn_dve{d}"], value("dve", "o0", s - 1))
                    if s - 1 >= 0:
                        pe.wait_ge(S[f"dn_dve{d}"], value("dve", "t4", s - 1))
                    g = bg_st[:, 1, ch % 2, ch // 2, 4 * d:4 * d + 4]
                    mm(ps[:, 4 * d, 0:256], same_head, flat(part(gM, d)), start=True, stop=True)
                    mm(ps[:, 4 * d, 256:260], upto_bd[:, d, :], g, start=True, stop=True)
                    mm(ps[:, 4 * d, 260:264], same_head, g, start=True, stop=True).then_inc(S[f"dn_pe{d}"], 1)
                elif slot == "keys":
                    pe.wait_ge(S[f"dn_stage{d}"], value("stage", "v1", s))
                    if s - 1 >= 0:
                        pe.wait_ge(S[f"dn_act{d}"], value("act", "vn", s - 1))
                    if s - 1 >= 0:
                        pe.wait_ge(S[f"dn_dve{d}"], value("dve", "s1", s - 1))
                    for p in range(4):
                        last = mm(ps[:, 4 * d + 1, p * P:(p + 1) * P].rearrange("p (x c) -> p x c", x=2), k_bd[:, 4 * d + p, :],
                                  dT[:, p:p + 5:4, cols], start=True, stop=True)
                    last.then_inc(S[f"dn_pe{d}"], 1)
                    for p in range(4):
                        last = turn128(ps[:, 4 * d + 2, p * P:(p + 1) * P], k_bd[:, 4 * d + p, :], ident)
                    last.then_inc(S[f"dn_pe{d}"], 1)
                    product(d, half(d, 3, 0), v_bd, lambda p: eye_st)
                elif slot == "state":
                    pe.wait_ge(S[f"dn_dve{d}"], value("dve", "diff", s))
                    product(d, half(d, 0, 0), k_bd, lambda p: st[:, 4 * d + p, :])
                    product(d, half(d, 0, 1), q_bd, lambda p: st[:, 4 * d + p, :])
                    pe.wait_ge(S[f"dn_dve{d}"], value("dve", "l1", s))
                    pe.wait_ge(S[f"dn_act{d}"], value("act", "kt", s))
                    product(d, half(d, 2, 0), L_bd, lambda p: eye_st)
                elif slot == "t0":
                    pe.wait_ge(S[f"dn_act{d}"], value("act", "xb01", s))
                    pe.wait_ge(S[f"dn_dve{d}"], value("dve", "o0", s))
                    product(d, half(d, 0, 0), X_bd, lambda p: eye_st)
                elif slot[0] == "x":
                    pe.wait_ge(S[f"dn_dve{d}"], value("dve", f"u{level - 1}", s))
                    product(d, half(d, 2, 0), L_bd, lambda p: U_st[:, 4 * d + p, :])
                elif slot[0] == "u":
                    pe.wait_ge(S[f"dn_dve{d}"], value("dve", f"x{level}", s))
                    pe.wait_ge(S[f"dn_act{d}"], value("act", f"tb{level - 1}1", s))
                    product(d, half(d, 3, 0), T_bd, lambda p: X_st[:, 4 * d + p, :])
                    if level < LEVELS - 1:
                        pe.wait_ge(S[f"dn_act{d}"], value("act", f"xb{level}1", s))
                        product(d, half(d, 0, 0), X_bd, lambda p: T_st[:, 4 * d + p, :])
                elif slot == "new":
                    pe.wait_ge(S[f"dn_dve{d}"], value("dve", "ub1", s))
                    product(d, half(d, 1, 0), U_bd, lambda p: R_st[:, 4 * d + p, :])
                else:
                    pe.wait_ge(S[f"dn_act{d}"], value("act", "vn", s))
                    product(d, half(d, 2, 0), A_bd, lambda p: vn[:, 4 * d + p, :])
                    pe.wait_ge(S[f"dn_dve{d}"], value("dve", "vd", s))
                    product(d, half(d, 3, 0), ktok_bd, lambda p: vd[:, 4 * d + p, :])
            for d in range(2):
                if value("pe", "s", NCK - 1) > 0:
                    pe.wait_ge(S[f"dn_pe{d}"], value("pe", "s", NCK - 1))
            pe.sem_inc(S["arrivals"], 1)
            pe.wait_ge(S["arrivals"], 5 * 4)

            for u in range(NCH // 2):
                if u - 1 > 0:
                    pe.wait_ge(S["od_ready"], u - 1)
                for cc in range(2):
                    pe.wait_ge(S["on_ready"], 2 * u + cc + 1)
                    for p in range(4):
                        last = mm(ps[:, u % 2, p * P + cc * C:p * P + (cc + 1) * C], on_bd[cc][:, p, :], eye_st, start=True, stop=True)
                last.then_inc(S["odT_mm"], 1)
            pe.wait_ge(S["dgw_in"], 16)
            for n in range(4):
                for g, (c0, w) in enumerate(GROUPS):
                    u = 3 * n + g
                    if u - 1 > 0:
                        pe.wait_ge(S["gate_used"], u - 1)
                    for k in range(KD):
                        last = mm(ps[:, 2 + u % 2, 0:w], dgw[:, k, n * P:(n + 1) * P], hT[:, k, c0:c0 + w], start=(k == 0), stop=(k == KD - 1))
                    last.then_inc(S["gate_mm"], 1)
            pe.wait_ge(S["gate_used"], 12)
            pe.sem_inc(S["arrivals"], 1)
            pe.wait_ge(S["arrivals"], 5 * 5)

            pe.wait_ge(S["attn_back"], 16)
            for u, (c, g) in enumerate(MU):
                c0, w = GROUPS[g]
                pe.wait_ge(S[f"mw_in{c % 2}"], landed(c, 2, 4))
                if u - 1 > 0:
                    pe.wait_ge(S["merged"], u - 1)
                b = mw[c % 2]
                o = 4 * (u % 2)
                wk = b[:, 0:2048].rearrange("p (x k n) -> p x k n", x=2, k=KD)
                wb = b[:, 2048:3072].rearrange("p (x k n) -> p x k n", x=2, k=4)
                for x in range(2):
                    for k in range(KD):
                        mm(ps[:, o + x, 0:w], wk[:, x, k, :], hT[:, k, c0:c0 + w], start=(k == 0), stop=(k == KD - 1))
                    for k in range(4):
                        last = mm(ps[:, o + 2 + x, 0:w], wb[:, x, k, :], (aoT, odT)[x][:, k, c0:c0 + w], start=(k == 0), stop=(k == 3))
                last.then_inc(S["merge_mm"], 1)
                if g == 2:
                    pe.wait_ge(S["merge_mm"], u + 1)
                    pe.sem_inc(S["mw_used"], 1)
            pe.wait_ge(S["merged"], len(MU))
            pe.sem_inc(S["arrivals"], 1)
            pe.wait_ge(S["arrivals"], 5 * 6)

            for u in range(16):
                pe.wait_ge(S["row_rhs"], u + 1)
                if u - 1 > 0:
                    pe.wait_ge(S["row_used"], u - 1)
                mm(ps[:, u % 2, :], ones, row_rhs[u % 2], start=True, stop=True).then_inc(S["row_mm"], 1)
            pe.wait_ge(S["ow_in"], 16)
            pe.wait_ge(S["row_used"], 16)
            for n in range(NT):
                if n - 1 > 0:
                    pe.wait_ge(S["out_used"], n - 1)
                for h in range(2):
                    for k in range(KD):
                        last = mm(ps[:, 2 * (n % 2) + h, :], mT[:, k, n * P:(n + 1) * P], ow[:, k, h * 512:(h + 1) * 512],
                                  start=(k == 0), stop=(k == KD - 1))
                last.then_inc(S["out_mm"], 1)
            pe.wait_ge(S["out_used"], NT)
            pe.sem_inc(S["arrivals"], 1)
            pe.wait_ge(S["arrivals"], 5 * 7)

            pe.wait_ge(S["rw_in"], 48)
            for n in range(NT):
                pe.wait_ge(S["h2_ready"], n + 1)
                for h in range(2):
                    u = 2 * n + h
                    if u - 1 > 0:
                        pe.wait_ge(S["h2t_used"], u - 1)
                    for k in range(4):
                        last = turn128(ps[:, u % 2, k * P:(k + 1) * P], h2[n % 2][:, (4 * h + k) * P:(4 * h + k + 1) * P], ident)
                    last.then_inc(S["h2t_mm"], 1)
                pe.wait_ge(S["h2t_used"], 2 * n + 2)
                if n - 1 > 0:
                    pe.wait_ge(S["rout_used"], n - 1)
                for k in range(KD):
                    last = mm(ps[:, 2 + n % 2, 0:20], h2T[n % 2][:, k, :], rw[:, k, :], start=(k == 0), stop=(k == KD - 1))
                last.then_inc(S["rout_mm"], 1)
            pe.wait_ge(S["masks_ready"], 1)
            mm(ps[:, 4, 0:NT * NE], before, flat(m_all), start=True, stop=True)
            mm(ps[:, 5, 0:NT * NE], ones, flat(m_all), start=True, stop=True).then_inc(S["rank_mm"], 1)
            pe.wait_ge(S["pos_ready"], 1)
            def turn_slots(t):
                pe.wait_ge(S[f"hs_in{t % 2}"], landed(t, 2))
                for h in range(2):
                    if 2 * t - 1 + h > 0:
                        pe.wait_ge(S["hst_used"], 2 * t - 1 + h)
                    for k in range(4):
                        last = turn128(ps[:, h, k * P:(k + 1) * P], hs[t % 2][:, (4 * h + k) * P:(4 * h + k + 1) * P], ident)
                    last.then_inc(S["hst_mm"], 1)

            turn_slots(0)
            for t in range(MT):
                b = ew[t % 2]
                pe.wait_ge(S["hst_used"], 2 * t + 2)
                pe.wait_ge(S[f"ew_in{t % 2}"], landed(t, 2, 3))
                if t > 0:
                    pe.wait_ge(S["hid_ready"], t)
                for k in range(KD):
                    last = mm(ps[:, 2, :], hsT[t % 2][:, k, :], b[:, k * 512:(k + 1) * 512], start=(k == 0), stop=(k == KD - 1))
                last.then_inc(S["gu_mm"], 1)
                if t + 1 < MT:
                    turn_slots(t + 1)
                pe.wait_ge(S["hid_ready"], t + 1)
                for k in range(2):
                    last = turn128(ps[:, 3, k * P:(k + 1) * P], hid[:, k * P:(k + 1) * P], ident)
                last.then_inc(S["hidt_mm"], 1)
                pe.wait_ge(S["hidt_used"], t + 1)
                if t - 1 > 0:
                    pe.wait_ge(S["ysb_ready"], t - 1)
                o = 4 + 2 * (t % 2)
                for h in range(2):
                    for k in range(2):
                        last = mm(ps[:, o + h, :], hidT[:, k, :], b[:, 4096 + k * D + h * 512:4096 + k * D + (h + 1) * 512],
                                  start=(k == 0), stop=(k == 1))
                last.then_inc(S["dn_mm"], 1)
                pe.wait_ge(S["dn_mm"], t + 1)
                pe.sem_inc(S["ew_used"], 1)
            pe.sem_inc(S["arrivals"], 1)
            pe.wait_ge(S["arrivals"], 5 * 8)

        @block.scalar
        def _(act):
            f = nc.scalar.activation
            act.wait_ge(S["params_in"], 16 * 18)
            f(cond_s[:], cond[:], ACT.Sigmoid).then_inc(S["cond_sig"], 1)
            act.wait_ge(S["cond_sig"], count("cond_sig"))
            act.wait_ge(S["eps_ready"], 1)
            for n in range(NT):
                act.wait_ge(S[f"x_in{n % 3}"], landed(n, 3))
                f(junk, xs[n % 3], ACT.Square, accum_out=stat[:, n:n + 1]).then_inc(S["act_chain"], 1)
                act.wait_ge(S["act_chain"], count("act_chain"))
                f(stat[:, 16 + n:17 + n], stat[:, n:n + 1], ACT.Sqrt, bias=eps_unit, scale=1.0 / D).then_inc(S["ssx_ready"], 1)
                act.wait_ge(S["ssx_ready"], count("ssx_ready"))
                act.wait_ge(S["rstdx_ready"], n + 1)
                if 2 * (n - 1) > 0:
                    act.wait_ge(S["xt_done"], 2 * (n - 1))
                f(xn[n % 2], xs[n % 3], ACT.Copy, scale=stat[:, 16 + n:17 + n]).then_inc(S["xn_ready"], 1)
                act.wait_ge(S["xn_ready"], count("xn_ready"))
                if n == 1:
                    for i in range(12):
                        act.wait_ge(S["wmod_used"], i + 1)
                        if i > 1:
                            act.wait_ge(S["mod_turned"], i - 1)
                        f(mod_rows[i % 2], ps[0:2, 5 + i % 2, :], ACT.Copy).then_inc(S["mod_row"], 1)

            def roots(n):
                if stats(n):
                    if n > 0:
                        act.wait_ge(S["tile_done"], n)
                    for g, (c0, w) in enumerate(GROUPS):
                        act.wait_ge(S["ssq"], 3 * n + g + 1)
                        f(scratch(n)[3][:, c0:c0 + w], ps[:, 4 + g, 0:w], ACT.Sqrt, bias=eps_head if n < NA else eps_unit).then_inc(S["root_ready"], 1)
                        act.wait_ge(S["root_ready"], count("root_ready"))

            def tile(n, first):
                raw, sq, tmp, _ = scratch(n)
                if n - 1 > 0:
                    act.wait_ge(S["tile_done"], n - 1)
                for g, (c0, w) in enumerate(GROUPS):
                    u = 3 * n + g
                    act.wait_ge(S["gemm"], u + 1)
                    o = c0 + 1 if g == 0 else c0 + 3
                    f(raw[:, o:o + w], ps[:, u % 4, 0:w], ACT.Copy).then_inc(S["gemm_used"], 1)
                    act.wait_ge(S["gemm_used"], count("gemm_used"))
                if n > first:
                    roots(n - 1)
                if n < NA:
                    for g, (c0, w) in enumerate(GROUPS):
                        o = c0 + 1 if g == 0 else c0 + 3
                        signal = "sq_ready" if g == 2 else "act_chain"
                        f(sq[:, c0:c0 + w], raw[:, o:o + w], ACT.Square).then_inc(S[signal], 1)
                        act.wait_ge(S[signal], count(signal))
                else:
                    if n - NA + 1 > 0:
                        act.wait_ge(S["conv_ready"], n - NA + 1)
                    f(sq, tmp, ACT.Sigmoid).then_inc(S["sigm_ready"], 1)
                    act.wait_ge(S["sigm_ready"], count("sigm_ready"))
                    if n - NA + 1 > 0:
                        act.wait_ge(S["z_ready"], n - NA + 1)
                    if stats(n):
                        f(sq, out_of(n), ACT.Square).then_inc(S["sq_ready"], 1)
                        act.wait_ge(S["sq_ready"], count("sq_ready"))

            for n in range(NA):
                tile(n, 0)
            roots(NA - 1)
            act.wait_ge(S["dec_abs"], 1)
            f(bt, ba[:, :, 0:16], ACT.Sigmoid).then_inc(S["beta_ready"], 1)
            act.wait_ge(S["beta_ready"], count("beta_ready"))
            f(gt, gt, ACT.Exp, scale=-1.0).then_inc(S["act_chain"], 1)
            act.wait_ge(S["act_chain"], count("act_chain"))
            f(gt, gt, ACT.Ln, bias=one_c).then_inc(S["act_chain"], 1)
            act.wait_ge(S["act_chain"], count("act_chain"))
            f(a_log[:], a_log[:], ACT.Exp).then_inc(S["dec_ln"], 1)
            act.wait_ge(S["dec_ln"], count("dec_ln"))
            act.sem_inc(S["arrivals"], 1)
            act.wait_ge(S["arrivals"], 5 * 1)

            NI = len(ITEMS)

            def probs(i):
                nk = keys(ITEMS[i][0])[1]
                act.wait_ge(S["mx_ready"], i + 1)
                if i - 1 > 0:
                    act.wait_ge(S["pt_mm"], i - 1)
                w = nk * P
                src = ps[:, 3 * (i % 2):3 * (i % 2) + 3, :].rearrange("p b c -> p (b c)")[:, 0:w]
                col = 8 * ((i // 8) % 2) + ITEMS[i][2] + 4 * ITEMS[i][1]
                f(p_sb[i % 2][:, 0:w], src, ACT.Exp, bias=ast[:, 32 + i % 2:33 + i % 2], scale=HD ** -0.5,
                  accum_out=ast[:, col:col + 1]).then_inc(S["p_ready"], 1)
                act.wait_ge(S["p_ready"], count("p_ready"))

            def probs_turned(i):
                if i < CTX_ITEMS:
                    return
                act.wait_ge(S["pt_mm"], i + 1)
                if i - 1 > 0:
                    act.wait_ge(S["pv_done"], i - 1)
                b = 3 * (i % 2)
                f(flat(pT[i % 2])[:, 512:1536], ps[:, b + 1:b + 3, :].rearrange("p b c -> p (b c)"), ACT.Copy).then_inc(S["pt_act"], 1)
                act.wait_ge(S["pt_act"], count("pt_act"))

            def out_turned(qt):
                act.wait_ge(S["ot_mm"], qt + 1)
                f(oT[:, :, qt * P:(qt + 1) * P], ps[:, 6 + qt % 2, :].rearrange("p (a c) -> p a c", a=4), ACT.Copy).then_inc(S["ot_used"], 1)
                act.wait_ge(S["ot_used"], count("ot_used"))

            for i in range(NI + 2):
                if i < NI:
                    probs(i)
                if 1 <= i <= NI:
                    probs_turned(i - 1)
                if i >= 2 and (i - 2) % 8 == 3 and i > 8:
                    out_turned((i - 2) // 8 - 1)
            out_turned(NT - 1)
            act.sem_inc(S["arrivals"], 1)
            act.wait_ge(S["arrivals"], 5 * 2)
            act.wait_ge(S["bd_zeroed"], 1)
            for n in range(NA, len(TILES)):
                tile(n, NA)
            act.sem_inc(S["arrivals"], 1)
            act.wait_ge(S["arrivals"], 5 * 3)

            act.wait_ge(S["bd_zeroed"], 2)
            for d, s, slot in SCHEDULE:
                level = int(slot[1:]) if slot[0] in "xu" else 0

                def diagonal(st, bd):
                    for h in range(2):
                        lo = slice(h * C, (h + 1) * C)
                        f(part(bd, d)[lo, :, lo], part(st, d)[lo], ACT.Copy).then_inc(S[f"dn_act{d}"], 1)
                        act.wait_ge(S[f"dn_act{d}"], count(f"dn_act{d}"))

                if slot == "decay":
                    act.wait_ge(S[f"dn_dve{d}"], value("dve", "glg", s))
                    x = gs[:, d, :]
                    f(x[:, 12:24], x[:, 0:12], ACT.Exp).then_inc(S[f"dn_act{d}"], 1)
                    act.wait_ge(S[f"dn_act{d}"], count(f"dn_act{d}"))
                    act.wait_ge(S[f"dn_dve{d}"], value("dve", "abs", s))
                    f(part(E, d), part(Dm, d), ACT.Exp, scale=-1.0).then_inc(S[f"dn_act{d}"], 1)
                    act.wait_ge(S[f"dn_act{d}"], count(f"dn_act{d}"))
                elif slot == "keys":
                    act.wait_ge(S[f"dn_pe{d}"], value("pe", "kt", s))
                    f(flat(part(ktok_bd, d)), ps[:, 4 * d + 2, :], ACT.Copy).then_inc(S[f"dn_act{d}"], 1)
                    act.wait_ge(S[f"dn_act{d}"], count(f"dn_act{d}"))
                    act.wait_ge(S[f"dn_pe{d}"], value("pe", "v", s))
                    f(part(V_st, d), half(d, 3, 0), ACT.Copy).then_inc(S[f"dn_act{d}"], 1)
                    act.wait_ge(S[f"dn_act{d}"], count(f"dn_act{d}"))
                elif slot == "state":
                    act.wait_ge(S[f"dn_dve{d}"], value("dve", "x0", s))
                    diagonal(X_st, X_bd)
                elif slot == "t0":
                    act.wait_ge(S[f"dn_dve{d}"], value("dve", "t0", s))
                    diagonal(T_st, T_bd)
                elif slot[0] == "x" and level < LEVELS - 1:
                    act.wait_ge(S[f"dn_dve{d}"], value("dve", f"x{level}", s))
                    diagonal(X_st, X_bd)
                elif slot[0] == "u" and level < LEVELS - 1:
                    act.wait_ge(S[f"dn_dve{d}"], value("dve", f"t{level}", s))
                    diagonal(T_st, T_bd)
                elif slot == "new":
                    act.wait_ge(S[f"dn_pe{d}"], value("pe", "vn", s))
                    f(part(vn, d), half(d, 1, 0), ACT.Copy).then_inc(S[f"dn_act{d}"], 1)
                    act.wait_ge(S[f"dn_act{d}"], count(f"dn_act{d}"))
            act.sem_inc(S["arrivals"], 1)
            act.wait_ge(S["arrivals"], 5 * 4)
            f(onsq, R1[:, 0:5120], ACT.Square).then_inc(S["osq_ready"], 1)
            act.wait_ge(S["osq_ready"], count("osq_ready"))
            act.wait_ge(S["onr_sum"], 1)
            f(onr, onr, ACT.Sqrt, bias=eps_head).then_inc(S["onr_root"], 1)
            act.wait_ge(S["onr_root"], count("onr_root"))
            for n in range(4):
                for g, (c0, w) in enumerate(GROUPS):
                    u = 3 * n + g
                    act.wait_ge(S["gate_mm"], u + 1)
                    if u > 0:
                        act.wait_ge(S["gate_used"], u)
                    f(sgd[:, 0:w], ps[:, 2 + u % 2, 0:w], ACT.Sigmoid).then_inc(S["gsig_ready"], 1)
                    act.wait_ge(S["gsig_ready"], count("gsig_ready"))
            act.sem_inc(S["arrivals"], 1)
            act.wait_ge(S["arrivals"], 5 * 5)
            for u, (c, g) in enumerate(MU):
                w = GROUPS[g][1]
                act.wait_ge(S["merge_mm"], u + 1)
                if u - 1 > 0:
                    act.wait_ge(S["merged"], u - 1)
                for x in range(2):
                    f(sg[2 * (u % 2) + x][:, 0:w], ps[:, 4 * (u % 2) + x, 0:w], ACT.Sigmoid).then_inc(S["msig_ready"], 1)
                    act.wait_ge(S["msig_ready"], count("msig_ready"))
            act.sem_inc(S["arrivals"], 1)
            act.wait_ge(S["arrivals"], 5 * 6)
            for u in range(16):
                act.wait_ge(S["row_mm"], u + 1)
                r, c, h = u // 4, (u // 2) % 2, u % 2
                f(rows[:, r, c, h * 512:(h + 1) * 512], ps[:, u % 2, :], ACT.Copy).then_inc(S["row_used"], 1)
                act.wait_ge(S["row_used"], count("row_used"))
            act.sem_inc(S["arrivals"], 1)
            act.wait_ge(S["arrivals"], 5 * 7)
            for n in range(NT):
                f(y_sb[0], x2[:, n, :], ACT.Square, accum_out=stat[:, 32 + n:33 + n]).then_inc(S["act_chain"], 1)
                act.wait_ge(S["act_chain"], count("act_chain"))
            f(stat[:, 32:42], stat[:, 32:42], ACT.Sqrt, bias=eps_unit, scale=1.0 / D).then_inc(S["ss2_ready"], 1)
            act.wait_ge(S["ss2_ready"], count("ss2_ready"))
            for n in range(NT):
                for h in range(2):
                    u = 2 * n + h
                    act.wait_ge(S["h2t_mm"], u + 1)
                    if n - 1 > 0:
                        act.wait_ge(S["rout_mm"], n - 1)
                    f(h2T[n % 2][:, 4 * h:4 * h + 4, :], ps[:, u % 2, :].rearrange("p (k t) -> p k t", k=4), ACT.Copy).then_inc(S["h2t_used"], 1)
                    act.wait_ge(S["h2t_used"], count("h2t_used"))
            act.wait_ge(S["lg_shift"], 1)
            f(flat(r_e5), flat(r_e5), ACT.Exp).then_inc(S["lg_exp"], 1)
            act.wait_ge(S["lg_exp"], count("lg_exp"))
            def slots_turned(t):
                for h in range(2):
                    act.wait_ge(S["hst_mm"], 2 * t + h + 1)
                    if t - 1 > 0:
                        act.wait_ge(S["gu_mm"], t - 1)
                    f(hsT[t % 2][:, 4 * h:4 * h + 4, :], ps[:, h, :].rearrange("p (k t) -> p k t", k=4), ACT.Copy).then_inc(S["hst_used"], 1)
                    act.wait_ge(S["hst_used"], count("hst_used"))

            slots_turned(0)
            for t in range(MT):
                act.wait_ge(S["gu_mm"], t + 1)
                f(sgh, ps[:, 2, 0:FF], ACT.Sigmoid).then_inc(S["gu_sig"], 1)
                act.wait_ge(S["gu_sig"], count("gu_sig"))
                if t + 1 < MT:
                    slots_turned(t + 1)
                act.wait_ge(S["dn_mm"], t + 1)
                if t - 2 >= 0:
                    act.wait_ge(S[f"y_out{(t - 2) % 2}"], landed(t - 2, 2))
                o = 4 + 2 * (t % 2)
                f(y_sb[t % 2], ps[:, o:o + 2, :].rearrange("p b c -> p (b c)"), ACT.Copy).then_inc(S["ysb_ready"], 1)
                act.wait_ge(S["ysb_ready"], count("ysb_ready"))
                act.dma_start(y_d[t * P:(t + 1) * P, :], y_sb[t % 2]).then_inc(S[f"y_out{t % 2}"], 16)
            for t in (MT - 2, MT - 1):
                act.wait_ge(S[f"y_out{t % 2}"], landed(t, 2))
            act.sem_inc(S["arrivals"], 1)
            act.wait_ge(S["arrivals"], 5 * 8)
            for n in range(NT):
                act.wait_ge(S["x3_ready"], n + 1)
                f(y_sb[0], x2[:, n, :], ACT.Square, accum_out=stat[:, 48 + n:49 + n]).then_inc(S["act_chain"], 1)
                act.wait_ge(S["act_chain"], count("act_chain"))
                f(stat[:, 48 + n:49 + n], stat[:, 48 + n:49 + n], ACT.Sqrt, bias=eps_unit, scale=1.0 / D).then_inc(S["ss3_ready"], 1)
                act.wait_ge(S["ss3_ready"], count("ss3_ready"))

        @block.vector
        def _(dve):
            v = nc.vector

            def bc(x, shape):
                return x.to_broadcast([P] + shape)

            for col, x in ((0, 1.0), (2, HD * EPS), (3, EPS)):
                signal = "eps_ready" if col == 3 else "dve_chain"
                v.memset(epsc[:, col:col + 1], x).then_inc(S[signal], 1)
                dve.wait_ge(S[signal], count(signal))
            dve.wait_ge(S["params_in"], 16 * 18)
            dve.wait_ge(S["cond_sig"], 1)
            v.tensor_tensor(cond_s[:], cond_s[:], cond[:], ALU.mult).then_inc(S["cond_ready"], 1)
            dve.wait_ge(S["cond_ready"], count("cond_ready"))
            for n in range(NT):
                dve.wait_ge(S["ssx_ready"], n + 1)
                v.reciprocal(stat[:, 16 + n:17 + n], stat[:, 16 + n:17 + n]).then_inc(S["rstdx_ready"], 1)
                dve.wait_ge(S["rstdx_ready"], count("rstdx_ready"))
                if n == 1:
                    dve.wait_ge(S["mod_turned"], 12)
                    v.tensor_tensor(mod[:], ps[:, 0, 0:96].rearrange("p (f c) -> p f c", c=2), bc(b_mod[:].unsqueeze(2), [48, 2]), ALU.add).then_inc(S["dve_chain"], 1)
                    dve.wait_ge(S["dve_chain"], count("dve_chain"))
                    for A_, f0, nw in ((A1, 8, norm_mix), (A2, 32, norm_ffn)):
                        v.scalar_tensor_tensor(A_[:], mod[:, f0:f0 + KD, :], 1.0, bc(nw[:].unsqueeze(2), [KD, 2]), ALU.add, ALU.mult).then_inc(S["dve_chain"], 1)
                        dve.wait_ge(S["dve_chain"], count("dve_chain"))
                if n >= 1:
                    for m in ([n - 1] if n < NT - 1 else [n - 1, n]):
                        ci = 0 if m < 2 else 1
                        for h in range(2):
                            u = 2 * m + h
                            dve.wait_ge(S["xt_done"], u + 1)
                            for k in range(4):
                                kk = 4 * h + k
                                signal = "xt_used" if k == 3 else "dve_chain"
                                v.tensor_scalar(hT[:, kk, m * P:(m + 1) * P], ps[:, 1 + u % 4, k * P:(k + 1) * P],
                                                A1[:, kk, ci:ci + 1], mod[:, kk, ci:ci + 1], ALU.mult, ALU.add).then_inc(S[signal], 1)
                                dve.wait_ge(S[signal], count(signal))
            v.tensor_scalar(qk_w[:], qk_w[:], 8.0, None, ALU.mult).then_inc(S["dve_chain"], 1)
            dve.wait_ge(S["dve_chain"], count("dve_chain"))
            v.tensor_scalar(dnn_w[:], dnn_w[:], 8.0, None, ALU.mult).then_inc(S["dve_chain"], 1)
            dve.wait_ge(S["dve_chain"], count("dve_chain"))

            SEG = [(0, 256, 1), (256, 1024, 259)]

            def norm_tile(n):
                raw, _, tmp, rstd = scratch(n)
                y = out_of(n)
                dve.wait_ge(S["root_ready"], 3 * n + 3)
                v.reciprocal(rstd, rstd).then_inc(S["dve_chain"], 1)
                dve.wait_ge(S["dve_chain"], count("dve_chain"))
                wcol = qk_w[:, 0:1] if TILES[n][0] == "aq" else qk_w[:, 1:2]
                for x, (c0, w, o) in enumerate(SEG):
                    signal = "y_ready" if x else "dve_chain"
                    v.scalar_tensor_tensor(y[:, c0:c0 + w], raw[:, o:o + w], wcol, rstd[:, c0:c0 + w], ALU.mult, ALU.mult).then_inc(S[signal], 1)
                    dve.wait_ge(S[signal], count(signal))
                dve.wait_ge(S["past_in"], 96)
                for g in (1, 2):
                    dve.wait_ge(S["rot_mm"], 2 * n + g)
                    c0, w = GROUPS[g]
                    v.tensor_tensor(tmp[:, c0:c0 + w], ps[:, 4 + g, 0:w], sin_t[:, c0 - CTX:c0 - CTX + w], ALU.mult).then_inc(S["rot_used"], 1)
                    dve.wait_ge(S["rot_used"], count("rot_used"))
                v.tensor_tensor(y[:, CTX:T], y[:, CTX:T], cos_t, ALU.mult).then_inc(S["dve_chain"], 1)
                dve.wait_ge(S["dve_chain"], count("dve_chain"))
                v.tensor_tensor(y[:, CTX:T], y[:, CTX:T], tmp[:, CTX:T], ALU.add).then_inc(S["tile_done"], 1)
                dve.wait_ge(S["tile_done"], count("tile_done"))

            for n in range(NA):
                norm_tile(n)
            for n in range(NT):
                dve.wait_ge(S["vba_mm"], n + 1)
                v.tensor_copy(v_sb[:, n, :], ps[:, n % 2, 0:P]).then_inc(S["dve_chain"], 1)
                dve.wait_ge(S["dve_chain"], count("dve_chain"))
                v.tensor_copy(ba[:, n, :], ps[:, n % 2, P:160]).then_inc(S["vba_used"], 1)
                dve.wait_ge(S["vba_used"], count("vba_used"))
            dve.wait_ge(S["pastT"], 1)
            v.tensor_copy(kT[:, T:T + PAST], ps[:, 2, :]).then_inc(S["pastT_used"], 1)
            dve.wait_ge(S["pastT_used"], count("pastT_used"))
            dve.wait_ge(S["kout_mm"], 1)
            v.tensor_copy(flat(ktok), ps[:, 3, 0:2 * P]).then_inc(S["kout_used"], 1)
            dve.wait_ge(S["kout_used"], count("kout_used"))
            v.tensor_tensor(zt, ba[:, :, 16:32], bc(dt_b[:].unsqueeze(1), [NT, 16]), ALU.add).then_inc(S["dve_chain"], 1)
            dve.wait_ge(S["dve_chain"], count("dve_chain"))
            v.scalar_tensor_tensor(gt, zt, -1.0, zt, ALU.mult, ALU.max).then_inc(S["dec_abs"], 1)
            dve.wait_ge(S["dec_abs"], count("dec_abs"))
            v.tensor_scalar(zt, zt, 0.0, None, ALU.max).then_inc(S["dve_chain"], 1)
            dve.wait_ge(S["dve_chain"], count("dve_chain"))
            dve.wait_ge(S["beta_ready"], 1)
            dve.wait_ge(S["dec_ln"], 1)
            v.tensor_tensor(gt, gt, zt, ALU.add).then_inc(S["dve_chain"], 1)
            dve.wait_ge(S["dve_chain"], count("dve_chain"))
            v.scalar_tensor_tensor(gt, gt, -1.0, bc(a_log[:].unsqueeze(1), [NT, 16]), ALU.mult, ALU.mult).then_inc(S["dve_chain"], 1)
            dve.wait_ge(S["dve_chain"], count("dve_chain"))
            for h in range(2):
                v.tensor_copy(bg[:, 0, h], bt.rearrange("p n (e h) -> p h n e", h=2)[:, h]).then_inc(S["dve_chain"], 1)
                dve.wait_ge(S["dve_chain"], count("dve_chain"))
                signal = "bg_ready" if h else "dve_chain"
                v.tensor_copy(bg[:, 1, h], gt.rearrange("p n (e h) -> p h n e", h=2)[:, h]).then_inc(S[signal], 1)
                dve.wait_ge(S[signal], count(signal))
            dve.sem_inc(S["arrivals"], 1)
            dve.wait_ge(S["arrivals"], 5 * 1)

            NI = len(ITEMS)

            def largest(i):
                w = keys(ITEMS[i][0])[1] * P
                dve.wait_ge(S["sc_ready"], i + 1)
                if i - 1 > 0:
                    dve.wait_ge(S["p_ready"], i - 1)
                src = ps[:, 3 * (i % 2):3 * (i % 2) + 3, :].rearrange("p b c -> p (b c)")[:, 0:w]
                v.tensor_reduce(ast[:, 34:35], src, AX.X, ALU.max).then_inc(S["dve_chain"], 1)
                dve.wait_ge(S["dve_chain"], count("dve_chain"))
                v.tensor_scalar(ast[:, 32 + i % 2:33 + i % 2], ast[:, 34:35], -HD ** -0.5, None, ALU.mult).then_inc(S["mx_ready"], 1)
                dve.wait_ge(S["mx_ready"], count("mx_ready"))

            def probs_turned(i):
                dve.wait_ge(S["pt_mm"], i + 1)
                if i - 1 > 0:
                    dve.wait_ge(S["pv_done"], i - 1)
                w = 256 if i < CTX_ITEMS else 512
                v.tensor_copy(flat(pT[i % 2])[:, 0:w], ps[:, 3 * (i % 2), 0:w]).then_inc(S["pt_dve"], 1)
                dve.wait_ge(S["pt_dve"], count("pt_dve"))

            def heads_out(qt):
                dve.wait_ge(S["pv_done"], 8 * (qt + 1))
                if qt > 0:
                    dve.wait_ge(S["ot_mm"], qt)
                v.reciprocal(ast[:, 16:24], ast[:, 8 * (qt % 2):8 * (qt % 2) + 8]).then_inc(S["dve_chain"], 1)
                dve.wait_ge(S["dve_chain"], count("dve_chain"))
                v.tensor_tensor(o_tok.rearrange("p (h d) -> p h d", h=NH), bank8(6 + qt % 2), bc(ast[:, 16:24].unsqueeze(2), [NH, HD]), ALU.mult).then_inc(S["o_ready"], 1)
                dve.wait_ge(S["o_ready"], count("o_ready"))

            for i in range(NI + 2):
                if i < NI:
                    largest(i)
                if 1 <= i <= NI:
                    probs_turned(i - 1)
                if i >= 2 and (i - 2) % 8 == 7:
                    heads_out((i - 2) // 8)
            dve.sem_inc(S["arrivals"], 1)
            dve.wait_ge(S["arrivals"], 5 * 2)

            dve.wait_ge(S["bd_zeroed"], 1)

            def convolve(n):
                raw, _, tmp, _ = scratch(n)
                ct = TILES.index(("dq", 0))
                dve.wait_ge(S["gemm_used"], 3 * n + 3)
                for tap in (1, 0, 2):
                    wc = conv_w[:, n - ct, tap:tap + 1]
                    for x, (c0, w, o) in enumerate(SEG):
                        src = raw[:, o - 1 + tap:o - 1 + tap + w]
                        if tap == 1:
                            v.tensor_scalar(tmp[:, c0:c0 + w], src, wc, None, ALU.mult).then_inc(S["dve_chain"], 1)
                            dve.wait_ge(S["dve_chain"], count("dve_chain"))
                        else:
                            signal = "conv_ready" if tap == 2 and x else "dve_chain"
                            v.scalar_tensor_tensor(tmp[:, c0:c0 + w], src, wc, tmp[:, c0:c0 + w], ALU.mult, ALU.add).then_inc(S[signal], 1)
                            dve.wait_ge(S[signal], count(signal))

            def silu(n):
                _, sq, tmp, _ = scratch(n)
                if n - NA + 1 > 0:
                    dve.wait_ge(S["sigm_ready"], n - NA + 1)
                v.tensor_tensor(out_of(n), tmp, sq, ALU.mult).then_inc(S["z_ready"], 1)
                dve.wait_ge(S["z_ready"], count("z_ready"))
                if not stats(n):
                    v.tensor_scalar(epsc[:, 1:2], epsc[:, 0:1], 1.0, None, ALU.mult).then_inc(S["tile_done"], 1)
                    dve.wait_ge(S["tile_done"], count("tile_done"))

            def unit(n):
                rstd = scratch(n)[3]
                dve.wait_ge(S["root_ready"], 3 * n + 3)
                v.reciprocal(rstd, rstd).then_inc(S["dve_chain"], 1)
                dve.wait_ge(S["dve_chain"], count("dve_chain"))
                sc = HD ** -0.5 if TILES[n][0] == "dq" else 1.0
                v.scalar_tensor_tensor(out_of(n), out_of(n), sc, rstd, ALU.mult, ALU.mult).then_inc(S["tile_done"], 1)
                dve.wait_ge(S["tile_done"], count("tile_done"))

            for n in range(NA, len(TILES) + 1):
                if n < len(TILES):
                    convolve(n)
                if n - 1 >= NA and stats(n - 1):
                    unit(n - 1)
                if n < len(TILES):
                    silu(n)
            dve.sem_inc(S["arrivals"], 1)
            dve.wait_ge(S["arrivals"], 5 * 3)

            dve.wait_ge(S["bd_zeroed"], 2)
            dve.wait_ge(S["state_in"], 64)
            for d, s, slot in SCHEDULE:
                st = part(S_ctx if s < CTX_CH else S_lat, d)
                ch = CHUNKS[s][d]
                x = gs[:, d, :]
                level = int(slot[1:]) if slot[0] in "xu" else 0
                eye4 = bc(eye_st.unsqueeze(1), [4, C])

                def row(c0):
                    return bc(gs[:, d, c0:c0 + 4].unsqueeze(2), [4, C])

                def x_level(l):
                    dve.wait_ge(S[f"dn_pe{d}"], value("pe", f"x{l}", s))
                    v.tensor_tensor(part(X_st, d), half(d, 2, 0), bc(levels[:, d, l, :].unsqueeze(1), [4, C]), ALU.mult).then_inc(S[f"dn_dve{d}"], 1)
                    dve.wait_ge(S[f"dn_dve{d}"], count(f"dn_dve{d}"))

                if slot == "decay":
                    g = bg_st[:, 1, ch % 2, ch // 2, 4 * d:4 * d + 4]
                    v.tensor_tensor(part(gM, d), bc(upto[:, d, :].unsqueeze(1), [4, C]), bc(g.unsqueeze(2), [4, C]), ALU.mult).then_inc(S[f"dn_dve{d}"], 1)
                    dve.wait_ge(S[f"dn_dve{d}"], count(f"dn_dve{d}"))
                    v.tensor_copy(x[:, 24:28], bg_st[:, 0, ch % 2, ch // 2, 4 * d:4 * d + 4]).then_inc(S[f"dn_dve{d}"], 1)
                    dve.wait_ge(S[f"dn_dve{d}"], count(f"dn_dve{d}"))
                    dve.wait_ge(S[f"dn_pe{d}"], value("pe", "g", s))
                    v.tensor_copy(x[:, 0:8], ps[:, 4 * d, 256:264]).then_inc(S[f"dn_dve{d}"], 1)
                    dve.wait_ge(S[f"dn_dve{d}"], count(f"dn_dve{d}"))
                    v.tensor_tensor(x[:, 8:12], x[:, 4:8], x[:, 0:4], ALU.subtract).then_inc(S[f"dn_dve{d}"], 1)
                    dve.wait_ge(S[f"dn_dve{d}"], count(f"dn_dve{d}"))
                    v.tensor_tensor(part(Dm, d), row(0), half(d, 0, 0), ALU.subtract).then_inc(S[f"dn_dve{d}"], 1)
                    dve.wait_ge(S[f"dn_dve{d}"], count(f"dn_dve{d}"))
                    v.scalar_tensor_tensor(part(Dm, d), part(Dm, d), -1.0, part(Dm, d), ALU.mult, ALU.max).then_inc(S[f"dn_dve{d}"], 1)
                    dve.wait_ge(S[f"dn_dve{d}"], count(f"dn_dve{d}"))
                elif slot == "keys":
                    dve.wait_ge(S[f"dn_act{d}"], value("act", "e", s))
                    v.tensor_tensor(part(Dm, d), part(E, d), row(24), ALU.mult).then_inc(S[f"dn_dve{d}"], 1)
                    dve.wait_ge(S[f"dn_dve{d}"], count(f"dn_dve{d}"))
                    dve.wait_ge(S[f"dn_pe{d}"], value("pe", "kkq", s))
                    kkq = ps[:, 4 * d + 1, :].rearrange("p (a x c) -> p a x c", a=4, x=2)
                    for h in range(2):
                        lo = slice(h * C, (h + 1) * C)
                        v.tensor_tensor(part(L_bd, d)[lo, :, lo], kkq[lo, :, 1, :], part(Dm, d)[lo], ALU.mult).then_inc(S[f"dn_dve{d}"], 1)
                        dve.wait_ge(S[f"dn_dve{d}"], count(f"dn_dve{d}"))
                elif slot == "state":
                    x_level(0)
                    v.tensor_tensor(part(U_st, d), eye4, part(X_st, d), ALU.subtract).then_inc(S[f"dn_dve{d}"], 1)
                    dve.wait_ge(S[f"dn_dve{d}"], count(f"dn_dve{d}"))
                    v.tensor_tensor(part(R_st, d), half(d, 0, 0), row(12), ALU.mult).then_inc(S[f"dn_dve{d}"], 1)
                    dve.wait_ge(S[f"dn_dve{d}"], count(f"dn_dve{d}"))
                    v.tensor_tensor(part(o1, d), half(d, 0, 1), row(12), ALU.mult).then_inc(S[f"dn_dve{d}"], 1)
                    dve.wait_ge(S[f"dn_dve{d}"], count(f"dn_dve{d}"))
                elif slot == "t0":
                    dve.wait_ge(S[f"dn_pe{d}"], value("pe", "t0", s))
                    v.tensor_tensor(part(T_st, d), eye4, half(d, 0, 0), ALU.subtract).then_inc(S[f"dn_dve{d}"], 1)
                    dve.wait_ge(S[f"dn_dve{d}"], count(f"dn_dve{d}"))
                    v.tensor_tensor(part(E, d), part(E, d), bc(upto[:, d, :].unsqueeze(1), [4, C]), ALU.mult).then_inc(S[f"dn_dve{d}"], 1)
                    dve.wait_ge(S[f"dn_dve{d}"], count(f"dn_dve{d}"))
                    kkq = ps[:, 4 * d + 1, :].rearrange("p (a x c) -> p a x c", a=4, x=2)
                    for h in range(2):
                        lo = slice(h * C, (h + 1) * C)
                        v.tensor_tensor(part(A_bd, d)[lo, :, lo], kkq[lo, :, 0, :], part(E, d)[lo], ALU.mult).then_inc(S[f"dn_dve{d}"], 1)
                        dve.wait_ge(S[f"dn_dve{d}"], count(f"dn_dve{d}"))
                    dve.wait_ge(S[f"dn_act{d}"], value("act", "v", s))
                    v.tensor_tensor(part(R_st, d), part(V_st, d), part(R_st, d), ALU.subtract).then_inc(S[f"dn_dve{d}"], 1)
                    dve.wait_ge(S[f"dn_dve{d}"], count(f"dn_dve{d}"))
                    v.tensor_tensor(part(R_st, d), part(R_st, d), row(24), ALU.mult).then_inc(S[f"dn_dve{d}"], 1)
                    dve.wait_ge(S[f"dn_dve{d}"], count(f"dn_dve{d}"))
                elif slot[0] == "x":
                    x_level(level)
                elif slot[0] == "u" and level < LEVELS - 1:
                    dve.wait_ge(S[f"dn_pe{d}"], value("pe", f"u{level}", s))
                    v.tensor_tensor(part(U_st, d), part(U_st, d), half(d, 3, 0), ALU.subtract).then_inc(S[f"dn_dve{d}"], 1)
                    dve.wait_ge(S[f"dn_dve{d}"], count(f"dn_dve{d}"))
                    dve.wait_ge(S[f"dn_pe{d}"], value("pe", f"t{level}", s))
                    v.tensor_tensor(part(T_st, d), part(T_st, d), half(d, 0, 0), ALU.subtract).then_inc(S[f"dn_dve{d}"], 1)
                    dve.wait_ge(S[f"dn_dve{d}"], count(f"dn_dve{d}"))
                elif slot[0] == "u":
                    dve.wait_ge(S[f"dn_pe{d}"], value("pe", f"u{level}", s))
                    for h in range(2):
                        lo = slice(h * C, (h + 1) * C)
                        v.tensor_tensor(part(U_bd, d)[lo, :, lo], part(U_st, d)[lo], half(d, 3, 0)[lo], ALU.subtract).then_inc(S[f"dn_dve{d}"], 1)
                        dve.wait_ge(S[f"dn_dve{d}"], count(f"dn_dve{d}"))
                elif slot == "new":
                    dve.wait_ge(S[f"dn_act{d}"], value("act", "vn", s))
                    v.tensor_tensor(part(vd, d), part(vn, d), row(20), ALU.mult).then_inc(S[f"dn_dve{d}"], 1)
                    dve.wait_ge(S[f"dn_dve{d}"], count(f"dn_dve{d}"))
                else:
                    dve.wait_ge(S[f"dn_pe{d}"], value("pe", "av", s))
                    if s - 1 >= 0:
                        dve.wait_ge(S[f"dn_acc{d}"], value("acc", "o", s - 1))
                    v.tensor_tensor(part(oo, d), part(o1, d), half(d, 2, 0), ALU.add).then_inc(S[f"dn_dve{d}"], 1)
                    dve.wait_ge(S[f"dn_dve{d}"], count(f"dn_dve{d}"))
                    v.tensor_tensor(st, st, row(16), ALU.mult).then_inc(S[f"dn_dve{d}"], 1)
                    dve.wait_ge(S[f"dn_dve{d}"], count(f"dn_dve{d}"))
                    dve.wait_ge(S[f"dn_pe{d}"], value("pe", "s", s))
                    v.tensor_tensor(st, st, half(d, 3, 0), ALU.add).then_inc(S[f"dn_dve{d}"], 1)
                    dve.wait_ge(S[f"dn_dve{d}"], count(f"dn_dve{d}"))
            dve.sem_inc(S["arrivals"], 1)
            dve.wait_ge(S["arrivals"], 5 * 4)

            for cc in range(2):
                v.memset(flat(on_bd[cc]), 0.0).then_inc(S["dve_chain"], 1)
                dve.wait_ge(S["dve_chain"], count("dve_chain"))
            dve.wait_ge(S["osq_ready"], 1)
            v.tensor_reduce(onr, onsq.rearrange("p (n d) -> p n d", d=C), AX.X, ALU.add).then_inc(S["onr_sum"], 1)
            dve.wait_ge(S["onr_sum"], count("onr_sum"))
            dve.wait_ge(S["onr_root"], 1)
            v.reciprocal(onr, onr).then_inc(S["dve_chain"], 1)
            dve.wait_ge(S["dve_chain"], count("dve_chain"))
            for u in range(NCH // 2):
                for cc in range(2):
                    ch = 2 * u + cc
                    if u > 0:
                        dve.wait_ge(S["odT_mm"], u)
                    for h in range(2):
                        lo = slice(h * C, (h + 1) * C)
                        r = onr[lo, 4 * ch:4 * ch + 4].unsqueeze(2).to_broadcast([C, 4, C])
                        signal = "on_ready" if h else "dve_chain"
                        v.tensor_tensor(on_bd[cc][lo, :, lo], oacc[lo, ch], r, ALU.mult).then_inc(S[signal], 1)
                        dve.wait_ge(S[signal], count(signal))
                dve.wait_ge(S["odT_mm"], u + 1)
                v.tensor_scalar(odT[:, :, u * P:(u + 1) * P], ps[:, u % 2, :].rearrange("p (a c) -> p a c", a=4), dnn_w[:, 0:1], None, ALU.mult).then_inc(S["od_ready"], 1)
                dve.wait_ge(S["od_ready"], count("od_ready"))
            for n in range(4):
                for g, (c0, w) in enumerate(GROUPS):
                    u = 3 * n + g
                    dve.wait_ge(S["gsig_ready"], u + 1)
                    v.tensor_tensor(tdg[:, 0:w], ps[:, 2 + u % 2, 0:w], sgd[:, 0:w], ALU.mult).then_inc(S["gate_used"], 1)
                    dve.wait_ge(S["gate_used"], count("gate_used"))
                    v.tensor_tensor(odT[:, n, c0:c0 + w], odT[:, n, c0:c0 + w], tdg[:, 0:w], ALU.mult).then_inc(S["dve_chain"], 1)
                    dve.wait_ge(S["dve_chain"], count("dve_chain"))
            dve.sem_inc(S["arrivals"], 1)
            dve.wait_ge(S["arrivals"], 5 * 5)
            for u, (c, g) in enumerate(MU):
                c0, w = GROUPS[g]
                dve.wait_ge(S["msig_ready"], 2 * u + 2)
                for x in range(2):
                    v.tensor_tensor(m1[x][:, 0:w], ps[:, 4 * (u % 2) + 2 + x, 0:w], sg[2 * (u % 2) + x][:, 0:w], ALU.mult).then_inc(S["dve_chain"], 1)
                    dve.wait_ge(S["dve_chain"], count("dve_chain"))
                v.tensor_tensor(mT[:, c, c0:c0 + w], m1[0][:, 0:w], m1[1][:, 0:w], ALU.add).then_inc(S["merged"], 1)
                dve.wait_ge(S["merged"], count("merged"))
            dve.sem_inc(S["arrivals"], 1)
            dve.wait_ge(S["arrivals"], 5 * 6)
            sources = [mod[:, 16:24, :], A2[:], mod[:, 24:32, :], mod[:, 40:48, :]]
            for u in range(16):
                r, c, h = u // 4, (u // 2) % 2, u % 2
                if u - 1 > 0:
                    dve.wait_ge(S["row_mm"], u - 1)
                col = sources[r][:, 4 * h:4 * h + 4, c:c + 1]
                v.tensor_tensor(row_rhs[u % 2].rearrange("p (k n) -> p k n", k=4), bc(ident.unsqueeze(1), [4, P]), bc(col, [4, P]), ALU.mult).then_inc(S["row_rhs"], 1)
                dve.wait_ge(S["row_rhs"], count("row_rhs"))
            dve.wait_ge(S["row_used"], 16)
            for n in range(NT):
                ci = 0 if n < 2 else 1
                dve.wait_ge(S["out_mm"], n + 1)
                dve.wait_ge(S[f"xr_in{n % 2}"], landed(n, 2))
                b = 2 * (n % 2)
                v.tensor_tensor(x2[:, n, :], ps[:, b:b + 2, :].rearrange("p b c -> p (b c)"), rows[:, 0, ci, :], ALU.mult).then_inc(S["dve_chain"], 1)
                dve.wait_ge(S["dve_chain"], count("dve_chain"))
                v.tensor_tensor(x2[:, n, :], x2[:, n, :], xr[n % 2], ALU.add).then_inc(S["out_used"], 1)
                dve.wait_ge(S["out_used"], count("out_used"))
            dve.sem_inc(S["arrivals"], 1)
            dve.wait_ge(S["arrivals"], 5 * 7)
            dve.wait_ge(S["ss2_ready"], 1)
            v.reciprocal(stat[:, 32:42], stat[:, 32:42]).then_inc(S["dve_chain"], 1)
            dve.wait_ge(S["dve_chain"], count("dve_chain"))
            for n in range(NT + 1):
                if n < NT:
                    ci = 0 if n < 2 else 1
                    if 2 * (n - 1) > 0:
                        dve.wait_ge(S["h2t_mm"], 2 * (n - 1))
                    if n - 2 >= 0:
                        dve.wait_ge(S[f"h2_out{(n - 2) % 2}"], landed(n - 2, 2))
                    v.scalar_tensor_tensor(h2[n % 2], x2[:, n, :], stat[:, 32 + n:33 + n], rows[:, 1, ci, :], ALU.mult, ALU.mult).then_inc(S["dve_chain"], 1)
                    dve.wait_ge(S["dve_chain"], count("dve_chain"))
                    v.tensor_tensor(h2[n % 2], h2[n % 2], rows[:, 2, ci, :], ALU.add).then_inc(S["h2_ready"], 1)
                    dve.wait_ge(S["h2_ready"], count("h2_ready"))
                if n:
                    if n > 0:
                        dve.wait_ge(S["rout_mm"], n)
                    v.tensor_tensor(lg[:, n - 1, :], ps[:, 2 + (n - 1) % 2, 0:20], b_r[:], ALU.add).then_inc(S["rout_used"], 1)
                    dve.wait_ge(S["rout_used"], count("rout_used"))

            def first_only(oh):
                v.tensor_copy(r_seen, oh[:, :, 0:1]).then_inc(S["dve_chain"], 1)
                dve.wait_ge(S["dve_chain"], count("dve_chain"))
                for k in range(1, 4):
                    v.tensor_scalar(r_not, r_seen, -1.0, 1.0, ALU.mult, ALU.add).then_inc(S["dve_chain"], 1)
                    dve.wait_ge(S["dve_chain"], count("dve_chain"))
                    v.tensor_tensor(oh[:, :, k:k + 1], oh[:, :, k:k + 1], r_not, ALU.mult).then_inc(S["dve_chain"], 1)
                    dve.wait_ge(S["dve_chain"], count("dve_chain"))
                    v.tensor_tensor(r_seen, r_seen, oh[:, :, k:k + 1], ALU.add).then_inc(S["dve_chain"], 1)
                    dve.wait_ge(S["dve_chain"], count("dve_chain"))

            def top(x, mx, oh):
                v.tensor_reduce(mx, x, AX.X, ALU.max).then_inc(S["dve_chain"], 1)
                dve.wait_ge(S["dve_chain"], count("dve_chain"))
                v.tensor_tensor(oh, x, bc(mx, [NT, 4]), ALU.is_equal).then_inc(S["dve_chain"], 1)
                dve.wait_ge(S["dve_chain"], count("dve_chain"))
                first_only(oh)

            lgG = lg[:, :, 0:4]
            top(lgG, r_gm, r_ohg)
            v.tensor_tensor(r_e5[:, :, 0:4], lgG, bc(r_gm, [NT, 4]), ALU.subtract).then_inc(S["dve_chain"], 1)
            dve.wait_ge(S["dve_chain"], count("dve_chain"))
            for e in range(4):
                v.tensor_tensor(r_sel, lg[:, :, 4 + e:20:4], r_ohg, ALU.mult).then_inc(S["dve_chain"], 1)
                dve.wait_ge(S["dve_chain"], count("dve_chain"))
                v.tensor_reduce(r_el[:, :, e:e + 1], r_sel, AX.X, ALU.add).then_inc(S["dve_chain"], 1)
                dve.wait_ge(S["dve_chain"], count("dve_chain"))
            top(r_el, r_m1, r_oh1)
            v.scalar_tensor_tensor(r_el2, r_oh1, -3e38, r_el, ALU.mult, ALU.add).then_inc(S["dve_chain"], 1)
            dve.wait_ge(S["dve_chain"], count("dve_chain"))
            top(r_el2, r_m2, r_oh2)
            v.tensor_tensor(r_e5[:, :, 4:5], r_m2, r_m1, ALU.subtract).then_inc(S["lg_shift"], 1)
            dve.wait_ge(S["lg_shift"], count("lg_shift"))
            for oh, dst in ((r_oh1, m_one), (r_oh2, m_two)):
                for g in range(4):
                    v.tensor_tensor(dst[:, :, 4 * g:4 * g + 4], oh, bc(r_ohg[:, :, g:g + 1], [NT, 4]), ALU.mult).then_inc(S["dve_chain"], 1)
                    dve.wait_ge(S["dve_chain"], count("dve_chain"))
            v.tensor_tensor(m_all, m_one, m_two, ALU.add).then_inc(S["masks_ready"], 1)
            dve.wait_ge(S["masks_ready"], count("masks_ready"))
            dve.wait_ge(S["lg_exp"], 1)
            v.tensor_reduce(r_gm, r_e5[:, :, 0:4], AX.X, ALU.add).then_inc(S["dve_chain"], 1)
            dve.wait_ge(S["dve_chain"], count("dve_chain"))
            v.tensor_scalar(r_m1, r_e5[:, :, 4:5], 1.0, None, ALU.add).then_inc(S["dve_chain"], 1)
            dve.wait_ge(S["dve_chain"], count("dve_chain"))
            v.tensor_tensor(r_gm, r_gm, r_m1, ALU.mult).then_inc(S["dve_chain"], 1)
            dve.wait_ge(S["dve_chain"], count("dve_chain"))
            v.reciprocal(wts[:, 0].unsqueeze(2), r_gm).then_inc(S["dve_chain"], 1)
            dve.wait_ge(S["dve_chain"], count("dve_chain"))
            v.tensor_tensor(wts[:, 1].unsqueeze(2), wts[:, 0].unsqueeze(2), r_e5[:, :, 4:5], ALU.mult).then_inc(S["dve_chain"], 1)
            dve.wait_ge(S["dve_chain"], count("dve_chain"))
            dve.wait_ge(S["rank_mm"], 1)
            v.tensor_copy(flat(r_cnt), ps[:, 5, 0:NT * NE]).then_inc(S["dve_chain"], 1)
            dve.wait_ge(S["dve_chain"], count("dve_chain"))
            v.memset(r_pre[:, 0, :], 0.0).then_inc(S["dve_chain"], 1)
            dve.wait_ge(S["dve_chain"], count("dve_chain"))
            for n in range(NT):
                v.tensor_tensor(r_pre[:, n + 1, :], r_pre[:, n, :], r_cnt[:, n, :], ALU.add).then_inc(S["dve_chain"], 1)
                dve.wait_ge(S["dve_chain"], count("dve_chain"))
            total = r_pre[:, NT, :]
            v.tensor_tensor(r_cmp[:, 0:NE * NT].rearrange("p (e k) -> p e k", e=NE), bc(total.unsqueeze(2), [NE, NT]), bc(k128.unsqueeze(1), [NE, NT]), ALU.is_gt).then_inc(S["dve_chain"], 1)
            dve.wait_ge(S["dve_chain"], count("dve_chain"))
            v.tensor_reduce(r_nt, r_cmp[:, 0:NE * NT].rearrange("p (e k) -> p e k", e=NE), AX.X, ALU.add).then_inc(S["dve_chain"], 1)
            dve.wait_ge(S["dve_chain"], count("dve_chain"))
            v.tensor_tensor(r_cmp[:, 0:NE * NE].rearrange("p (e k) -> p e k", e=NE), precedes, bc(r_nt.unsqueeze(1), [NE, NE]), ALU.mult).then_inc(S["dve_chain"], 1)
            dve.wait_ge(S["dve_chain"], count("dve_chain"))
            v.tensor_reduce(r_base, r_cmp[:, 0:NE * NE].rearrange("p (e k) -> p e k", e=NE), AX.X, ALU.add).then_inc(S["dve_chain"], 1)
            dve.wait_ge(S["dve_chain"], count("dve_chain"))
            v.tensor_tensor(r_nt, r_nt, r_base, ALU.add).then_inc(S["dve_chain"], 1)
            dve.wait_ge(S["dve_chain"], count("dve_chain"))
            v.tensor_scalar(r_base, r_base, float(P), None, ALU.mult).then_inc(S["dve_chain"], 1)
            dve.wait_ge(S["dve_chain"], count("dve_chain"))
            v.tensor_tensor(r_cnt, r_pre[:, 0:NT, :], bc(r_base.unsqueeze(1), [NT, NE]), ALU.add).then_inc(S["dve_chain"], 1)
            dve.wait_ge(S["dve_chain"], count("dve_chain"))
            v.tensor_tensor(r_cnt, r_cnt, ps[:, 4, 0:NT * NE].rearrange("p (n e) -> p n e", n=NT), ALU.add).then_inc(S["dve_chain"], 1)
            dve.wait_ge(S["dve_chain"], count("dve_chain"))
            for k, m in enumerate((m_one, m_two)):
                v.tensor_tensor(m, m, r_cnt, ALU.mult).then_inc(S["dve_chain"], 1)
                dve.wait_ge(S["dve_chain"], count("dve_chain"))
                v.tensor_reduce(r_pos[:, k, :], m, AX.X, ALU.add).then_inc(S["dve_chain"], 1)
                dve.wait_ge(S["dve_chain"], count("dve_chain"))
            v.tensor_copy(pos_i[:], r_pos).then_inc(S["dve_chain"], 1)
            dve.wait_ge(S["dve_chain"], count("dve_chain"))
            ends = r_cmp[:, 0:MT * NE].rearrange("p (t e) -> p t e", t=MT)
            v.tensor_tensor(ends, bc(tile_no.unsqueeze(2), [MT, NE]), bc(r_nt.unsqueeze(1), [MT, NE]), ALU.is_ge).then_inc(S["dve_chain"], 1)
            dve.wait_ge(S["dve_chain"], count("dve_chain"))
            v.tensor_reduce(r_tex, ends, AX.X, ALU.add).then_inc(S["dve_chain"], 1)
            dve.wait_ge(S["dve_chain"], count("dve_chain"))
            v.tensor_scalar(r_tex, r_tex, float(NE - 1), None, ALU.min).then_inc(S["dve_chain"], 1)
            dve.wait_ge(S["dve_chain"], count("dve_chain"))
            v.tensor_copy(tex_i[:], r_tex).then_inc(S["pos_ready"], 1)
            dve.wait_ge(S["pos_ready"], count("pos_ready"))
            for t in range(MT):
                dve.wait_ge(S["gu_sig"], t + 1)
                v.tensor_tensor(hid, ps[:, 2, 0:FF], sgh, ALU.mult).then_inc(S["dve_chain"], 1)
                dve.wait_ge(S["dve_chain"], count("dve_chain"))
                v.tensor_tensor(hid, hid, ps[:, 2, FF:2 * FF], ALU.mult).then_inc(S["hid_ready"], 1)
                dve.wait_ge(S["hid_ready"], count("hid_ready"))
                dve.wait_ge(S["hidt_mm"], t + 1)
                v.tensor_copy(flat(hidT), ps[:, 3, 0:FF]).then_inc(S["hidt_used"], 1)
                dve.wait_ge(S["hidt_used"], count("hidt_used"))
            dve.sem_inc(S["arrivals"], 1)
            dve.wait_ge(S["arrivals"], 5 * 8)
            for n in range(NT):
                ci = 0 if n < 2 else 1
                y0, y1 = yg[2 * (n % 2)], yg[2 * (n % 2) + 1]
                dve.wait_ge(S[f"y_in{n % 2}"], landed(n, 2, 2))
                v.tensor_scalar(y0, y0, wts[:, 0, n:n + 1], None, ALU.mult).then_inc(S["dve_chain"], 1)
                dve.wait_ge(S["dve_chain"], count("dve_chain"))
                v.scalar_tensor_tensor(y0, y1, wts[:, 1, n:n + 1], y0, ALU.mult, ALU.add).then_inc(S["dve_chain"], 1)
                dve.wait_ge(S["dve_chain"], count("dve_chain"))
                v.tensor_tensor(y0, y0, rows[:, 3, ci, :], ALU.mult).then_inc(S["dve_chain"], 1)
                dve.wait_ge(S["dve_chain"], count("dve_chain"))
                v.tensor_tensor(x2[:, n, :], x2[:, n, :], y0, ALU.add).then_inc(S["x3_ready"], 1)
                dve.wait_ge(S["x3_ready"], count("x3_ready"))
                dve.wait_ge(S["ss3_ready"], n + 1)
                st = stat[:, 48 + n:49 + n]
                v.reciprocal(st, st).then_inc(S["dve_chain"], 1)
                dve.wait_ge(S["dve_chain"], count("dve_chain"))
                v.scalar_tensor_tensor(x2[:, n, :], x2[:, n, :], st, nf_row, ALU.mult, ALU.mult).then_inc(S["out_ready"], 1)
                dve.wait_ge(S["out_ready"], count("out_ready"))

        @block.gpsimd
        def _(pool):
            g = nc.gpsimd
            g.iota(tok_i[:], pattern=[[P, NT]], base=0, channel_multiplier=1).then_inc(S["pool_chain"], 1)
            pool.wait_ge(S["pool_chain"], count("pool_chain"))
            g.memset(slot_i[:], 0).then_inc(S["pool_chain"], 1)
            pool.wait_ge(S["pool_chain"], count("pool_chain"))
            pool.dma_start(slot_d.rearrange("(t p) x -> p (t x)", p=P), slot_i[:]).then_inc(S["slot_zero"], 16)
            pool.wait_ge(S["slot_zero"], 16)
            pool.sem_inc(S["arrivals"], 1)
            pool.wait_ge(S["arrivals"], 5 * 1)
            pool.sem_inc(S["arrivals"], 1)
            pool.wait_ge(S["arrivals"], 5 * 2)
            for n in range(NA, NA + 2):
                raw = scratch(n)[0]
                for c0, w in ((0, 1), (257, 2), (1283, 1)):
                    signal = "bd_zeroed" if (n, c0) == (NA + 1, 1283) else "pool_chain"
                    g.memset(raw[:, c0:c0 + w], 0.0).then_inc(S[signal], 1)
                    pool.wait_ge(S[signal], count(signal))
            pool.sem_inc(S["arrivals"], 1)
            pool.wait_ge(S["arrivals"], 5 * 3)
            for b in (k_bd, q_bd, v_bd, L_bd, A_bd, X_bd, U_bd, T_bd):
                g.memset(flat(b), 0.0).then_inc(S["pool_chain"], 1)
                pool.wait_ge(S["pool_chain"], count("pool_chain"))
            g.memset(S_ctx[:], 0.0).then_inc(S["pool_chain"], 1)
            pool.wait_ge(S["pool_chain"], count("pool_chain"))
            g.memset(R1[:, 0:5120], 0.0).then_inc(S["bd_zeroed"], 1)
            pool.wait_ge(S["bd_zeroed"], count("bd_zeroed"))

            for d, s, slot in SCHEDULE:
                ch = CHUNKS[s][d]
                for s_next in ([0] if s == 0 and slot == "decay" else []) + ([s + 1] if slot == "t0" and s + 1 < NCK else []):
                    nx = CHUNKS[s_next][d]
                    if s_next - 1 >= 0:
                        pool.wait_ge(S[f"dn_pe{d}"], value("pe", "qs", s_next - 1))
                    for bd, a0 in ((k_bd, 4), (q_bd, 0), (v_bd, 8)):
                        for h in range(2):
                            lo = slice(h * C, (h + 1) * C)
                            g.tensor_copy(part(bd, d)[lo, :, lo], dT[lo, a0:a0 + 4, nx * C:(nx + 1) * C]).then_inc(S[f"dn_stage{d}"], 1)
                            pool.wait_ge(S[f"dn_stage{d}"], count(f"dn_stage{d}"))
                if slot == "out":
                    pool.wait_ge(S[f"dn_dve{d}"], value("dve", "o1", s))
                    g.tensor_tensor(oacc[:, ch], oacc[:, ch], part(oo, d), ALU.add).then_inc(S[f"dn_acc{d}"], 1)
                    pool.wait_ge(S[f"dn_acc{d}"], count(f"dn_acc{d}"))
            pool.sem_inc(S["arrivals"], 1)
            pool.wait_ge(S["arrivals"], 5 * 4)
            pool.sem_inc(S["arrivals"], 1)
            pool.wait_ge(S["arrivals"], 5 * 5)
            pool.sem_inc(S["arrivals"], 1)
            pool.wait_ge(S["arrivals"], 5 * 6)
            pool.sem_inc(S["arrivals"], 1)
            pool.wait_ge(S["arrivals"], 5 * 7)
            pool.wait_ge(S["pos_ready"], 1)
            for n in range(NT):
                for k in range(2):
                    pool.indirect_dma_start(slot_d, bass.IndirectOffsetOnAxis(ap=pos_i[:, k, n:n + 1], axis=0),
                                            tok_i[:, n:n + 1].bitcast(U32), None).then_inc(S["slot_scat"], 16)
            pool.wait_ge(S["slot_scat"], 32 * NT * 8 // 8)
            pool.dma_start(slot_i[:], slot_d.rearrange("(t p) x -> p (t x)", p=P)).then_inc(S["idx_in"], 16)
            pool.wait_ge(S["idx_in"], 16)
            for n in (NT - 2, NT - 1):
                pool.wait_ge(S[f"h2_out{n % 2}"], landed(n, 2))
            for t in range(MT):
                if 2 * (t - 1) > 0:
                    pool.wait_ge(S["hst_mm"], 2 * (t - 1))
                pool.indirect_dma_start(hs[t % 2], None, h2_d, bass.IndirectOffsetOnAxis(ap=slot_i[:, t:t + 1], axis=0)
                                        ).then_inc(S[f"hs_in{t % 2}"], 16)
            pool.sem_inc(S["arrivals"], 1)
            pool.wait_ge(S["arrivals"], 5 * 8)
            for n in range(NT):
                if n - 1 > 0:
                    pool.wait_ge(S["x3_ready"], n - 1)
                for k in range(2):
                    pool.indirect_dma_start(yg[2 * (n % 2) + k], None, y_d, bass.IndirectOffsetOnAxis(ap=pos_i[:, k, n:n + 1], axis=0)
                                            ).then_inc(S[f"y_in{n % 2}"], 16)


_INS = ["x_prompt", "x_sample", "c", "cache_attn_k", "cache_attn_v", "state_delta", "c_ctx", "w_mod", "b_mod", "norm_mix",
        "norm_ffn", "norm_final", "w_in", "q_norm", "k_norm", "conv_w", "a_log", "dt_bias", "dn_norm", "w_attn_br", "w_dn_br",
        "w_out", "w_rg", "b_rg", "w_re", "b_re", "w_gate_e", "w_up_e", "w_down_e"]
_OUTS = [(1, CTX, D), (1, LAT, D), (1, 1, NKV, CTX, HD), (1, 1, NKV, CTX, HD), (1, 1, 2, 8, HD, HD)]


def kernel(**inputs):
    import concourse.bacc as _bacc
    from concourse.bass_utils import run_bass_kernel_spmd as _run

    nc = _bacc.Bacc("TRN2", target_bir_lowering=False, num_devices=1)
    arrays, aps = {}, {}
    for name in _INS:
        x = np.ascontiguousarray(inputs[name])
        arrays[f"in_{name}_dram"] = x
        aps[name] = nc.dram_tensor(f"in_{name}_dram", x.shape, mybir.dt.from_np(x.dtype), kind="ExternalInput").ap()
    outs = [nc.dram_tensor(f"out_{i}_dram", s, F32, kind="ExternalOutput").ap() for i, s in enumerate(_OUTS)]
    build(nc, aps, outs)
    r = _run(nc, [arrays], core_ids=[0])
    return tuple(r.results[0][f"out_{i}_dram"] for i in range(len(_OUTS)))
```
